# Optimizing a Trainium2 kernel written in Bass

```python
import jax, jax.numpy as jnp
from jax import lax
import numpy as np

D_MODEL = 2048
BATCH = 1
SEQ = 256
DEPTH = 2

GRID_W = 64
CTX_LEN = 256

HD = 64
H_A = 8
D_A = H_A * HD
H_B = 12
HKV_B = 4
D_B = H_B * HD
KV_B = HKV_B * HD
H_C = 6
NOPE_C = 128
ROPE_DIM = 64
QK_C = NOPE_C + ROPE_DIM
V_C = 128
D_C = H_C * V_C
Q_LORA = 768
KV_LORA = 512
D_MIX = D_A + D_B + D_C
N_IN = 3 * D_A + D_B + 2 * KV_B + Q_LORA + KV_LORA + ROPE_DIM + D_MIX

NA_ROWS = 8
NA_COLS = 16
SW_WINDOW = 128
SW_BLOCK = 128
Q_BLOCK = 128

ROPE_BASE = 10000.0
ADA_SCALE = 0.5
EPS = 1e-6
NEG_INF = -1e30


def rms(x, w):
    xf = x.astype(jnp.float32)
    y = xf * lax.rsqrt(jnp.mean(xf * xf, axis=-1, keepdims=True) + EPS)
    return (y * w.astype(jnp.float32)).astype(x.dtype)

def axial_rope(L, dim, dtype):
    t = jnp.arange(L)
    row = (t // GRID_W).astype(jnp.float32)
    col = (t % GRID_W).astype(jnp.float32)
    n_freq = dim // 4
    inv = ROPE_BASE ** (-jnp.arange(n_freq, dtype=jnp.float32) / n_freq)
    ar = row[:, None] * inv
    ac = col[:, None] * inv
    ang = jnp.concatenate([ar, ar, ac, ac], axis=-1)
    return jnp.cos(ang).astype(dtype), jnp.sin(ang).astype(dtype)

def apply_rope2d(x, cos, sin):
    x1, x2, x3, x4 = jnp.split(x, 4, axis=-1)
    rot = jnp.concatenate([-x2, x1, -x4, x3], axis=-1)
    return x * cos[None, :, None, :] + rot * sin[None, :, None, :]

def split_points():
    sizes = (D_A, D_A, D_A, D_B, KV_B, KV_B, Q_LORA, KV_LORA, ROPE_DIM, D_MIX)
    return [int(p) for p in np.cumsum(sizes)[:-1]]

def project_stream(h, w_in, qn_a, kn_a, qn_b, kn_b, qa_norm, kva_norm, w_qb, w_kvb, qn_c, kn_c, rope):
    B, L, _ = h.shape
    u = h @ w_in
    qa, ka, va, qb, kb, vb, cq, ckv, kpe, z = jnp.split(u, split_points(), axis=-1)

    def heads(t, n):
        return t.reshape(B, L, n, -1)

    qa = rms(heads(qa, H_A), qn_a)
    ka = rms(heads(ka, H_A), kn_a)
    va = heads(va, H_A)
    qb = rms(heads(qb, H_B), qn_b)
    kb = rms(heads(kb, HKV_B), kn_b)
    vb = heads(vb, HKV_B)
    qc = rms(heads(rms(cq, qa_norm) @ w_qb, H_C), qn_c)
    kvc = heads(rms(ckv, kva_norm) @ w_kvb, H_C)
    kc = jnp.concatenate(
        [kvc[..., :NOPE_C], jnp.broadcast_to(kpe[:, :, None, :], (B, L, H_C, ROPE_DIM))], axis=-1)
    kc = rms(kc, kn_c)
    vc = kvc[..., NOPE_C:]
    if rope is not None:
        cos, sin = rope
        qb = apply_rope2d(qb, cos, sin)
        kb = apply_rope2d(kb, cos, sin)
        qc = jnp.concatenate([qc[..., :NOPE_C], apply_rope2d(qc[..., NOPE_C:], cos, sin)], axis=-1)
        kc = jnp.concatenate([kc[..., :NOPE_C], apply_rope2d(kc[..., NOPE_C:], cos, sin)], axis=-1)
    return (qa, ka, va, qb, kb, vb, qc, kc, vc, z)

def natten_latent(q, k, v, kc, vc, rpb):
    B, L, H, D = q.shape
    rows = L // GRID_W
    wr = min(NA_ROWS, rows)
    ncb = GRID_W // NA_COLS
    span = 2 * NA_COLS
    cb = np.arange(ncb)
    kcol = np.clip(cb * NA_COLS - NA_COLS // 2, 0, GRID_W - span)[:, None] + np.arange(span)
    qcol = cb[:, None] * NA_COLS + np.arange(NA_COLS)
    qstart = np.clip(qcol - NA_COLS // 2, 0, GRID_W - NA_COLS)
    col_ok = (kcol[:, None, :] >= qstart[:, :, None]) & (kcol[:, None, :] < qstart[:, :, None] + NA_COLS)
    dc_idx = (np.clip(kcol[:, None, :] - qcol[:, :, None], -(NA_COLS - 1), NA_COLS - 1)
              + NA_COLS - 1).astype(np.int32)
    qg = q.reshape(B, rows, ncb, NA_COLS, H, D)
    kg = k.reshape(B, rows, GRID_W, H, D)[:, :, kcol]
    vg = v.reshape(B, rows, GRID_W, H, D)[:, :, kcol]
    scale = D ** -0.5
    n_loc = wr * span

    def row_fn(r):
        rs = jnp.clip(r - wr // 2, 0, rows - wr)
        qr = lax.dynamic_index_in_dim(qg, r, axis=1, keepdims=False)
        kr = lax.dynamic_slice_in_dim(kg, rs, wr, axis=1)
        vr = lax.dynamic_slice_in_dim(vg, rs, wr, axis=1)
        dr_idx = rs + jnp.arange(wr) - r + NA_ROWS - 1
        bias = rpb[:, dr_idx[None, None, :, None], dc_idx[:, :, None, :]]
        s_loc = jnp.einsum('bnqhd,brnkhd->bhnqrk', qr, kr,
                           preferred_element_type=jnp.float32) * scale + bias
        s_loc = jnp.where(col_ok[:, :, None, :], s_loc, NEG_INF)
        s_ctx = jnp.einsum('bnqhd,bchd->bhnqc', qr, kc, preferred_element_type=jnp.float32) * scale
        s = jnp.concatenate([s_loc.reshape(B, H, ncb, NA_COLS, n_loc), s_ctx], axis=-1)
        p = jax.nn.softmax(s, axis=-1).astype(v.dtype)
        p_loc = p[..., :n_loc].reshape(B, H, ncb, NA_COLS, wr, span)
        o = (jnp.einsum('bhnqrk,brnkhd->bnqhd', p_loc, vr)
             + jnp.einsum('bhnqc,bchd->bnqhd', p[..., n_loc:], vc))
        return o.reshape(B, GRID_W, H, D)

    o = lax.map(row_fn, jnp.arange(rows))
    return o.transpose(1, 0, 2, 3, 4).reshape(B, L, H, D)

def swa_latent(q, k, v, kc, vc, sink):
    B, L, H, D = q.shape
    Hkv = k.shape[2]
    G = H // Hkv
    Lc = kc.shape[1]
    nb = L // SW_BLOCK
    span = SW_BLOCK + 2 * SW_WINDOW
    pad = ((0, 0), (SW_WINDOW, SW_WINDOW), (0, 0), (0, 0))
    kp = jnp.pad(k, pad)
    vp = jnp.pad(v, pad)
    qb = q.reshape(B, nb, SW_BLOCK, Hkv, G, D).transpose(1, 0, 2, 3, 4, 5)
    snk = sink.reshape(Hkv, G).astype(jnp.float32)[None, :, :, None, None]
    scale = D ** -0.5

    def blk(args):
        i, qi = args
        k0 = i * SW_BLOCK
        ki = lax.dynamic_slice_in_dim(kp, k0, span, axis=1)
        vi = lax.dynamic_slice_in_dim(vp, k0, span, axis=1)
        qpos = k0 + jnp.arange(SW_BLOCK)
        kpos = k0 - SW_WINDOW + jnp.arange(span)
        ok = (kpos >= 0) & (kpos < L) & (jnp.abs(qpos[:, None] - kpos[None, :]) <= SW_WINDOW)
        s_loc = jnp.einsum('bqkgd,bjkd->bkgqj', qi, ki, preferred_element_type=jnp.float32) * scale
        s_loc = jnp.where(ok, s_loc, NEG_INF)
        s_ctx = jnp.einsum('bqkgd,bckd->bkgqc', qi, kc, preferred_element_type=jnp.float32) * scale
        s = jnp.concatenate([s_loc, s_ctx, jnp.broadcast_to(snk, s_loc.shape[:-1] + (1,))], axis=-1)
        p = jax.nn.softmax(s, axis=-1).astype(v.dtype)
        o = (jnp.einsum('bkgqj,bjkd->bqkgd', p[..., :span], vi)
             + jnp.einsum('bkgqc,bckd->bqkgd', p[..., span:span + Lc], vc))
        return o.reshape(B, SW_BLOCK, H, D)

    o = lax.map(blk, (jnp.arange(nb), qb))
    return o.transpose(1, 0, 2, 3, 4).reshape(B, L, H, D)

def mla_latent(q, k, v, kc, vc):
    B, L, H, D = q.shape
    Dv = v.shape[-1]
    nb = L // Q_BLOCK
    k_all = jnp.concatenate([kc, k], axis=1)
    v_all = jnp.concatenate([vc, v], axis=1)
    qb = q.reshape(B, nb, Q_BLOCK, H, D).transpose(1, 0, 2, 3, 4)
    scale = D ** -0.5

    def blk(qi):
        s = jnp.einsum('bqhd,bkhd->bhqk', qi, k_all, preferred_element_type=jnp.float32) * scale
        p = jax.nn.softmax(s, axis=-1).astype(v.dtype)
        return jnp.einsum('bhqk,bkhd->bqhd', p, v_all)

    o = lax.map(blk, qb)
    return o.transpose(1, 0, 2, 3, 4).reshape(B, L, H, Dv)

def ctx_attn(q, k, v, sink=None):
    B, Lc, H, D = q.shape
    Hkv = k.shape[2]
    G = H // Hkv
    qg = q.reshape(B, Lc, Hkv, G, D)
    s = jnp.einsum('bqkgd,bckd->bkgqc', qg, k, preferred_element_type=jnp.float32) * (D ** -0.5)
    if sink is not None:
        snk = sink.reshape(Hkv, G).astype(jnp.float32)[None, :, :, None, None]
        s = jnp.concatenate([s, jnp.broadcast_to(snk, s.shape[:-1] + (1,))], axis=-1)
    p = jax.nn.softmax(s, axis=-1)[..., :Lc].astype(v.dtype)
    return jnp.einsum('bkgqc,bckd->bqkgd', p, v).reshape(B, Lc, H, v.shape[-1])

def merge_out(o_a, o_b, o_c, z, w_out):
    B, L = o_a.shape[:2]
    y = jnp.concatenate([o_a.reshape(B, L, -1), o_b.reshape(B, L, -1), o_c.reshape(B, L, -1)], axis=-1)
    return (y * jax.nn.silu(z)) @ w_out

def first_inputs(seed: int = 0) -> dict:
    key = jax.random.key(seed)
    ks = jax.random.split(key, 21)
    f32 = jnp.float32

    def nrm(k, shape, s):
        return jax.random.normal(k, shape, f32) * s

    def gain(k, shape):
        return 1.0 + 0.02 * jax.random.normal(k, shape, f32)

    return {
        "x": nrm(ks[0], (BATCH, SEQ, D_MODEL), 1.0),
        "c": nrm(ks[1], (BATCH, D_MODEL), 1.0),
        "ctx": nrm(ks[2], (BATCH, CTX_LEN, D_MODEL), 1.0),
        "c_ctx": nrm(ks[3], (D_MODEL,), 1.0),
        "norm_w": gain(ks[4], (DEPTH, D_MODEL)),
        "w_ada": nrm(ks[5], (DEPTH, D_MODEL, 3 * D_MODEL), ADA_SCALE * D_MODEL ** -0.5),
        "b_ada": nrm(ks[6], (DEPTH, 3 * D_MODEL), 0.01),
        "w_in": nrm(ks[7], (DEPTH, D_MODEL, N_IN), D_MODEL ** -0.5),
        "qn_a": gain(ks[8], (DEPTH, HD)),
        "kn_a": gain(ks[9], (DEPTH, HD)),
        "rpb_a": nrm(ks[10], (DEPTH, H_A, 2 * NA_ROWS - 1, 2 * NA_COLS - 1), 0.1),
        "qn_b": gain(ks[11], (DEPTH, HD)),
        "kn_b": gain(ks[12], (DEPTH, HD)),
        "sink_b": nrm(ks[13], (DEPTH, H_B), 0.5),
        "qa_norm": gain(ks[14], (DEPTH, Q_LORA)),
        "kva_norm": gain(ks[15], (DEPTH, KV_LORA)),
        "w_qb": nrm(ks[16], (DEPTH, Q_LORA, H_C * QK_C), Q_LORA ** -0.5),
        "w_kvb": nrm(ks[17], (DEPTH, KV_LORA, H_C * (NOPE_C + V_C)), KV_LORA ** -0.5),
        "qn_c": gain(ks[18], (DEPTH, QK_C)),
        "kn_c": gain(ks[19], (DEPTH, QK_C)),
        "w_out": nrm(ks[20], (DEPTH, D_MIX, D_MODEL), D_MIX ** -0.5),
    }

def first_block(x, c, ctx, c_ctx, norm_w, w_ada, b_ada, w_in, qn_a, kn_a, rpb_a, qn_b, kn_b, sink_b,
              qa_norm, kva_norm, w_qb, w_kvb, qn_c, kn_c, w_out):
    B, L, _ = x.shape
    cos, sin = axial_rope(L, ROPE_DIM, x.dtype)
    sc = jax.nn.silu(c)
    scc = jax.nn.silu(c_ctx)
    xc = ctx
    for l in range(DEPTH):
        last = l == DEPTH - 1
        shift, scale, gate = jnp.split(sc @ w_ada[l] + b_ada[l], 3, axis=-1)
        shift_c, scale_c, gate_c = jnp.split(scc @ w_ada[l] + b_ada[l], 3, axis=-1)
        h = rms(x, norm_w[l]) * (1.0 + scale[:, None]) + shift[:, None]
        hc = rms(xc, norm_w[l]) * (1.0 + scale_c) + shift_c
        weights = (w_in[l], qn_a[l], kn_a[l], qn_b[l], kn_b[l], qa_norm[l], kva_norm[l],
                   w_qb[l], w_kvb[l], qn_c[l], kn_c[l])
        qa, ka, va, qb, kb, vb, qc, kc, vc, z = project_stream(h, *weights, rope=(cos, sin))
        qa_c, ka_c, va_c, qb_c, kb_c, vb_c, qc_c, kc_c, vc_c, z_c = project_stream(hc, *weights, rope=None)
        o_a = natten_latent(qa, ka, va, ka_c, va_c, rpb_a[l])
        o_b = swa_latent(qb, kb, vb, kb_c, vb_c, sink_b[l])
        o_c = mla_latent(qc, kc, vc, kc_c, vc_c)
        x = x + gate[:, None] * merge_out(o_a, o_b, o_c, z, w_out[l])
        if not last:
            oa_c = ctx_attn(qa_c, ka_c, va_c)
            ob_c = ctx_attn(qb_c, kb_c, vb_c, sink_b[l])
            oc_c = ctx_attn(qc_c, kc_c, vc_c)
            xc = xc + gate_c * merge_out(oa_c, ob_c, oc_c, z_c, w_out[l])
    return x


DEPTH_2 = 1

N_META = 16
POOL_WIDTH = D_MODEL
POOL_WINDOWS = (2, 4, 8, 16)
N_POOL_GROUPS = len(POOL_WINDOWS)
POOL_GROUP = POOL_WIDTH // N_POOL_GROUPS
CONV_WIDTH = D_MODEL
CONV_K = 3
N_BRANCHES = 2
FFN_HIDDEN = ((8 * D_MODEL // 3 + 255) // 256) * 256
IN_PROJ_WIDTH = POOL_WIDTH + 3 * CONV_WIDTH + N_BRANCHES * D_MODEL


def rms_norm(x, g):
    xf = x.astype(jnp.float32)
    y = xf * lax.rsqrt(jnp.mean(xf * xf, axis=-1, keepdims=True) + EPS)
    return (y * g.astype(jnp.float32)).astype(x.dtype)

def causal_multiscale_pool(u):
    b, l, _ = u.shape
    ug = u.reshape(b, l, N_POOL_GROUPS, POOL_GROUP).astype(jnp.float32)
    c = jnp.concatenate([jnp.zeros((b, 1, N_POOL_GROUPS, POOL_GROUP), jnp.float32),
                         jnp.cumsum(ug, axis=1)], axis=1)
    t1 = jnp.arange(1, l + 1, dtype=jnp.float32)
    outs = []
    for gi, w in enumerate(POOL_WINDOWS):
        cg = c[:, :, gi]
        c_lag = jnp.pad(cg, ((0, 0), (w - 1, 0), (0, 0)))[:, :l]
        win_sum = cg[:, 1:] - c_lag
        count = jnp.minimum(t1, jnp.float32(w))[None, :, None]
        outs.append(win_sum / count - ug[:, :, gi])
    return jnp.stack(outs, axis=2).astype(u.dtype)

def causal_depthwise_conv(v, w):
    l = v.shape[1]
    vp = jnp.pad(v, ((0, 0), (CONV_K - 1, 0), (0, 0)))
    return sum(w[k][None, None, :] * vp[:, k:k + l] for k in range(CONV_K))

def second_inputs(seed: int = 0) -> dict:
    key = jax.random.key(seed)
    ks = jax.random.split(key, 16)
    f32 = jnp.float32
    nrm = lambda k, shape, scale: jax.random.normal(k, shape, f32) * scale
    return {
        "x": nrm(ks[0], (BATCH, SEQ, D_MODEL), 1.0),
        "meta_tokens": nrm(ks[1], (N_META, D_MODEL), 1.0),
        "norm_mix_g": 1.0 + nrm(ks[2], (D_MODEL,), 0.02),
        "w_in": nrm(ks[3], (D_MODEL, IN_PROJ_WIDTH), D_MODEL ** -0.5),
        "b_gate": nrm(ks[4], (N_BRANCHES * D_MODEL,), 0.02),
        "pool_w": nrm(ks[5], (N_POOL_GROUPS, POOL_GROUP, POOL_GROUP), POOL_GROUP ** -0.5),
        "pool_scale": 1.0 + nrm(ks[6], (POOL_WIDTH,), 0.02),
        "conv_w": nrm(ks[7], (CONV_K, CONV_WIDTH), CONV_K ** -0.5),
        "conv_out_w": nrm(ks[8], (CONV_WIDTH, D_MODEL), CONV_WIDTH ** -0.5),
        "w_o": nrm(ks[9], (D_MODEL, D_MODEL), D_MODEL ** -0.5),
        "norm_ffn_g": 1.0 + nrm(ks[10], (D_MODEL,), 0.02),
        "w_gate_up": nrm(ks[11], (D_MODEL, 2 * FFN_HIDDEN), D_MODEL ** -0.5),
        "w_down": nrm(ks[12], (FFN_HIDDEN, D_MODEL), FFN_HIDDEN ** -0.5),
        "norm_final_g": 1.0 + nrm(ks[13], (D_MODEL,), 0.02),
    }

def second_block(x, meta_tokens, norm_mix_g, w_in, b_gate, pool_w, pool_scale, conv_w,
              conv_out_w, w_o, norm_ffn_g, w_gate_up, w_down, norm_final_g):
    b = x.shape[0]
    meta = jnp.broadcast_to(meta_tokens[None].astype(x.dtype), (b, N_META, D_MODEL))
    h = jnp.concatenate([meta, x], axis=1)

    splits = np.cumsum([POOL_WIDTH, CONV_WIDTH, CONV_WIDTH, CONV_WIDTH, D_MODEL]).tolist()
    for _ in range(DEPTH_2):
        hn = rms_norm(h, norm_mix_g)
        proj = hn @ w_in
        u, gb_in, gc_in, v_in, ga_lin, gbr_lin = jnp.split(proj, splits, axis=-1)

        pooled = causal_multiscale_pool(u)
        y_a = jnp.einsum("blgc,gcd->blgd", pooled, pool_w).reshape(b, -1, POOL_WIDTH)
        y_a = y_a * pool_scale

        y_b = (gb_in * causal_depthwise_conv(gc_in * v_in, conv_w)) @ conv_out_w

        gates = jax.nn.sigmoid(jnp.concatenate([ga_lin, gbr_lin], axis=-1) + b_gate)
        g_a, g_b = jnp.split(gates, 2, axis=-1)
        h = h + (g_a * y_a + g_b * y_b) @ w_o

        hn = rms_norm(h, norm_ffn_g)
        gate, up = jnp.split(hn @ w_gate_up, 2, axis=-1)
        h = h + (jax.nn.silu(gate) * up) @ w_down

    out = rms_norm(h, norm_final_g)
    return out[:, N_META:]


def setup_inputs(seed=0):
    out = dict(first_inputs(seed))
    for name, value in second_inputs(seed + 1).items():
        if name != "x":
            out[name + "_2"] = value
    return out


def reference(
    x, c, ctx, c_ctx, norm_w, w_ada, b_ada, w_in, qn_a, kn_a, rpb_a, qn_b, kn_b, sink_b,
    qa_norm, kva_norm, w_qb, w_kvb, qn_c, kn_c, w_out, meta_tokens_2, norm_mix_g_2, w_in_2,
    b_gate_2, pool_w_2, pool_scale_2, conv_w_2, conv_out_w_2, w_o_2, norm_ffn_g_2, w_gate_up_2,
    w_down_2, norm_final_g_2,
):
    x = first_block(
        x, c, ctx, c_ctx, norm_w, w_ada, b_ada, w_in, qn_a, kn_a, rpb_a, qn_b, kn_b, sink_b,
        qa_norm, kva_norm, w_qb, w_kvb, qn_c, kn_c, w_out,
    )
    return second_block(
        x, meta_tokens_2, norm_mix_g_2, w_in_2, b_gate_2, pool_w_2, pool_scale_2, conv_w_2,
        conv_out_w_2, w_o_2, norm_ffn_g_2, w_gate_up_2, w_down_2, norm_final_g_2,
    )


_drawn_inputs = setup_inputs


def setup_inputs(seed=0):
    import zlib

    import numpy as np

    out = dict(_drawn_inputs(seed))
    spreads = {}
    factors = {'norm_w': 8.0,
     'b_ada': 8.0,
     'qn_a': 8.0,
     'kn_a': 8.0,
     'rpb_a': 8.0,
     'qn_b': 8.0,
     'kn_b': 8.0,
     'sink_b': 8.0,
     'qa_norm': 8.0,
     'kva_norm': 8.0,
     'w_qb': 3.327,
     'qn_c': 8.0,
     'kn_c': 8.0,
     'norm_mix_g_2': 2.993,
     'b_gate_2': 8.0,
     'pool_scale_2': 47.021,
     'norm_ffn_g_2': 20.173,
     'norm_final_g_2': 7.772}
    for name, (base, spread) in spreads.items():
        noise = np.random.default_rng([zlib.crc32(name.encode()), seed]).standard_normal(out[name].shape)
        drawn = base * np.exp(spread * noise) if base else spread * noise
        out[name] = __import__('jax').numpy.asarray(drawn.astype(out[name].dtype))
    for name, factor in factors.items():
        out[name] = (out[name] * factor).astype(out[name].dtype)
    return out
```

```python
import concourse.bass as bass
import numpy as np
from concourse import mybir

F32 = mybir.dt.float32
F32R = mybir.dt.float32r
ALU = mybir.AluOpType
ACT = mybir.ActivationFunctionType
AXX = mybir.AxisListType.X

P = 128
D = 2048
DT = D // P
L = 256
LC = 256
DEPTH = 2
HD = 64
H_A, H_B, HKV_B, H_C = 8, 12, 4, 6
NOPE, ROPE, V_C = 128, 64, 128
QK_C = NOPE + ROPE
Q_LORA, KV_LORA = 768, 512
GRID_W, NA_COLS, NA_ROWS = 64, 16, 8
SW = 128
META = 16
N2 = META + L
FFN = 5632
FT = FFN // P
WINDOWS = (2, 4, 8, 16)
EPS = 1e-6
NEG = -1e30

CH = 1024
RING = 4

T_QA, T_QB, T_CQ, T_KA, T_VA, T_KB, T_VB, T_CKV, T_KPE = 0, 4, 10, 16, 20, 24, 26, 28, 32
NT = 33
T_QN, T_QR, T_KR, T_KN, T_VC = 0, 6, 10, 16, 22
T_COPY_C = (13, 14, 15, 28, 29, 30)
B_ORDER = [h for g in (0, 6) for a in range(g, g + 3) for h in (a, a + 3)]


def table(fields):
    at, out = 0, {}
    for name, n in fields:
        out[name] = (at, at + n)
        at += n
    return out, at


CONST, NCONST = table([
    ("ident", P), ("rev", P), ("rot", P), ("cos", L), ("sin", L), ("band", 2 * P), ("cols", L),
    ("pair", 66), ("cq", 34), ("ckv", 34), ("nope", 23), ("rope", 22), ("kpe", 12), ("mean", 1), ("sum4", 2), ("eps", 1)])
PARAM, NPARAM = table([
    ("b_ada", 2 * 48), ("norm_w", 2 * DT), ("qn_a", 2), ("kn_a", 2), ("qn_b", 2), ("kn_b", 2),
    ("qa_norm", 2 * 6), ("kva_norm", 2 * 4), ("qn_n", 2), ("qn_r", 2), ("kn_n", 2), ("kn_r", 2),
    ("sink", 2 * H_B), ("cond", 2 * DT), ("norm_mix", DT), ("b_gate", 2 * DT),
    ("pool_scale", DT), ("conv_w", 3 * DT), ("norm_ffn", DT), ("norm_final", DT)])


class Mark:
    __slots__ = ("of", "v")

    def __init__(self, of, v):
        self.of, self.v = of, v


class Count:

    def __init__(self, prog, handle=None, step=1):
        self.prog, self.handle, self.step, self.v = prog, handle, step, 0
        prog.counts.append(self)

    def inc(self, ins):
        ins.then_inc(self.handle, self.step)
        self.v += self.step
        m = Mark(self, self.v)
        self.prog.marks.append(m)
        return m


class Prog:

    def __init__(self, nc):
        self.nc, self.counts, self.marks = nc, [], []
        self.turn = None
        self.start, self.stride = {}, {}
        self.body = 0
        self.nsem = 0

    def sem(self, name, step=1):
        self.nsem += 1
        return Count(self, self.nc.alloc_semaphore(name), step)

    def value(self, of, v):
        if self.turn is None or v <= self.start[of] or not self.stride[of]:
            return v
        return v + (self.turn - 2) * self.stride[of]

    def wait(self, eng, *marks):
        best = {}
        for m in marks:
            if m is None:
                continue
            if isinstance(m, (list, tuple)):
                for x in m:
                    if x is not None and (x.of not in best or best[x.of] < x.v):
                        best[x.of] = x.v
            elif m.of not in best or best[m.of] < m.v:
                best[m.of] = m.v
        for of, v in best.items():
            eng.wait_ge(of.handle, self.value(of, v))

    def repeat(self, n, body):
        if n <= 3:
            for i in range(n):
                body(i)
            return
        assert self.turn is None
        body(0)
        start = {c: c.v for c in self.counts}
        body(1)
        after = {c: c.v for c in self.counts}
        self.marks = []
        with self.nc.Fori(2, n) as turn:
            self.turn, self.start = turn, start
            self.stride = {c: after[c] - start[c] for c in self.counts}
            self.body = 1
            body(turn)
        self.turn, self.body = None, 0
        for c in self.counts:
            assert c.v - after[c] == self.stride[c]
            c.v += (n - 3) * self.stride[c]
        for m in self.marks:
            m.v += (n - 3) * self.stride[m.of]
        self.marks = []


def host_chunks():
    out = []

    def stage(name, layer, kt, groups, mt):
        kpc = CH // (mt * P)
        for cols in groups:
            for k0 in range(0, kt, kpc):
                out.append((name, layer, k0, min(kpc, kt - k0), cols))

    def span(a, n):
        return [[(a + i, a + i + 512)] for i in range(0, n, 512)]

    for l in range(DEPTH):
        stage("w_ada", l, DT, span(0, 3 * D), 4)
    qa, ka, va = 0, 512, 1024
    qb, kb, vb = 1536, 2304, 2560
    cq, ckv, kpe, z = 2816, 3584, 4096, 4160
    qb_cols = [(qb + h * HD, qb + h * HD + HD) for h in B_ORDER]
    z_cols = [(z, z + 512)] + [(z + 512 + h * HD, z + 512 + h * HD + HD) for h in B_ORDER] + [
        (z + 1280, z + 2048)]

    def grouped(cols):
        flat = [c for a, b in cols for c in range(a, b, HD)]
        return [[(c, c + HD) for c in flat[i:i + 8]] for i in range(0, len(flat), 8)]

    for l in range(DEPTH):
        stage("w_in", l, DT, grouped(z_cols), 4)
        stage("w_in", l, DT, grouped([(qa, qa + 512)] + qb_cols + [(cq, cq + 768)]), 4)
        stage("w_in", l, DT, grouped([(ka, ka + 512), (va, va + 512), (kb, kb + 256),
                                      (vb, vb + 256), (ckv, ckv + 512)]), 4)
        stage("w_in", l, DT, [[(kpe, kpe + HD)] * 2], 1)
        c = [(h * QK_C, h * QK_C + NOPE) for h in range(H_C)]
        c += [(h * QK_C + NOPE, (h + 1) * QK_C) for h in range(H_C)]
        flat = [x for a, b in c for x in range(a, b, HD)]
        stage("w_qb", l, 6, [[(x, x + HD) for x in flat[i:i + 6]] for i in range(0, 18, 6)], 3)
        c = [(h * 256, h * 256 + NOPE) for h in range(H_C)]
        c += [(h * 256 + NOPE, h * 256 + 256) for h in range(H_C)]
        stage("w_kvb", l, 4, [c[i:i + 4] for i in range(0, 12, 4)], 4)
        stage("w_out", l, DT, span(0, D), 4)
    stage("w_in_2", None, DT, span(0, D), 4)
    for g in range(4):
        stage("pool_w_2", g, 4, span(0, 512), 4)
    for j in range(4):
        for part in (2, 3, 1):
            stage("w_in_2", None, DT, span(part * D + j * 512, 512), 4)
    for j in range(4):
        for part in (4, 5):
            stage("w_in_2", None, DT, span(part * D + j * 512, 512), 4)
        stage("conv_out_w_2", None, DT, span(j * 512, 512), 4)
    stage("w_o_2", None, DT, span(0, D), 4)
    stage("w_gate_up_2", None, DT,
          [[(g * 256, g * 256 + 256), (FFN + g * 256, FFN + g * 256 + 256)] for g in range(FT // 2)], 4)
    stage("w_down_2", None, FT, span(0, D), 4)
    return out


def build(nc, stream, xT, metaT, const_d, param_d, sel_d, rpb_d, z_d, x_d, out_d, dbg=None):
    pr = Prog(nc)
    wait, value = pr.wait, pr.value
    SP, AC, VE, PO, PE = nc.sync, nc.scalar, nc.vector, nc.gpsimd, nc.tensor

    act_n, dve_n, pool_n, pe_n = (pr.sem(n) for n in ("act_n", "dve_n", "pool_n", "pe_n"))
    raw_n = [pr.sem(f"raw_n{i}", 16) for i in range(RING)]
    load_n = [pr.sem(f"load_n{i}", 16) for i in range(10)]
    store_n = [pr.sem(f"store_n{i}", 16) for i in range(4)]
    chunk = Count(pr)

    def act(ins):
        return act_n.inc(ins)

    def dve(ins):
        return dve_n.inc(ins)

    def pool(ins):
        return pool_n.inc(ins)

    def pe(ins):
        return pe_n.inc(ins)

    base = (nc.sbuf_base + 63) // 64 * 64
    place = [base]

    def region(nbytes):
        at = place[0]
        place[0] += (nbytes + 31) // 32 * 32
        return at

    def sb(name, shape, dt, at):
        n = 4 * int(np.prod(shape[1:]))
        assert at + n <= nc.sbuf_usable_end, (name, at + n)
        return nc.alloc_sbuf_tensor_at("sb_" + name, list(shape), dt, offset=at)

    def own(name, shape, dt=F32):
        return sb(name, shape, dt, region(4 * int(np.prod(shape[1:]))))

    const = own("const", [P, NCONST])
    param = own("param", [P, NPARAM])
    ada = own("ada", [P, 2 * 48, 2])
    amul = own("amul", [P, DT, 2])
    cond = own("cond", [P, DT, 2])
    cond4 = own("cond4", [P, DT, 4], F32R)
    wq8 = own("wq8", [P, 8])
    nsink = own("nsink", [P, H_B])
    stat = own("stat", [P, 4, 4])
    raw = own("raw", [P, RING, CH])
    whi = own("whi", [P, RING, CH], F32R)
    wlo = own("wlo", [P, RING, CH], F32R)
    block = region(153600)
    HB = 16 * 512 * 4
    HH = sb("hi", [P, DT, 512], F32R, block)
    HL = sb("lo", [P, DT, 512], F32R, block + HB)
    T = sb("T", [P, NT, 512], F32, block + 2 * HB)
    tmp_at = block + 2 * HB + NT * 2048
    TMP = sb("tmp", [P, 10, 512], F32, tmp_at)
    arow = sb("arow", [4, 512], F32, tmp_at)
    sel = sb("sel", [32, 16, P], F32, tmp_at)
    bias = [sb(f"bias{t}", [P, H_A, L], F32, block + t * HB + 10 * 2048) for t in range(2)]
    ka_copy = sb("ka_copy", [P, 512], F32, block + 15 * 2048)
    NB = DT * N2 * 4
    PH = sb("pooled_hi", [P, DT, N2], F32R, block)
    PL = sb("pooled_lo", [P, DT, N2], F32R, block + NB)
    CHI = sb("conv_hi", [P, DT, N2], F32R, block + 2 * NB)
    CLO = sb("conv_lo", [P, DT, N2], F32R, block + 3 * NB)
    YA = sb("ya", [P, DT, N2], F32, block + 4 * NB)
    G4 = sb("g4", [P, 4, N2], F32, block + 5 * NB)
    FH = sb("ffn_hi", [P, FT, N2], F32R, block)
    FL = sb("ffn_lo", [P, FT, N2], F32R, block + FT * N2 * 4)
    hn_at = block + 2 * FT * N2 * 4
    NH = sb("hn_hi", [P, DT, N2], F32R, hn_at)
    NL = sb("hn_lo", [P, DT, N2], F32R, hn_at + NB)
    t3_at = hn_at + 2 * NB
    res_at = block + 153600 - NB
    assert t3_at + 4 * N2 * 4 <= res_at and block + 5 * NB + 4 * (N2 + 2) * 4 <= hn_at
    RES = sb("res", [P, DT, N2], F32, res_at)
    T2 = sb("tmp2", [P, 8, N2 + 16], F32, block + 3 * NB)
    T3 = sb("tmp3", [P, 4, N2], F32, t3_at)
    T4 = sb("tmp4", [P, 4, N2], F32, hn_at)
    CV = sb("cv", [P, 4, N2 + 2], F32, block + 5 * NB)
    PS = nc.alloc_psum_tensor("ps", [P, 8, 512], F32)

    def C(name, rows=P):
        a, b = CONST[name]
        return const[0:rows, a:b]

    def Pm(name, i, n=1):
        a = PARAM[name][0] + i
        return param[:, a:a + n]

    ident = C("ident")

    def load(q, eng, out, in_):
        return load_n[q].inc(eng.dma_start(out, in_))

    def store(q, eng, out, in_):
        return store_n[q].inc(eng.dma_start(out, in_))

    table_in = [load(0, PO, const[:, :], const_d), load(0, PO, param[:, :], param_d)][-1]

    raw_free = [None] * RING
    hl_free = [None] * RING
    st = {"pos": 0, "set": 0}

    def next_weights(width):
        s = st["pos"] % RING
        st["pos"] += 1
        wait(SP, raw_free[s])
        landed = raw_n[s].inc(SP.dma_start(raw[:, s, 0:width], stream[value(chunk, chunk.v)][:, 0:width]))
        chunk.v += 1
        wait(AC, landed, hl_free[s])
        rounded = act(AC.activation(whi[:, s, 0:width], raw[:, s, 0:width], ACT.Copy))
        wait(VE, rounded, landed, hl_free[s])
        split = dve(VE.tensor_tensor(wlo[:, s, 0:width], raw[:, s, 0:width],
                                     whi[:, s, 0:width].bitcast(F32), ALU.subtract))
        raw_free[s] = split
        return s, split

    set_free = [[], []]
    pend = []

    def flush(turn_shift=0):
        while pend:
            fn, g, bank0, done = pend.pop(0)
            set_free[bank0 // 4] = fn(g, bank0, done)

    def next_set():
        st["set"] ^= 1
        return 4 * (st["set"] ^ 1)

    def gemm(groups, kt, mt, n, hi, lo, evac, ready=None):
        kpc = CH // (mt * P)
        nch = -(-kt // kpc)

        def one(g, u, first):
            bank0 = next_set()
            for c in range(nch):
                ks = list(range(c * kpc, min(kt, (c + 1) * kpc)))
                s, split = next_weights(len(ks) * mt * P)
                if c == 0:
                    wait(PE, set_free[bank0 // 4])
                wait(PE, split)
                for j, k in enumerate(ks):
                    if first and ready is not None:
                        wait(PE, ready[k])
                    for m in range(mt):
                        o = PS[:, bank0 + m, 0:n]
                        w0 = (j * mt + m) * P
                        wh, wl = whi[:, s, w0:w0 + P], wlo[:, s, w0:w0 + P]
                        PE.matmul(o, wh, hi[:, k, 0:n], start=(k == 0), stop=False)
                        PE.matmul(o, wh, lo[:, k, 0:n], start=False, stop=False)
                        mm = PE.matmul(o, wl, hi[:, k, 0:n], start=False, stop=(k == kt - 1))
                hl_free[s] = done = pe(mm)
                if c == min(RING - 1, nch - 1):
                    flush()
            pend.append((evac, g, bank0, done))

        def turn(i):
            if pr.body:
                pend[:] = [(evac, 2 * (i - 1) + 1, pend[0][2], pend[0][3])]
            for u in range(2):
                one(2 * i + u, u, pr.body == 0 and isinstance(i, int) and i == 0 and u == 0)

        if groups % 2 == 0 and groups > 4:
            assert 2 * nch % RING == 0
            pr.repeat(groups // 2, turn)
            pend[:] = [(evac, groups - 1, pend[0][2], pend[0][3])]
        else:
            for g in range(groups):
                one(g, g, g == 0)

    wait(AC, table_in)
    wait(VE, table_in)
    a0 = PARAM["cond"][0]
    silu_c = act(AC.activation(cond[:, :, :].rearrange("p a b -> p (a b)"), param[:, a0:a0 + 2 * DT], ACT.Silu))
    wait(AC, silu_c)
    chi = act(AC.activation(cond4[:, :, 0:2], cond[:, :, :], ACT.Copy))
    wait(VE, chi)
    cond_ready = dve(VE.tensor_tensor(cond4[:, :, 2:4], cond[:, :, :], cond4[:, :, 0:2].bitcast(F32),
                                      ALU.subtract))
    s0 = PARAM["sink"][0]
    for l in range(DEPTH):
        for j, (name, scale) in enumerate((("qn_a", HD ** -0.5), ("qn_b", HD ** -0.5),
                                           ("qn_n", QK_C ** -0.5), ("qn_r", QK_C ** -0.5))):
            consts_ready = dve(VE.tensor_scalar(wq8[:, 4 * l + j:4 * l + j + 1], Pm(name, l), float(scale),
                                                None, ALU.mult))

    ada_last = {}
    ada_g = ada[:, :, :].rearrange("p (g m) s -> p g m s", m=4)
    b_ada_g = Pm("b_ada", 0, 2 * 48).rearrange("p (g m) -> p g m", m=4)

    def ada_evac(g, bank0, done):
        wait(AC, done, ada_last.get("turned"))
        row = act(AC.activation(arow[:, :], PS[0:4, bank0, :], ACT.Copy))
        wait(PE, row, ada_last.get("added"))
        for m in range(4):
            mm = PE.matmul(PS[:, bank0 + 1, 2 * m:2 * m + 2], arow[:, m * P:(m + 1) * P], C("sum4", 4),
                           start=True, stop=True)
        ada_last["turned"] = turned = pe(mm)
        wait(VE, turned)
        for s in range(2):
            added = dve(VE.tensor_tensor(ada_g[:, g, :, s], PS[:, bank0 + 1, s:8:2], b_ada_g[:, g, :], ALU.add))
        ada_last["added"] = added
        return [row, added]

    def ada_turn(i):
        if pr.body:
            pend[:] = [(ada_evac, 2 * (i - 1) + 1, pend[0][2], pend[0][3])]
        for u in range(2):
            bank0 = next_set()
            for c in range(8):
                s, split = next_weights(CH)
                if c == 0:
                    wait(PE, set_free[bank0 // 4], cond_ready)
                wait(PE, split)
                for j in range(2):
                    k = 2 * c + j
                    o = PS[0:4, bank0, :]
                    PE.matmul(o, cond4[:, k, :], whi[:, s, j * 512:(j + 1) * 512], start=(k == 0), stop=False)
                    mm = PE.matmul(o, cond4[:, k, :], wlo[:, s, j * 512:(j + 1) * 512], start=False,
                                   stop=(k == DT - 1))
                hl_free[s] = done = pe(mm)
                if c == RING - 1:
                    flush()
            pend.append((ada_evac, 2 * i + u, bank0, done))

    ring = {}

    def slot(name, n):
        r = ring.setdefault(name, [0, [None] * n])
        i = r[0] % n
        r[0] += 1
        return i, r

    def root(src, dst, marks, n, mean_scale=1.0):
        wait(AC, *marks)
        rows = dst.shape[0]
        r = act(AC.activation(dst, src, ACT.Sqrt, bias=C("eps", rows), scale=mean_scale))
        wait(VE, r)
        return dve(VE.reciprocal(dst, dst)), r

    def layer(l, x_tiles, x_ready):
        last = l == DEPTH - 1
        nq = L if last else L + LC
        streams = 1 if last else 2
        A0 = 48 * l
        wait(VE, ada_last["added"], ring.get("amul_free"))
        for s in range(2):
            nw = param[:, PARAM["norm_w"][0] + DT * l:PARAM["norm_w"][0] + DT * (l + 1)]
            am = dve(VE.scalar_tensor_tensor(amul[:, :, s], ada[:, A0 + DT:A0 + 2 * DT, s], 1.0, nw,
                                             ALU.add, ALU.mult))
        wait(VE, am)
        wait(AC, am, ada_last["added"])
        if l == 0:
            acc = square_sum(lambda k: T[:, k, :], 512, x_ready)
        else:
            acc = ring["acc"]
        wait(PE, acc, *set_free)
        msq = pe(PE.matmul(PS[:, 7, :], C("mean").to_broadcast([P, P]), TMP[:, 5, :], start=True, stop=True))
        rstd, rt = root(PS[:, 7, :], TMP[:, 4, :], [msq], 512)
        set_free[1] = [rt]
        h_ready = []
        free = [[None] * 2 for _ in range(2)]
        wait(VE, rstd, x_ready[0])
        wait(AC, ring.get("y_free"))
        for k in range(DT):
            i = k % 2
            wait(VE, free[0][i], x_ready[k])
            for s in range(2):
                c = slice(256 * s, 256 * s + 256)
                m1 = dve(VE.scalar_tensor_tensor(TMP[:, 6 + i, c], x_tiles(k)[:, c], amul[:, k, s:s + 1],
                                                 TMP[:, 4, c], ALU.mult, ALU.mult))
            wait(AC, m1, free[1][i])
            for s in range(2):
                c = slice(256 * s, 256 * s + 256)
                m2 = act(AC.activation(TMP[:, 8 + i, c], TMP[:, 6 + i, c], ACT.Identity,
                                       bias=ada[:, A0 + k, s:s + 1]))
            free[0][i] = m2
            wait(AC, m2)
            m3 = act(AC.activation(HH[:, k, :], TMP[:, 8 + i, :], ACT.Copy))
            wait(VE, m3)
            m4 = dve(VE.tensor_tensor(HL[:, k, :], TMP[:, 8 + i, :], HH[:, k, :].bitcast(F32), ALU.subtract))
            free[1][i] = m4
            h_ready.append(m4)
        ring["amul_free"] = m1
        if l > 0:
            x_kept = [ring["x_stored"]]
        else:
            x_kept = [m1]

        zr = {"free": [None, None]}

        def z_evac(g, bank0, done):
            wait(AC, done)
            for m in range(4):
                i = m % 2
                wait(AC, zr["free"][i])
                a = act(AC.activation(TMP[:, 6 + i, 0:nq], PS[:, bank0 + m, 0:nq], ACT.Silu))
                wait(PO, a)
                zr["free"][i] = store(i, PO, z_d[4 * g + m][:, 0:nq], TMP[:, 6 + i, 0:nq])
            return [a]

        def to_T(t0, n):
            def evac(g, bank0, done):
                wait(AC, done, x_kept)
                wait(VE, done, x_kept)
                for m in range(4):
                    dst = T[:, t0 + 4 * g + m, 0:n]
                    if m % 2:
                        a = act(AC.activation(dst, PS[:, bank0 + m, 0:n], ACT.Copy))
                    else:
                        v = dve(VE.tensor_copy(dst, PS[:, bank0 + m, 0:n]))
                return [a, v]
            return evac

        wait(AC, m4, m1)
        gemm(4, DT, 4, nq, HH, HL, z_evac, h_ready)
        gemm(4, DT, 4, nq, HH, HL, to_T(T_QA, nq))
        gemm(4, DT, 4, 512, HH, HL, to_T(T_KA, 512))

        def kpe_evac(g, bank0, done):
            wait(AC, done)
            return [act(AC.activation(T[:, T_KPE, :], PS[:, bank0, :], ACT.Copy))]

        gemm(1, DT, 1, 512, HH, HL, kpe_evac)
        z_stored = list(zr["free"])
        flush()
        proj = [set_free[0], set_free[1]]
        everything = lambda: [Mark(x, x.v) for x in (act_n, dve_n, pe_n, pool_n)]

        jobs = [(T_QA + t, "pair", t, nq) for t in range(4)]
        jobs += [(T_KA + t, "pair", 4 + t, 512) for t in range(4)]
        jobs += [(T_QB + t, "pair", 8 + t, nq) for t in range(6)]
        jobs += [(T_KB + t, "pair", 14 + t, 512) for t in range(2)]
        jobs += [(T_CQ + t, "cq", 0, nq) for t in range(6)]
        jobs += [(T_CKV + t, "ckv", 0, 512) for t in range(4)]
        jobs.sort(key=lambda j: -j[3])
        all_done = everything()
        wait(PO, all_done)
        sel_in = load(1, PO, sel[:, :, :], sel_d)
        wait(AC, all_done, z_stored)
        wait(PE, all_done)
        wait(VE, all_done)

        def fan_in(jobs, rows, lhs, nb):
            free = [None] * 3
            for n, (tile, kind, t, cols) in enumerate(jobs):
                i = n % 3
                wait(AC, free[i])
                a = act(AC.activation(TMP[:, 5 + i, 0:cols], T[:, tile, 0:cols], ACT.Square))
                wait(PE, a)
                free[i] = pe(PE.matmul(PS[0:rows, nb, 0:cols], lhs(kind, t), TMP[:, 5 + i, 0:cols],
                                       start=(n == 0), stop=(n == len(jobs) - 1)))
            return free[i]

        def lhs1(kind, t):
            a = CONST[kind][0]
            if kind == "pair":
                return const[:, a + 32 - 2 * t:a + 32 - 2 * t + 34]
            return const[:, a:a + 34]

        done = fan_in(jobs, 34, lhs1, 7)
        rr, _ = root(PS[0:34, 7, :], TMP[0:34, 4, :], [done], 512)
        weights = {T_QA: (wq8[:, 4 * l:4 * l + 1], 4), T_KA: (Pm("kn_a", l), 4),
                   T_QB: (wq8[:, 4 * l + 1:4 * l + 2], 6), T_KB: (Pm("kn_b", l), 2)}

        def spread(n, tile, lhs, rhs, wgt, cols, free, rows=slice(0, P), src=None):
            b = n % 4
            wait(PE, free[b])
            m = pe(PE.matmul(PS[:, b, 0:cols], lhs, rhs[:, 0:cols], start=True, stop=True))
            wait(VE, m)
            src = T[rows, tile, 0:cols] if src is None else src
            free[b] = dve(VE.scalar_tensor_tensor(T[rows, tile, 0:cols], src, wgt, PS[rows, b, 0:cols],
                                                  ALU.mult, ALU.mult))
            return free[b]

        wait(PE, rr, sel_in)
        free = [None] * 4
        normed = {}
        for n, (tile, kind, t, cols) in enumerate(jobs):
            if kind == "pair":
                lo_ = max(k for k in weights if k <= tile)
                normed[tile] = spread(n, tile, sel[:, t, :], TMP[0:32, 4, :], weights[lo_][0], cols, free)
            else:
                r = 32 + (kind == "ckv")
                base_, w_ = (T_CQ, "qa_norm") if kind == "cq" else (T_CKV, "kva_norm")
                i = tile - base_
                w_ap = Pm(w_, (6 if kind == "cq" else 4) * l + i)
                normed[tile] = spread(n, tile, const[0:34, r:r + 1].to_broadcast([34, P]), TMP[0:34, 4, :],
                                      w_ap, cols, free)

        def rope(tiles, marks, tmp=(6, 7)):
            free = [None] * 4
            tf = [None] * 2
            out = {}
            for n, tile in enumerate(tiles):
                b, i = n % 4, n % 2
                wait(PE, free[b], marks[tile])
                m = pe(PE.matmul(PS[:, b, 0:L], C("rot"), T[:, tile, 0:L], start=True, stop=True))
                wait(VE, m, tf[i])
                v = dve(VE.tensor_tensor(TMP[:, tmp[i], 0:L], PS[:, b, 0:L], C("sin"), ALU.mult))
                free[b] = v
                wait(PO, m)
                c = pool(PO.tensor_tensor(T[:, tile, 0:L], T[:, tile, 0:L], C("cos"), ALU.mult))
                wait(VE, v, c)
                tf[i] = out[tile] = dve(VE.tensor_tensor(T[:, tile, 0:L], T[:, tile, 0:L],
                                                         TMP[:, tmp[i], 0:L], ALU.add))
            return out

        wait(PE, *[m for m in free])
        wait(VE, done)
        roped = rope([T_QB + t for t in range(6)] + [T_KB + t for t in range(2)], normed)

        def turn_values(t0, nf, marks):
            wait(PE, marks)
            flat = T[:, t0:t0 + nf, :].rearrange("p a b -> p (a b)")
            for t in range(4):
                for f in range(nf):
                    at = (t * nf + f) * P
                    mm = PE.transpose(PS[:, at // 512, at % 512:at % 512 + P],
                                      T[:, t0 + f, t * P:(t + 1) * P], ident)
            m = pe(mm)
            wait(AC, m)
            wait(VE, m)
            out = []
            for b in range(nf):
                if b % 2:
                    out.append(act(AC.activation(T[:, t0 + b, :], PS[:, b, :], ACT.Copy)))
                else:
                    out.append(dve(VE.tensor_copy(T[:, t0 + b, :], PS[:, b, :])))
            return out

        va_ready = turn_values(T_VA, 4, everything())
        vb_ready = turn_values(T_VB, 2, everything())

        wait(PO, everything())
        pad = 2 * GRID_W - 1
        for t in range(2):
            for half in range(2):
                for h in range(H_A):
                    off = ((l * H_A + h) * (2 * NA_ROWS - 1) + NA_ROWS - 1 - (2 * t + half)) * pad
                    src = bass.AP(rpb_d.tensor, off, [[1, 64], [pad, 4], [1, 64]])
                    bias_in = load(2 + t, PO, bias[t][64 * half:64 * half + 64, h, :].rearrange(
                        "p (a b) -> p a b", a=4), src)
        masked = []
        for t in range(2):
            wait(PO, Mark(load_n[2 + t], load_n[2 + t].v))
            for h in range(H_A):
                mk = pool(PO.tensor_tensor(bias[t][:, h, :], bias[t][:, h, :], C("cols"), ALU.add))
        masked = [mk]

        wait(VE, everything())
        wait(AC, everything())
        wait(PE, everything(), masked)
        wait(PO, *z_stored)
        ns = dve(VE.tensor_scalar(nsink[:, :], param[:, s0 + H_B * l:s0 + H_B * (l + 1)], -1.0, None, ALU.mult))
        wait(VE, ns)
        wait(AC, ns)
        state = {"S": [None] * 3, "P": [None] * 3, "PT": [None, None], "T": [None] * 2, "O": None,
                 "z": None, "stat": [None] * 4, "y": None, "copy": {}, "n": 0, "t": 0, "zin": None,
                 "qfree": None, "vfree": None, "ymark": None}
        queue = []

        def unit(u, terms, nk, sinks, turn):
            b = u % 3
            wait(PE, state["S"][b])
            for j, (lt, rt_, c0, cn) in enumerate(terms):
                mm = PE.matmul(PS[:, b, c0:c0 + cn], lt, rt_, start=(j == 0), stop=(j == len(terms) - 1),
                               skip_group_check=True)
            scored = pe(mm)
            i = u % 4
            wait(VE, scored, state["stat"][i])
            S = PS[:, b, 0:nk]
            mx = dve(VE.tensor_reduce(stat[:, i, 0:1], S, AXX, ALU.max, negate=True))
            if sinks is not None:
                wait(VE, mx)
                mx = dve(VE.tensor_tensor(stat[:, i, 0:1], stat[:, i, 0:1], sinks[0], ALU.min))
            wait(AC, mx, state["P"][b], state["stat"][i])
            ex = act(AC.activation(TMP[:, b, 0:nk], S, ACT.Exp, bias=stat[:, i, 0:1],
                                   accum_out=stat[:, i, 1:2]))
            state["S"][b] = ex
            if sinks is not None:
                ex = act(AC.activation(stat[:, i, 3:4], sinks[1], ACT.Exp, bias=stat[:, i, 0:1]))
                wait(VE, ex)
                sm = dve(VE.tensor_tensor(stat[:, i, 1:2], stat[:, i, 1:2], stat[:, i, 3:4], ALU.add))
                wait(VE, sm)
            else:
                wait(VE, ex)
            rc = dve(VE.reciprocal(stat[:, i, 2:3], stat[:, i, 1:2]))
            wait(VE, rc)
            pn = dve(VE.tensor_scalar(TMP[:, b, 0:nk], TMP[:, b, 0:nk], stat[:, i, 2:3], None, ALU.mult))
            state["stat"][i] = pn
            return b, pn

        def turned(u, b, pn, nk, pt, q0):
            tb = 3 + u % 2
            wait(PE, pn, state["T"][u % 2])
            for kt in range(nk // P):
                mm = PE.transpose(PS[:, tb, kt * P:(kt + 1) * P], TMP[:, b, kt * P:(kt + 1) * P], ident)
            m = pe(mm)
            state["P"][b] = m
            src = PS[:, tb, 0:nk].rearrange("p (a b) -> p a b", b=P)
            dst = pt[:, :, q0:q0 + P]
            if u % 2:
                wait(AC, m, state["PT"])
                e = act(AC.activation(dst, src, ACT.Copy))
            else:
                wait(VE, m, state["PT"])
                e = dve(VE.tensor_copy(dst, src))
            state["T"][u % 2] = e
            return e

        PTL = TMP[:, 8:10, :].rearrange("p a b -> p (a b)").rearrange("p (k q) -> p k q", q=256)
        PTC = TMP[:, 5, :].rearrange("p (k q) -> p k q", q=256)

        def y_tile(idx, turn, heads, score_terms, v_of, v_rows, y_index, sinks_of, zbuf):
            zi = load(zbuf + 2, PO, TMP[:, zbuf, 0:nq], z_d[y_index][:, 0:nq])
            zin = [zi]
            us = [(h, qt) for h in range(heads) for qt in range(2 * streams)]
            pt_marks = {}

            def after(u, h, qt, b, pn):
                ctx_ = qt >= 2
                nk = 256 if ctx_ else 512
                pt = PTC if ctx_ else PTL
                e = turned(u, b, pn, nk, pt, P * (qt % 2))
                pt_marks[(h, qt)] = e
                if qt % 2 == 0:
                    return
                wait(PE, pt_marks[(h, qt - 1)], pt_marks[(h, qt)])
                if h == 0 and not ctx_:
                    wait(PE, state["O"])
                c0 = 256 * ctx_
                kts = [2, 3] if ctx_ else [0, 1, 2, 3]
                for n, kt in enumerate(kts):
                    mm = PE.matmul(PS[v_rows(h), 5, c0:c0 + 256], v_of(h, kt), pt[:, n, :],
                                   start=(n == 0), stop=(n == len(kts) - 1))
                state["o_done"] = o_done = pe(mm)
                state["PT"][ctx_] = o_done
                if (h, qt) == us[-1]:
                    finish(o_done)

            def finish(o_done):
                wait(VE, o_done, zin, state["y"])
                y1 = dve(VE.tensor_tensor(TMP[:, 4, 0:nq], PS[:, 5, 0:nq], TMP[:, zbuf, 0:nq], ALU.mult))
                state["O"] = y1
                state["zfree"][zbuf] = y1
                wait(AC, y1)
                y2 = act(AC.activation(HH[:, y_index, 0:nq], TMP[:, 4, 0:nq], ACT.Copy))
                wait(VE, y2)
                state["y"] = dve(VE.tensor_tensor(HL[:, y_index, 0:nq], TMP[:, 4, 0:nq],
                                                  HH[:, y_index, 0:nq].bitcast(F32), ALU.subtract))

            for h, qt in us:
                u = state["n"]
                state["n"] += 1
                b, pn = unit(u, score_terms(h, qt), 256 if qt >= 2 else 512,
                             sinks_of(h) if sinks_of else None, turn)
                queue.append((after, (u, h, qt, b, pn)))
                if len(queue) > 1:
                    fn, args = queue.pop(0)
                    fn(*args)

        state["zfree"] = {6: None, 7: None}

        def drain():
            while queue:
                fn, args = queue.pop(0)
                fn(*args)

        def half(h):
            return slice(64 * (h % 2), 64 * (h % 2) + 64)

        for i in range(4):
            def terms(h, qt, i=i):
                q = T[half(h), T_QA + i, P * qt:P * qt + P]
                if qt >= 2:
                    return [(q, T[half(h), T_KA + i, 256:512], 0, 256)]
                return [(q, T[half(h), T_KA + i, :], 0, 512),
                        (C("rev"), bias[qt][:, 2 * i + h, :], 0, 256)]

            def v_of(h, kt, i=i):
                return T[:, T_VA + kt, P * i + 64 * h:P * i + 64 * h + 64]

            zb = 6 + i % 2
            wait(PO, state["zfree"][zb])
            y_tile(i, None, 2, terms, v_of, half, i, None, zb)
        for i in range(6):
            kvt = i // 3

            def terms(h, qt, i=i, kvt=kvt):
                q = T[half(h), T_QB + i, P * qt:P * qt + P]
                if qt >= 2:
                    return [(q, T[half(h), T_KB + kvt, 256:512], 0, 256)]
                a = CONST["band"][0] + P * qt
                return [(q, T[half(h), T_KB + kvt, :], 0, 512),
                        (ident, const[:, a:a + P], P * (1 - qt), P)]

            vflat = T[:, T_VB:T_VB + 2, :].rearrange("p a b -> p (a b)")

            def v_of(h, kt, kvt=kvt):
                c = 256 * kt + P * kvt + 64 * h
                return vflat[:, c:c + 64]

            def sinks_of(h, i=i):
                c = s0 + H_B * l + 2 * i + h
                return nsink[:, 2 * i + h:2 * i + h + 1], param[:, c:c + 1]

            zb = 6 + i % 2
            wait(PO, state["zfree"][zb])
            y_tile(i, None, 2, terms, v_of, half, 4 + i, sinks_of, zb)
        drain()

        def split_into(t0, n, cols, dst0):
            out = []
            wait(AC, everything())
            wait(VE, everything())
            for i in range(n):
                a = act(AC.activation(HH[:, dst0 + i, 0:cols], T[:, t0 + i, 0:cols], ACT.Copy))
                wait(VE, a)
                out.append(dve(VE.tensor_tensor(HL[:, dst0 + i, 0:cols], T[:, t0 + i, 0:cols],
                                                HH[:, dst0 + i, 0:cols].bitcast(F32), ALU.subtract)))
            return out

        def evac_c(t0, mt, n):
            def evac(g, bank0, done):
                wait(AC, done)
                wait(VE, done)
                marks = []
                for m in range(mt):
                    dst = T[:, t0 + mt * g + m, 0:n]
                    if m % 2:
                        marks.append(act(AC.activation(dst, PS[:, bank0 + m, 0:n], ACT.Copy)))
                    else:
                        marks.append(dve(VE.tensor_copy(dst, PS[:, bank0 + m, 0:n])))
                return marks
            return evac

        wait(PO, everything())
        sel_in = load(1, PO, sel[:, :, :], sel_d)
        cq_ready = split_into(T_CQ, 6, nq, 10)
        set_free[0] = set_free[1] = everything()
        gemm(3, 6, 3, nq, HH[:, 10:16, :], HL[:, 10:16, :], evac_c(0, 3, nq), cq_ready)
        flush()
        ckv_ready = split_into(T_CKV, 4, 512, 10)
        gemm(3, 4, 4, 512, HH[:, 10:14, :], HL[:, 10:14, :], evac_c(T_KN, 4, 512), ckv_ready)
        flush()
        wait(AC, everything())
        wait(PE, everything())
        wait(VE, everything())
        jobs = [(T_KN + h, "nope", 6 + h, 512) for h in range(6)] + [(T_KPE, "kpe", 0, 512)]
        jobs += [(T_QN + h, "nope", h, nq) for h in range(6)] + [(T_QR + t, "rope", t, nq) for t in range(3)]

        def lhs2(kind, t):
            a = CONST[kind][0]
            if kind == "nope":
                return const[:, a + 11 - t:a + 23 - t]
            if kind == "rope":
                return const[:, a + 10 - 2 * t:a + 22 - 2 * t]
            return const[:, a:a + 12]

        done = fan_in(jobs, 12, lhs2, 7)
        rr, _ = root(PS[0:12, 7, :], TMP[0:12, 4, :], [done], 512)
        wait(VE, rr)
        kp = dve(VE.tensor_scalar(T[:, T_KPE, :], T[:, T_KPE, :], Pm("kn_r", l), None, ALU.mult))
        wait(PE, rr, sel_in)
        free = [None] * 4
        n = 0
        marks = {T_KPE: kp}
        for h in range(6):
            for tile, r, w_, cols in ((T_QN + h, h, wq8[:, 4 * l + 2:4 * l + 3], nq),
                                      (T_KN + h, 6 + h, Pm("kn_n", l), 512)):
                spread(n, tile, const[0:12, r:r + 1].to_broadcast([12, P]), TMP[0:12, 4, :], w_, cols, free)
                n += 1
        for t in range(3):
            marks[T_QR + t] = spread(n, T_QR + t, sel[0:12, t, :], TMP[0:12, 4, :], wq8[:, 4 * l + 3:4 * l + 4],
                                     nq, free)
            n += 1
        wait(PE, free)
        wait(VE, done)
        roped = rope([T_KPE] + [T_QR + t for t in range(3)], marks)
        wait(PE, everything())
        wait(VE, roped[T_KPE])
        free = [None] * 4
        for t in range(3):
            b = t
            m = pe(PE.matmul(PS[:, b, :], sel[0:12, 3 + t, :], TMP[0:12, 4, :], start=True, stop=True))
            wait(VE, m)
            dve(VE.tensor_tensor(T[:, T_KR + t, :], T[:, T_KPE, :], PS[:, b, :], ALU.mult))
        turn_values(T_VC, 6, everything())
        for e in (PE, VE, AC, PO):
            wait(e, everything())
        vcf = T[:, T_VC:T_VC + 6, :].rearrange("p a b -> p (a b)")
        for h_ in range(6):
            def terms(h, qt, h_=h_):
                q = slice(P * qt, P * qt + P)
                k = slice(256, 512) if qt >= 2 else slice(0, 512)
                n = 256 if qt >= 2 else 512
                return [(T[:, T_QN + h_, q], T[:, T_KN + h_, k], 0, n),
                        (T[half(h_), T_QR + h_ // 2, q], T[half(h_), T_KR + h_ // 2, k], 0, n)]

            def v_of(h, kt, h_=h_):
                c = 768 * kt + P * h_
                return vcf[:, c:c + P]

            zb = 6 + h_ % 2
            wait(PO, state["zfree"][zb])
            y_tile(h_, None, 1, terms, v_of, lambda h: slice(0, P), 10 + h_, None, zb)
        drain()

        wait(PO, everything())
        if l == 0:
            xo = [load(5, PO, T[:, 16:32, :], xT)]
        else:
            xo = [load(5, PO, T[:, 16:32, :], x_d)]
            meta_in = load(6, PO, RES[:, :, 0:META], metaT)
        set_free[0] = set_free[1] = everything()
        for e in (AC, VE, PO):
            wait(e, everything())
        x_new = []
        sq = {"free": [None, None], "acc": None, "n": 0}

        def out_evac(g, bank0, done):
            marks = []
            wait(VE, done, xo)
            for m in range(4):
                k = 4 * g + m
                for s in range(streams):
                    c = slice(256 * s, 256 * s + 256)
                    dst = RES[:, k, META:] if last else T[:, k, c]
                    v = dve(VE.scalar_tensor_tensor(dst, PS[:, bank0 + m, c],
                                                    ada[:, A0 + 2 * DT + k, s:s + 1], T[:, 16 + k, c],
                                                    ALU.mult, ALU.add))
                marks.append(v)
                x_new.append(v)
                if not last:
                    square_add(T[:, k, :], 512, v, k == 0, sq)
            return marks

        gemm(4, DT, 4, nq, HH, HL, out_evac, [state["y"]] * DT)
        flush()
        if last:
            ring["meta"] = meta_in
            return x_new
        wait(PO, *x_new)
        ring["x_stored"] = store(2, PO, x_d, T[:, 0:16, :])
        wait(PO, ring["x_stored"])
        ring["acc"] = sq["acc"]
        ring["y_free"] = Mark(pe_n, pe_n.v)
        return x_new

    def square_add(src, n, ready, first, sq, bufs=None, acc=None):
        bufs = bufs or [TMP[:, 8, :], TMP[:, 9, :]]
        acc = acc if acc is not None else TMP[:, 5, :]
        if first:
            wait(AC, ready, sq.get("start"))
            a = act(AC.activation(acc[:, 0:n], src, ACT.Square))
            sq["acc"] = a
            return
        i = sq["n"] % 2
        sq["n"] += 1
        wait(AC, ready, sq["free"][i])
        a = act(AC.activation(bufs[i][:, 0:n], src, ACT.Square))
        wait(PO, a, sq["acc"])
        sq["acc"] = sq["free"][i] = pool(PO.tensor_tensor(acc[:, 0:n], acc[:, 0:n], bufs[i][:, 0:n], ALU.add))

    def square_sum(src, n, ready):
        sq = {"free": [None, None], "acc": None, "n": 0}
        for k in range(DT):
            square_add(src(k), n, ready[k], k == 0, sq)
        return sq["acc"]

    x_in = load(7, PO, T[:, 0:16, :], xT)
    pr.repeat(12, ada_turn)
    pend[:] = [(ada_evac, 23, pend[0][2], pend[0][3])]
    flush()
    new = layer(0, lambda k: T[:, k, :], [x_in] * DT)
    new = layer(1, lambda k: T[:, k, :], new)
    second(pr, locals(), new)
    return pr


def second(pr, env, x_new):
    nc = pr.nc
    wait = pr.wait
    SP, AC, VE, PO, PE = nc.sync, nc.scalar, nc.vector, nc.gpsimd, nc.tensor
    (act, dve, pool, pe, gemm, flush, C, Pm, PS, RES, NH, NL, PH, PL, CHI, CLO, YA, G4, FH, FL, T2, T3, T4, CV,
     set_free, square_add, ring, param, act_n, dve_n, pe_n, pool_n, store, out_d, root) = (
        env[k] for k in ("act dve pool pe gemm flush C Pm PS RES NH NL PH PL CHI CLO YA G4 FH FL T2 T3 T4 CV "
                         "set_free square_add ring param act_n dve_n pe_n pool_n store out_d root").split())
    N = N2
    everything = lambda: [Mark(x, x.v) for x in (act_n, dve_n, pe_n, pool_n)]
    norm_tmp = [T2[:, j, 0:N] for j in range(4)]
    last_tmp = [T4[:, j, :] for j in range(4)]

    def sync_all():
        for e in (AC, VE, PO, PE):
            wait(e, everything())

    def norm(acc, wname, hi, lo, hi_free=None, out=None, tmp=norm_tmp):
        ACC, RSTD = tmp[:2]
        wait(PE, acc, *set_free)
        msq = pe(PE.matmul(PS[:, 7, 0:N], C("mean").to_broadcast([P, P]), ACC, start=True, stop=True))
        rstd, rt = root(PS[:, 7, 0:N], RSTD, [msq], N)
        set_free[1] = [rt]
        wait(VE, rstd)
        ready, free = [], [None, None]
        for k in range(DT):
            i = k % 2
            if out is not None:
                ready.append(dve(VE.scalar_tensor_tensor(out[:, k, :], RES[:, k, :], Pm(wname, k), RSTD,
                                                         ALU.mult, ALU.mult)))
                continue
            wait(VE, free[i])
            m = dve(VE.scalar_tensor_tensor(T2[:, 4 + i, 0:N], RES[:, k, :], Pm(wname, k), RSTD,
                                            ALU.mult, ALU.mult))
            wait(AC, m, hi_free)
            a = act(AC.activation(hi[:, k, :], T2[:, 4 + i, 0:N], ACT.Copy))
            wait(VE, a, hi_free)
            free[i] = dve(VE.tensor_tensor(lo[:, k, :], T2[:, 4 + i, 0:N], hi[:, k, :].bitcast(F32), ALU.subtract))
            ready.append(free[i])
        return ready

    sync_all()
    wait(AC, ring["meta"])
    wait(VE, ring["meta"])
    sq = {"free": [None, None], "acc": None, "n": 0}
    for k in range(DT):
        square_add(RES[:, k, :], N, None, k == 0, sq, norm_tmp[2:], norm_tmp[0])
    hn = norm(sq["acc"], "norm_mix", NH, NL)
    sync_all()

    zero = None
    for j in range(8):
        zero = dve(VE.memset(T2[:, j, 0:16], 0.0))
    pooled = []
    uf = {"free": [[], []]}

    def u_evac(g, bank0, done):
        w = WINDOWS[g]
        free = []
        wait(AC, done, zero)
        for m in range(4):
            k = 4 * g + m
            base = 4 * (m % 2)
            wait(AC, uf["free"][m % 2])
            u = act(AC.activation(T2[:, base, 16:16 + N], PS[:, bank0 + m, 0:N], ACT.Copy))
            free = u
            src, step, prev = base, 1, u
            wait(VE, uf["free"][m % 2])
            while step < w:
                dst = base + 1 + (src - base) % 2
                wait(VE, prev)
                prev = dve(VE.tensor_tensor(T2[:, dst, 16:16 + N], T2[:, src, 16:16 + N],
                                            T2[:, src, 16 - step:16 + N - step], ALU.add))
                src, step = dst, step * 2
            wait(VE, prev)
            q = base + 3
            dve(VE.scalar_tensor_tensor(T2[:, q, 16 + w - 1:16 + N], T2[:, src, 16 + w - 1:16 + N], 1.0 / w,
                                        T2[:, base, 16 + w - 1:16 + N], ALU.mult, ALU.subtract))
            for t in range(w - 1):
                prev = dve(VE.scalar_tensor_tensor(T2[:, q, 16 + t:17 + t], T2[:, src, 16 + t:17 + t],
                                                   1.0 / (t + 1), T2[:, base, 16 + t:17 + t],
                                                   ALU.mult, ALU.subtract))
            wait(AC, prev)
            a = act(AC.activation(PH[:, k, :], T2[:, q, 16:16 + N], ACT.Copy))
            wait(VE, a, prev)
            v = dve(VE.tensor_tensor(PL[:, k, :], T2[:, q, 16:16 + N], PH[:, k, :].bitcast(F32), ALU.subtract))
            uf["free"][m % 2] = [v]
            pooled.append(v)
        return [free]

    gemm(4, DT, 4, N, NH, NL, u_evac, hn)
    flush()

    def ya_evac(gp):
        def evac(g, bank0, done):
            wait(VE, done)
            for m in range(4):
                k = 4 * gp + m
                v = dve(VE.tensor_scalar(YA[:, k, :], PS[:, bank0 + m, 0:N], Pm("pool_scale", k), None, ALU.mult))
            return [v]
        return evac

    for gp in range(4):
        gemm(1, 4, 4, N, PH[:, 4 * gp:4 * gp + 4, :], PL[:, 4 * gp:4 * gp + 4, :], ya_evac(gp),
             pooled[4 * gp:4 * gp + 4])
    flush()

    for m in range(4):
        zero = dve(VE.memset(CV[:, m, 0:2], 0.0))
    cf = {"conv": None, "gc": [None] * 4, "cv": [None] * 4}
    conv_ready = []

    def gc_evac(g, bank0, done):
        wait(AC, done, zero, cf["conv"])
        out = []
        for m in range(4):
            a = act(AC.activation(CV[:, m, 2:2 + N], PS[:, bank0 + m, 0:N], ACT.Copy))
            cf["gc"][m] = a
        return [a]

    def v_evac(g, bank0, done):
        wait(VE, done, *cf["gc"])
        for m in range(4):
            v = dve(VE.tensor_tensor(CV[:, m, 2:2 + N], CV[:, m, 2:2 + N], PS[:, bank0 + m, 0:N], ALU.mult))
            cf["cv"][m] = v
        free = v
        return [free]

    def gb_evac(j):
        def evac(g, bank0, done):
            wait(VE, done, *cf["cv"])
            for m in range(4):
                k = 4 * j + m
                Y = T3[:, m % 2, 0:N]
                wait(VE, cf.get(("y", m % 2)))
                a = dve(VE.tensor_scalar(Y, CV[:, m, 0:N], Pm("conv_w", k), None, ALU.mult))
                for tap in (1, 2):
                    wait(VE, a)
                    a = dve(VE.scalar_tensor_tensor(Y, CV[:, m, tap:tap + N], Pm("conv_w", DT * tap + k), Y,
                                                    ALU.mult, ALU.add))
                wait(VE, a)
                a = dve(VE.tensor_tensor(Y, Y, PS[:, bank0 + m, 0:N], ALU.mult))
                free = a
                wait(AC, a)
                h = act(AC.activation(CHI[:, k, :], Y, ACT.Copy))
                wait(VE, h)
                v = dve(VE.tensor_tensor(CLO[:, k, :], Y, CHI[:, k, :].bitcast(F32), ALU.subtract))
                cf[("y", m % 2)] = v
                conv_ready.append(v)
            cf["conv"] = free
            return [free]
        return evac

    for j in range(4):
        gemm(1, DT, 4, N, NH, NL, gc_evac)
        gemm(1, DT, 4, N, NH, NL, v_evac)
        gemm(1, DT, 4, N, NH, NL, gb_evac(j))

    gt = {"g": None, "y": None}
    mixed = []

    def ga_evac(j):
        def evac(g, bank0, done):
            wait(AC, done)
            for m in range(4):
                k = 4 * j + m
                i = 2 + m % 2
                wait(AC, cf.get(("s", m % 2)))
                a = act(AC.activation(T3[:, i, 0:N], PS[:, bank0 + m, 0:N], ACT.Sigmoid, bias=Pm("b_gate", k)))
                wait(VE, a)
                cf[("s", m % 2)] = dve(VE.tensor_tensor(YA[:, k, :], YA[:, k, :], T3[:, i, 0:N], ALU.mult))
            gt["ya"] = cf[("s", 1)]
            return [a]
        return evac

    def gbr_evac(j):
        def evac(g, bank0, done):
            wait(AC, done, gt["g"])
            for m in range(4):
                a = act(AC.activation(G4[:, m, :], PS[:, bank0 + m, 0:N], ACT.Sigmoid,
                                      bias=Pm("b_gate", DT + 4 * j + m)))
            gt["gr"] = a
            return [a]
        return evac

    def mix_evac(j):
        def evac(g, bank0, done):
            wait(VE, done, gt["gr"], gt["ya"])
            for m in range(4):
                k = 4 * j + m
                Y = T3[:, m % 2, 0:N]
                wait(VE, cf.get(("y", m % 2)))
                a = dve(VE.tensor_tensor(Y, PS[:, bank0 + m, 0:N], G4[:, m, :], ALU.mult))
                free = a
                wait(VE, a)
                a = dve(VE.tensor_tensor(Y, Y, YA[:, k, :], ALU.add))
                wait(AC, a)
                h = act(AC.activation(PH[:, k, :], Y, ACT.Copy))
                wait(VE, h)
                v = dve(VE.tensor_tensor(PL[:, k, :], Y, PH[:, k, :].bitcast(F32), ALU.subtract))
                cf[("y", m % 2)] = v
                mixed.append(v)
            gt["g"] = free
            return [free]
        return evac

    for j in range(4):
        gemm(1, DT, 4, N, NH, NL, ga_evac(j))
        gemm(1, DT, 4, N, NH, NL, gbr_evac(j))
        gemm(1, DT, 4, N, CHI, CLO, mix_evac(j), conv_ready)
    flush()

    def add_evac(sq, tmp):
        def evac(g, bank0, done):
            wait(VE, done)
            for m in range(4):
                k = 4 * g + m
                v = dve(VE.tensor_tensor(RES[:, k, :], RES[:, k, :], PS[:, bank0 + m, 0:N], ALU.add))
                square_add(RES[:, k, :], N, v, k == 0, sq, tmp[2:], tmp[0])
            return [v]
        return evac

    sync_all()
    sq = {"free": [None, None], "acc": None, "n": 0}
    gemm(4, DT, 4, N, PH, PL, add_evac(sq, norm_tmp), mixed)
    flush()
    hn = norm(sq["acc"], "norm_ffn", NH, NL, Mark(pe_n, pe_n.v))
    sync_all()

    ff = {"s": [None] * 2, "y": [None] * 2, "last": None}

    def ffn_evac(g, bank0, done):
        wait(AC, done)
        wait(VE, done)
        for m in range(2):
            wait(AC, ff["s"][m])
            a = act(AC.activation(T3[:, 2 + m, 0:N], PS[:, bank0 + m, 0:N], ACT.Silu))
            wait(VE, a, ff["y"][m])
            Y = T3[:, m, 0:N]
            v = dve(VE.tensor_tensor(Y, T3[:, 2 + m, 0:N], PS[:, bank0 + 2 + m, 0:N], ALU.mult))
            ff["s"][m] = v
            free = v
            wait(AC, v)
            h = act(AC.activation(FH[:, 2 * g + m, :], Y, ACT.Copy))
            wait(VE, h)
            ff["y"][m] = dve(VE.tensor_tensor(FL[:, 2 * g + m, :], Y, FH[:, 2 * g + m, :].bitcast(F32),
                                              ALU.subtract))
        return [a, free]

    gemm(FT // 2, DT, 4, N, NH, NL, ffn_evac, hn)
    flush()
    sq = {"free": [None, None], "acc": None, "n": 0, "start": Mark(pe_n, pe_n.v)}
    wait(AC, sq["start"])
    gemm(4, FT, 4, N, FH, FL, add_evac(sq, last_tmp), [ff["y"][1]] * FT)
    flush()
    norm(sq["acc"], "norm_final", None, None, out=RES, tmp=last_tmp)
    wait(SP, *everything())
    o = store(3, SP, out_d, RES[:, :, META:])
    wait(SP, o)
    for e in (AC, VE, PO, PE):
        wait(e, o)


def constants():
    c = np.zeros((P, NCONST), np.float32)

    def put(name, v):
        a, b = CONST[name]
        c[:v.shape[0], a:b] = v

    i = np.arange(P)
    put("ident", np.eye(P, dtype=np.float32))
    rev = np.zeros((P, P), np.float32)
    rev[i, (i // 64) * 64 + 63 - i % 64] = 1
    put("rev", rev)
    rot = np.zeros((P, P), np.float32)
    for m in range(P):
        b = m % 64 // 16
        rot[m + 16 if b % 2 == 0 else m - 16, m] = -1 if b % 2 == 0 else 1
    put("rot", rot)
    t = np.arange(L)
    nf = ROPE // 4
    inv = np.float32(10000.0) ** (-np.arange(nf, dtype=np.float32) / np.float32(nf))
    ar = (t // GRID_W).astype(np.float32)[:, None] * inv
    ac = (t % GRID_W).astype(np.float32)[:, None] * inv
    ang = np.concatenate([ar, ar, ac, ac], axis=-1).T
    put("cos", np.tile(np.cos(ang), (2, 1)).astype(np.float32))
    put("sin", np.tile(np.sin(ang), (2, 1)).astype(np.float32))
    q = np.arange(L)
    band = np.where(np.abs(q[:, None] - q[None, :]) <= SW, 0.0, NEG).astype(np.float32)
    put("band", np.concatenate([band[:P, P:], band[P:, :P]], axis=1))
    qc = 63 - i % 64
    start = np.clip(qc - NA_COLS // 2, 0, GRID_W - NA_COLS)[:, None]
    kc = np.arange(GRID_W)[None, :]
    ok = (kc >= start) & (kc < start + NA_COLS)
    put("cols", np.tile(np.where(ok, 0.0, NEG), (1, 4)).astype(np.float32))
    halves = np.zeros((P, 2), np.float32)
    halves[:64, 0] = halves[64:, 1] = 1
    v = np.zeros((P, 66), np.float32)
    v[:, 32:34] = halves / HD
    put("pair", v)
    v = np.zeros((P, 34), np.float32)
    v[:, 32] = 1 / Q_LORA
    put("cq", v)
    v = np.zeros((P, 34), np.float32)
    v[:, 33] = 1 / KV_LORA
    put("ckv", v)
    v = np.zeros((P, 23), np.float32)
    v[:, 11] = 1 / QK_C
    put("nope", v)
    v = np.zeros((P, 22), np.float32)
    v[:, 10:12] = halves / QK_C
    put("rope", v)
    v = np.zeros((P, 12), np.float32)
    v[:, 6:] = 1 / (2 * QK_C)
    put("kpe", v)
    put("mean", np.full((P, 1), 1 / D, np.float32))
    put("sum4", np.tile(np.eye(2, dtype=np.float32), (2, 1)))
    put("eps", np.full((P, 1), EPS, np.float32))
    sel = np.zeros((32, 16, P), np.float32)
    for t in range(16):
        sel[2 * t, t, :64] = sel[2 * t + 1, t, 64:] = 1
    return c, sel


def pack(inputs):
    f = {k: np.asarray(v) for k, v in inputs.items()}
    entries = host_chunks()
    stream = np.zeros((len(entries), P, CH), np.float32)
    y_rows = list(range(512)) + [512 + h * HD + d for h in B_ORDER for d in range(HD)] + list(range(1280, 2048))
    w_out = f["w_out"][:, y_rows, :]
    for n, (name, layer, k0, nk, cols) in enumerate(entries):
        w = w_out if name == "w_out" else f[name]
        if layer is not None:
            w = w[layer]
        blk = w[k0 * P:(k0 + nk) * P].reshape(nk, P, -1)
        width = sum(b - a for a, b in cols)
        dst = stream[n, :, :nk * width].reshape(P, nk, width)
        at = 0
        for a, b in cols:
            dst[:, :, at:at + b - a] = blk[:, :, a:b].transpose(1, 0, 2)
            at += b - a
    par = np.zeros((P, NPARAM), np.float32)

    def put(name, v):
        a, b = PARAM[name]
        par[:, a:b] = v

    def cols(v):
        return v.reshape(-1, P).T

    put("b_ada", cols(f["b_ada"]))
    put("norm_w", cols(f["norm_w"]))
    for n in ("qn_a", "kn_a", "qn_b", "kn_b"):
        put(n, np.tile(f[n].T, (2, 1)))
    put("qa_norm", cols(f["qa_norm"]))
    put("kva_norm", cols(f["kva_norm"]))
    for n in ("qn", "kn"):
        put(n + "_n", f[n + "_c"][:, :NOPE].T)
        put(n + "_r", np.tile(f[n + "_c"][:, NOPE:].T, (2, 1)))
    put("sink", np.broadcast_to(f["sink_b"][:, B_ORDER].reshape(1, -1), (P, 2 * H_B)))
    cond = np.stack([f["c"][0], f["c_ctx"]], axis=-1).reshape(DT, P, 2)
    put("cond", cond.transpose(1, 0, 2).reshape(P, -1))
    put("norm_mix", cols(f["norm_mix_g_2"]))
    put("b_gate", cols(f["b_gate_2"]))
    put("pool_scale", cols(f["pool_scale_2"]))
    put("conv_w", cols(f["conv_w_2"]))
    put("norm_ffn", cols(f["norm_ffn_g_2"]))
    put("norm_final", cols(f["norm_final_g_2"]))

    def tokens(x):
        return np.ascontiguousarray(x.T.reshape(DT, P, -1).transpose(1, 0, 2))

    xT = tokens(np.concatenate([f["x"][0], f["ctx"][0]], axis=0))
    metaT = tokens(f["meta_tokens_2"])
    rpb = np.zeros((DEPTH, H_A, 2 * NA_ROWS - 1, 2 * GRID_W - 1), np.float32)
    rpb[..., GRID_W - NA_COLS:GRID_W + NA_COLS - 1] = f["rpb_a"]
    const, sel = constants()
    return {"stream": stream, "xT": xT, "metaT": metaT, "const": const, "param": par, "sel": sel, "rpb": rpb}


def program(nc, arrays):
    a = {n: nc.dram_tensor(f"in_{n}", v.shape, F32, kind="ExternalInput").ap() for n, v in arrays.items()}
    z_d = nc.dram_tensor("z_scratch", (DT, P, 512), F32, kind="Internal").ap()
    x_d = nc.dram_tensor("x_scratch", (P, DT, 512), F32, kind="Internal").ap()
    out = nc.dram_tensor("out", (P, DT, L), F32, kind="ExternalOutput").ap()
    build(nc, a["stream"], a["xT"], a["metaT"], a["const"], a["param"], a["sel"], a["rpb"], z_d, x_d, out)


def kernel(**inputs):
    import concourse.bacc as bacc
    from concourse.bass_utils import run_bass_kernel_spmd

    nc = bacc.Bacc("TRN2", target_bir_lowering=False, num_devices=1)
    arrays = pack(inputs)
    program(nc, arrays)
    r = run_bass_kernel_spmd(nc, [{f"in_{n}": v for n, v in arrays.items()}], core_ids=[0])
    out = r.results[0]["out"]
    return np.ascontiguousarray(out.transpose(1, 0, 2).reshape(D, L).T).reshape(1, L, D)
```

```python
import concourse.bass as bass
import numpy as np
from concourse import mybir

F32 = mybir.dt.float32
F32R = mybir.dt.float32r
ALU = mybir.AluOpType
ACT = mybir.ActivationFunctionType
AXX = mybir.AxisListType.X

P = 128
D = 2048
DT = D // P
L = 256
LC = 256
DEPTH = 2
HD = 64
H_A, H_B, HKV_B, H_C = 8, 12, 4, 6
NOPE, ROPE, V_C = 128, 64, 128
QK_C = NOPE + ROPE
Q_LORA, KV_LORA = 768, 512
GRID_W, NA_COLS, NA_ROWS = 64, 16, 8
SW = 128
META = 16
N2 = META + L
FFN = 5632
FT = FFN // P
WINDOWS = (2, 4, 8, 16)
EPS = 1e-6
NEG = -1e30

ADA_FIRST = 8
CH = 1024
RING = 4

T_QA, T_QB, T_CQ, T_KA, T_VA, T_KB, T_VB, T_CKV, T_KPE = 0, 4, 10, 16, 20, 24, 26, 28, 32
NT = 33
T_QN, T_QR, T_KR, T_KN, T_VC = 0, 6, 10, 16, 22
T_COPY_C = (13, 14, 15, 28, 29, 30)
B_ORDER = [h for g in (0, 6) for a in range(g, g + 3) for h in (a, a + 3)]


def table(fields):
    at, out = 0, {}
    for name, n in fields:
        out[name] = (at, at + n)
        at += n
    return out, at


CONST, NCONST = table([
    ("ident", P), ("rev", P), ("rot", P), ("cos", L), ("sin", L), ("band", 2 * P), ("cols", GRID_W),
    ("pair", 66), ("cq", 34), ("ckv", 34), ("nope", 23), ("rope", 22), ("kpe", 12), ("mean", 1), ("halves", 2), ("sum4", 2), ("eps", 1)])
PARAM, NPARAM = table([
    ("b_ada", 2 * 48), ("norm_w", 2 * DT), ("qn_a", 2), ("kn_a", 2), ("qn_b", 2), ("kn_b", 2),
    ("qa_norm", 2 * 6), ("kva_norm", 2 * 4), ("qn_n", 2), ("qn_r", 2), ("kn_n", 2), ("kn_r", 2),
    ("sink", 2 * H_B), ("cond", 2 * DT), ("norm_mix", DT), ("b_gate", 2 * DT),
    ("pool_scale", DT), ("conv_w", 3 * DT), ("norm_ffn", DT), ("norm_final", DT)])


class Mark:
    __slots__ = ("of", "v")

    def __init__(self, of, v):
        self.of, self.v = of, v


class Count:

    def __init__(self, prog, handle=None, step=1):
        self.prog, self.handle, self.step, self.v = prog, handle, step, 0
        prog.counts.append(self)

    def inc(self, ins):
        ins.then_inc(self.handle, self.step)
        self.v += self.step
        m = Mark(self, self.v)
        self.prog.marks.append(m)
        return m


class Prog:

    def __init__(self, nc):
        self.nc, self.counts, self.marks = nc, [], []
        self.turn = None
        self.start, self.stride = {}, {}
        self.body = 0
        self.nsem = 0

    def sem(self, name, step=1):
        self.nsem += 1
        return Count(self, self.nc.alloc_semaphore(name), step)

    def value(self, of, v):
        if self.turn is None or v <= self.start[of] or not self.stride[of]:
            return v
        return v + (self.turn - 2) * self.stride[of]

    def wait(self, eng, *marks):
        best = {}
        for m in marks:
            if m is None:
                continue
            if isinstance(m, (list, tuple)):
                for x in m:
                    if x is not None and (x.of not in best or best[x.of] < x.v):
                        best[x.of] = x.v
            elif m.of not in best or best[m.of] < m.v:
                best[m.of] = m.v
        for of, v in best.items():
            eng.wait_ge(of.handle, self.value(of, v))

    def repeat(self, n, body):
        if n <= 3:
            for i in range(n):
                body(i)
            return
        assert self.turn is None
        body(0)
        start = {c: c.v for c in self.counts}
        body(1)
        after = {c: c.v for c in self.counts}
        self.marks = []
        with self.nc.Fori(2, n) as turn:
            self.turn, self.start = turn, start
            self.stride = {c: after[c] - start[c] for c in self.counts}
            self.body = 1
            body(turn)
        self.turn, self.body = None, 0
        for c in self.counts:
            assert c.v - after[c] == self.stride[c]
            c.v += (n - 3) * self.stride[c]
        for m in self.marks:
            m.v += (n - 3) * self.stride[m.of]
        self.marks = []


def host_chunks():
    out = []

    def stage(name, layer, kt, groups, mt):
        kpc = CH // (mt * P)
        for cols in groups:
            for k0 in range(0, kt, kpc):
                out.append((name, layer, k0, min(kpc, kt - k0), cols))

    def span(a, n):
        return [[(a + i, a + i + 512)] for i in range(0, n, 512)]

    for l in range(DEPTH):
        stage("w_ada", l, DT, span(0, 3 * D), 4)
    conditioning = out[ADA_FIRST * 8:]
    del out[ADA_FIRST * 8:]

    def conditioned(groups):
        out.extend(conditioning[:8 * groups])
        del conditioning[:8 * groups]

    qa, ka, va = 0, 512, 1024
    qb, kb, vb = 1536, 2304, 2560
    cq, ckv, kpe, z = 2816, 3584, 4096, 4160
    qb_cols = [(qb + h * HD, qb + h * HD + HD) for h in B_ORDER]
    z_cols = [(z, z + 512)] + [(z + 512 + h * HD, z + 512 + h * HD + HD) for h in B_ORDER] + [
        (z + 1280, z + 2048)]

    def grouped(cols):
        flat = [c for a, b in cols for c in range(a, b, HD)]
        return [[(c, c + HD) for c in flat[i:i + 8]] for i in range(0, len(flat), 8)]

    for l in range(DEPTH):
        stage("w_in", l, DT, grouped(z_cols), 4)
        stage("w_in", l, DT, grouped([(qa, qa + 512)] + qb_cols + [(cq, cq + 768)]), 4)
        stage("w_in", l, DT, grouped([(ka, ka + 512), (va, va + 512), (kb, kb + 256),
                                      (vb, vb + 256), (ckv, ckv + 512)]), 4)
        stage("w_in", l, DT, [[(kpe, kpe + HD)] * 2], 1)
        if l == 0:
            conditioned(10)
        c = [(h * QK_C, h * QK_C + NOPE) for h in range(H_C)]
        c += [(h * QK_C + NOPE, (h + 1) * QK_C) for h in range(H_C)]
        flat = [x for a, b in c for x in range(a, b, HD)]
        stage("w_qb", l, 6, [[(x, x + HD) for x in flat[i:i + 6]] for i in range(0, 18, 6)], 3)
        c = [(h * 256, h * 256 + NOPE) for h in range(H_C)]
        c += [(h * 256 + NOPE, h * 256 + 256) for h in range(H_C)]
        stage("w_kvb", l, 4, [c[i:i + 4] for i in range(0, 12, 4)], 4)
        if l == 0:
            conditioned(6)
            assert not conditioning
        stage("w_out", l, DT, span(0, D), 4)
    stage("w_in_2", None, DT, span(0, D), 4)
    for j in range(4):
        for part in (2, 3, 1):
            stage("w_in_2", None, DT, span(part * D + j * 512, 512), 4)
            if (j, part) == (0, 2):
                for g in range(4):
                    stage("pool_w_2", g, 4, span(0, 512), 4)
    for j in range(4):
        for part in (4, 5):
            stage("w_in_2", None, DT, span(part * D + j * 512, 512), 4)
        stage("conv_out_w_2", None, DT, span(j * 512, 512), 4)
    stage("w_o_2", None, DT, span(0, D), 4)
    stage("w_gate_up_2", None, DT,
          [[(g * 256, g * 256 + 256), (FFN + g * 256, FFN + g * 256 + 256)] for g in range(FT // 2)], 4)
    stage("w_down_2", None, FT, span(0, D), 4)
    return out


def build(nc, stream, xT, metaT, const_d, param_d, sel_d, rpb_d, z_d, x_d, out_d, dbg=None):
    pr = Prog(nc)
    wait, value = pr.wait, pr.value
    SP, AC, VE, PO, PE = nc.sync, nc.scalar, nc.vector, nc.gpsimd, nc.tensor

    act_n, dve_n, pool_n, pe_n = (pr.sem(n) for n in ("act_n", "dve_n", "pool_n", "pe_n"))
    raw_n = [pr.sem(f"raw_n{i}", 16) for i in range(RING)]
    load_n = [pr.sem(f"load_n{i}", 16) for i in range(10)]
    store_n = [pr.sem(f"store_n{i}", 16) for i in range(7)]
    chunk = Count(pr)

    def act(ins):
        return act_n.inc(ins)

    def dve(ins):
        return dve_n.inc(ins)

    def pool(ins):
        return pool_n.inc(ins)

    def pe(ins):
        return pe_n.inc(ins)

    base = (nc.sbuf_base + 63) // 64 * 64
    place = [base]

    def region(nbytes):
        at = place[0]
        place[0] += (nbytes + 31) // 32 * 32
        return at

    def sb(name, shape, dt, at):
        n = 4 * int(np.prod(shape[1:]))
        assert at + n <= nc.sbuf_usable_end, (name, at + n)
        return nc.alloc_sbuf_tensor_at("sb_" + name, list(shape), dt, offset=at)

    def own(name, shape, dt=F32):
        return sb(name, shape, dt, region(4 * int(np.prod(shape[1:]))))

    const = own("const", [P, NCONST])
    param = own("param", [P, NPARAM])
    ada = own("ada", [P, 2 * 48, 2])
    amul = own("amul", [P, DT, 2])
    cond = own("cond", [P, DT, 2])
    cond4 = own("cond4", [P, DT, 4], F32R)
    wq8 = own("wq8", [P, 8])
    nsink = own("nsink", [P, H_B])
    stat = own("stat", [P, 4, 4])
    raw = own("raw", [P, RING, CH])
    whi = own("whi", [P, RING, CH], F32R)
    wlo = own("wlo", [P, RING, CH], F32R)
    block = region(153600)
    HB = 16 * 512 * 4
    HH = sb("hi", [P, DT, 512], F32R, block)
    HL = sb("lo", [P, DT, 512], F32R, block + HB)
    T = sb("T", [P, NT, 512], F32, block + 2 * HB)
    tmp_at = block + 2 * HB + NT * 2048
    TMP = sb("tmp", [P, 10, 512], F32, tmp_at)
    arow = sb("arow", [4, 512], F32, tmp_at)
    sel = sb("sel", [32, 16, P], F32, tmp_at)
    bias = [sb(f"bias{t}", [P, 4 * H_A, GRID_W], F32, block + t * HB + 10 * 2048) for t in range(2)]
    q_up = sb("q_up", [P, 2, 512], F32, block + 14 * 2048)
    pt_up = sb("pt_up", [P, 4, 256], F32, block + HB + 14 * 2048)
    HF = sb("hi_f32", [P, DT, 512], F32, block)
    LF = sb("lo_f32", [P, DT, 512], F32, block + HB)
    NB = DT * N2 * 4
    PH = sb("pooled_hi", [P, DT, N2], F32R, block)
    PL = sb("pooled_lo", [P, DT, N2], F32R, block + NB)
    CHI = sb("conv_hi", [P, DT, N2], F32R, block + 2 * NB)
    CLO = sb("conv_lo", [P, DT, N2], F32R, block + 3 * NB)
    YA = sb("ya", [P, DT, N2], F32, block + 4 * NB)
    G4 = sb("g4", [P, 4, N2], F32, block + 5 * NB)
    FH = sb("ffn_hi", [P, FT, N2], F32R, block)
    FL = sb("ffn_lo", [P, FT, N2], F32R, block + FT * N2 * 4)
    hn_at = block + 2 * FT * N2 * 4
    NH = sb("hn_hi", [P, DT, N2], F32R, hn_at)
    NL = sb("hn_lo", [P, DT, N2], F32R, hn_at + NB)
    t3_at = hn_at + 2 * NB
    res_at = block + 153600 - NB
    assert t3_at + 4 * N2 * 4 <= res_at and block + 5 * NB + 4 * (N2 + 2) * 4 <= hn_at
    RES = sb("res", [P, DT, N2], F32, res_at)
    T2 = sb("tmp2", [P, 8, N2 + 16], F32, block + 3 * NB)
    T3 = sb("tmp3", [P, 4, N2], F32, t3_at)
    T4 = sb("tmp4", [P, 4, N2], F32, hn_at)
    CV = sb("cv", [P, 4, N2 + 2], F32, block + 5 * NB)
    PS = nc.alloc_psum_tensor("ps", [P, 8, 512], F32)

    def C(name, rows=P):
        a, b = CONST[name]
        return const[0:rows, a:b]

    def Pm(name, i, n=1):
        a = PARAM[name][0] + i
        return param[:, a:a + n]

    ident = C("ident")

    def load(q, eng, out, in_):
        return load_n[q].inc(eng.dma_start(out, in_))

    def store(q, eng, out, in_):
        return store_n[q].inc(eng.dma_start(out, in_))

    table_in = [load(0, PO, const[:, :], const_d), load(0, PO, param[:, :], param_d)][-1]

    raw_free = [None] * RING
    hl_free = [None] * RING
    st = {"pos": 0, "set": 0, "ahead": []}

    def next_weights(width, by_pool=False):
        s = st["pos"] % RING
        st["pos"] += 1
        wait(SP, raw_free[s])
        landed = raw_n[s].inc(SP.dma_start(raw[:, s, 0:width], stream[value(chunk, chunk.v)][:, 0:width]))
        chunk.v += 1
        wait(AC, landed, hl_free[s])
        rounded = act(AC.activation(whi[:, s, 0:width], raw[:, s, 0:width], ACT.Copy))
        lo_by, count = (PO, pool) if by_pool else (VE, dve)
        wait(lo_by, rounded, landed, hl_free[s])
        split = count(lo_by.tensor_tensor(wlo[:, s, 0:width], raw[:, s, 0:width],
                                          whi[:, s, 0:width].bitcast(F32), ALU.subtract))
        raw_free[s] = split
        return s, split

    set_free = [[], []]
    pend = []

    def step_evac():
        if pend:
            fn, g, bank0, done = pend[0]
            rest = st.pop("rest", None) or fn(g, bank0, done)
            if not isinstance(rest, list):
                try:
                    next(rest)
                    st["rest"] = rest
                    return
                except StopIteration as end:
                    rest = end.value
            set_free[bank0 // 4] = rest
            pend.pop(0)

    def flush():
        while pend:
            step_evac()

    def next_set():
        st["set"] ^= 1
        return 4 * (st["set"] ^ 1)

    def ahead(n, width, by_pool=False):
        for _ in range(n):
            st["ahead"].append(next_weights(width, by_pool))

    def weights(width):
        return st["ahead"].pop(0) if st["ahead"] else next_weights(width)

    def gemm(groups, kt, mt, n, hi, lo, evac, ready=None):
        kpc = CH // (mt * P)
        nch = -(-kt // kpc)

        def one(g, first):
            bank0 = next_set()
            free = set_free[bank0 // 4]
            for c in range(nch):
                ks = list(range(c * kpc, min(kt, (c + 1) * kpc)))
                s, split = weights(len(ks) * mt * P)
                made = [ready(k) if callable(ready) else ready[k] for k in ks] if first and ready else []
                wait(PE, split)
                for j, k in enumerate(ks):
                    if made:
                        wait(PE, made[j])
                    for m in range(mt):
                        if k == 0 and (m == 0 or len(free) == 4):
                            wait(PE, free[m] if len(free) == 4 else free)
                        o = PS[:, bank0 + m, 0:n]
                        w0 = (j * mt + m) * P
                        wh, wl = whi[:, s, w0:w0 + P], wlo[:, s, w0:w0 + P]
                        PE.matmul(o, wh, hi[:, k, 0:n], start=(k == 0), stop=False)
                        PE.matmul(o, wh, lo[:, k, 0:n], start=False, stop=False)
                        mm = PE.matmul(o, wl, hi[:, k, 0:n], start=False, stop=(k == kt - 1))
                hl_free[s] = done = pe(mm)
                if c == nch - 1:
                    flush()
                elif c >= RING - 1:
                    step_evac()
            pend.append((evac, g, bank0, done))

        def turn(i):
            if pr.body:
                pend[:] = [(evac, 2 * (i - 1) + 1, pend[0][2], pend[0][3])]
            for u in range(2):
                one(2 * i + u, pr.body == 0 and i == 0 and u == 0)

        if groups % 2 == 0 and groups > 4:
            assert 2 * nch % RING == 0
            pr.repeat(groups // 2, turn)
            pend[:] = [(evac, groups - 1, pend[0][2], pend[0][3])]
        else:
            for g in range(groups):
                one(g, g == 0)

    wait(AC, table_in)
    wait(VE, table_in)
    a0 = PARAM["cond"][0]
    silu_c = act(AC.activation(cond[:, :, :].rearrange("p a b -> p (a b)"), param[:, a0:a0 + 2 * DT], ACT.Silu))
    wait(AC, silu_c)
    chi = act(AC.activation(cond4[:, :, 0:2], cond[:, :, :], ACT.Copy))
    wait(VE, chi)
    cond_ready = dve(VE.tensor_tensor(cond4[:, :, 2:4], cond[:, :, :], cond4[:, :, 0:2].bitcast(F32),
                                      ALU.subtract))
    s0 = PARAM["sink"][0]
    for l in range(DEPTH):
        for j, (name, scale) in enumerate((("qn_a", HD ** -0.5), ("qn_b", HD ** -0.5),
                                           ("qn_n", QK_C ** -0.5), ("qn_r", QK_C ** -0.5))):
            consts_ready = dve(VE.tensor_scalar(wq8[:, 4 * l + j:4 * l + j + 1], Pm(name, l), float(scale),
                                                None, ALU.mult))

    ada_last = {}
    ada_g = ada[:, :, :].rearrange("p (g m) s -> p g m s", m=4)
    b_ada_g = Pm("b_ada", 0, 2 * 48).rearrange("p (g m) -> p g m", m=4)

    ada_pend = []
    ada_free = [None, None]
    ada_row = [arow]

    def ada_flush(parts=(0, 1, 2)):
        if not ada_pend:
            return
        g, b, done = ada_pend[0]
        row = ada_row[0]
        if 0 in parts:
            wait(AC, done, ada_last.get("turned"))
            ada_last["row"] = act(AC.activation(row[:, :], PS[0:4, 6 + b, :], ACT.Copy))
        if 1 in parts:
            wait(PE, ada_last["row"], ada_last.get("added"))
            for m in range(4):
                mm = PE.matmul(PS[:, 6 + b, 2 * m:2 * m + 2], row[:, m * P:(m + 1) * P], C("sum4", 4),
                               start=True, stop=True)
            ada_last["turned"] = pe(mm)
        if 2 in parts:
            wait(VE, ada_last["turned"])
            for s in range(2):
                added = dve(VE.tensor_tensor(ada_g[:, g, :, s], PS[:, 6 + b, s:8:2], b_ada_g[:, g, :], ALU.add))
            ada_last["added"] = ada_free[b] = added
            ada_pend.pop(0)

    def ada_chunk(g, c, b):
        s, split = weights(CH)
        wait(PE, split, cond_ready)
        if c == 0:
            wait(PE, ada_free[b])
        for j in range(2):
            k = 2 * c + j
            o = PS[0:4, 6 + b, :]
            PE.matmul(o, cond4[:, k, :], whi[:, s, j * 512:(j + 1) * 512], start=(k == 0), stop=False)
            mm = PE.matmul(o, cond4[:, k, :], wlo[:, s, j * 512:(j + 1) * 512], start=False,
                           stop=(k == DT - 1))
        hl_free[s] = done = pe(mm)
        return done

    def ada_turn(i):
        if pr.body:
            ada_pend[:] = [(2 * (i - 1) + 1, 1, ada_pend[0][2])]
        for u in range(2):
            for c in range(8):
                done = ada_chunk(2 * i + u, c, u)
                if pr.body == 0 and i == 0 and (u or c >= 4):
                    first_squares()
                if c == RING - 1:
                    ada_flush()
            ada_pend.append((2 * i + u, u, done))

    def ada_beside(first, row):
        ada_row[0] = row
        at = [0]

        def step():
            g, c = divmod(at[0], 8)
            at[0] += 1
            done = ada_chunk(first + g, c, g % 2)
            if c in (2, 4, 6):
                ada_flush([c // 2 - 1])
            if c == 7:
                ada_pend.append((first + g, g % 2, done))
        return step

    ring = {}

    def slot(name, n):
        r = ring.setdefault(name, [0, [None] * n])
        i = r[0] % n
        r[0] += 1
        return i, r

    def root(src, dst, marks, n, mean_scale=1.0):
        wait(AC, *marks)
        rows = dst.shape[0]
        r = act(AC.activation(dst, src, ACT.Sqrt, bias=C("eps", rows), scale=mean_scale))
        wait(VE, r)
        return dve(VE.reciprocal(dst, dst)), r

    def layer(l, x_tiles, x_ready):
        last = l == DEPTH - 1
        nq = L if last else L + LC
        streams = 1 if last else 2
        A0 = 48 * l
        wait(VE, Mark(dve_n, dve_n.v), ring.get("amul_free"))
        for s in range(2):
            nw = param[:, PARAM["norm_w"][0] + DT * l:PARAM["norm_w"][0] + DT * (l + 1)]
            am = dve(VE.scalar_tensor_tensor(amul[:, :, s], ada[:, A0 + DT:A0 + 2 * DT, s], 1.0, nw,
                                             ALU.add, ALU.mult))
        wait(VE, am)
        wait(AC, am)
        acc = ring["acc"]
        wait(PE, acc, *set_free)
        msq = pe(PE.matmul(PS[:, 7, :], C("mean").to_broadcast([P, P]), TMP[:, 5, :], start=True, stop=True))
        rstd, rt = root(PS[:, 7, :], TMP[:, 4, :], [msq], 512)
        set_free[1] = [rt]
        hs = {"free": [[None] * 2 for _ in range(2)], "last": None}
        wait(VE, rstd)

        def make_h(k):
            i = k % 2
            if k == 0:
                wait(AC, ring.get("y_free"))
            wait(VE, hs["free"][0][i], x_ready[k])
            for s in range(2):
                c = slice(256 * s, 256 * s + 256)
                m1 = dve(VE.scalar_tensor_tensor(TMP[:, 6 + i, c], x_tiles(k)[:, c], amul[:, k, s:s + 1],
                                                 TMP[:, 4, c], ALU.mult, ALU.mult))
            wait(AC, m1, hs["free"][1][i])
            for s in range(2):
                c = slice(256 * s, 256 * s + 256)
                m2 = act(AC.activation(TMP[:, 8 + i, c], TMP[:, 6 + i, c], ACT.Identity,
                                       bias=ada[:, A0 + k, s:s + 1]))
            hs["free"][0][i] = m2
            wait(AC, m2)
            m3 = act(AC.activation(HH[:, k, :], TMP[:, 8 + i, :], ACT.Copy))
            wait(VE, m3)
            m4 = dve(VE.tensor_tensor(HL[:, k, :], TMP[:, 8 + i, :], HH[:, k, :].bitcast(F32), ALU.subtract))
            hs["free"][1][i] = hs["last"] = m4
            ring["amul_free"] = m1
            return m4

        x_kept = ring.get("x_stored")

        zr = {"free": [None] * 4}

        def z_evac(g, bank0, done):
            wait(AC, done, hs["last"])
            out = []
            for m in range(4):
                wait(AC, zr["free"][m])
                out.append(act(AC.activation(TMP[:, 6 + m, 0:nq], PS[:, bank0 + m, 0:nq], ACT.Silu)))
                wait(PO, out[m])
                zr["free"][m] = store(m, PO, z_d[4 * g + m][:, 0:nq], TMP[:, 6 + m, 0:nq])
            return out

        def to_T(t0, n):
            def evac(g, bank0, done):
                wait(AC, done, x_kept)
                wait(VE, done, x_kept)
                out = []
                for m in range(4):
                    dst = T[:, t0 + 4 * g + m, 0:n]
                    if m % 2:
                        out.append(act(AC.activation(dst, PS[:, bank0 + m, 0:n], ACT.Copy)))
                    else:
                        out.append(dve(VE.tensor_copy(dst, PS[:, bank0 + m, 0:n])))
                return out
            return evac

        gemm(4, DT, 4, nq, HH, HL, z_evac, make_h)
        gemm(4, DT, 4, nq, HH, HL, to_T(T_QA, nq))
        gemm(4, DT, 4, 512, HH, HL, to_T(T_KA, 512))

        def kpe_evac(g, bank0, done):
            wait(AC, done)
            return [act(AC.activation(T[:, T_KPE, :], PS[:, bank0, :], ACT.Copy))]

        gemm(1, DT, 1, 512, HH, HL, kpe_evac)
        z_stored = list(zr["free"])
        ahead(3 if last else RING, 2 * 3 * P if last else CH)
        flush()
        proj = [set_free[0], set_free[1]]
        everything = lambda: [Mark(x, x.v) for x in (act_n, dve_n, pe_n, pool_n)]

        jobs = [(T_QA + t, "pair", t, nq) for t in range(4)]
        jobs += [(T_KA + t, "pair", 4 + t, 512) for t in range(4)]
        jobs += [(T_QB + t, "pair", 8 + t, nq) for t in range(6)]
        jobs += [(T_KB + t, "pair", 14 + t, 512) for t in range(2)]
        jobs += [(T_CQ + t, "cq", 0, nq) for t in range(6)]
        jobs += [(T_CKV + t, "ckv", 0, 512) for t in range(4)]
        jobs.sort(key=lambda j: -j[3])
        all_done = everything()
        wait(PO, all_done)
        sel_in = load(1, PO, sel[:, :, :], sel_d)
        wait(AC, all_done, z_stored)
        wait(PE, all_done)
        wait(VE, all_done)
        def turn_values(t0, nf, marks, b0=0, by_dve=False):
            wait(PE, marks)
            flat = T[:, t0:t0 + nf, :].rearrange("p a b -> p (a b)")
            for t in range(4):
                for f in range(nf):
                    at = (t * nf + f) * P
                    mm = PE.transpose(PS[:, b0 + at // 512, at % 512:at % 512 + P],
                                      T[:, t0 + f, t * P:(t + 1) * P], ident)
            m = pe(mm)
            if not by_dve:
                wait(AC, m)
            wait(VE, m)
            out = []
            for b in range(nf):
                if b % 2 and not by_dve:
                    out.append(act(AC.activation(T[:, t0 + b, :], PS[:, b0 + b, :], ACT.Copy)))
                else:
                    out.append(dve(VE.tensor_copy(T[:, t0 + b, :], PS[:, b0 + b, :])))
            return out

        turn_values(T_VA, 4, None, 0, True)
        turn_values(T_VB, 2, None, 4, True)

        wait(SP, everything())
        pad = 2 * GRID_W - 1
        for t in range(2):
            for half in range(2):
                off = (l * (2 * NA_ROWS - 1) + NA_ROWS - 1 - (2 * t + half)) * H_A * pad
                src = bass.AP(rpb_d.tensor, off, [[1, 64], [pad, 4 * H_A], [1, 64]])
                load(2 + t, SP, bias[t][64 * half:64 * half + 64, :, :], src)
        masked = []
        for t in range(2):
            wait(PO, Mark(load_n[2 + t], load_n[2 + t].v))
            masked.append(pool(PO.tensor_tensor(bias[t][:, :, :], bias[t][:, :, :],
                                                C("cols").unsqueeze(1).to_broadcast([P, 4 * H_A, 64]), ALU.add)))


        def fan_in(jobs, rows, lhs, nb):
            free = [None] * 3
            for n, (tile, kind, t, cols) in enumerate(jobs):
                i = n % 3
                wait(AC, free[i])
                a = act(AC.activation(TMP[:, 5 + i, 0:cols], T[:, tile, 0:cols], ACT.Square))
                wait(PE, a)
                free[i] = pe(PE.matmul(PS[0:rows, nb, 0:cols], lhs(kind, t), TMP[:, 5 + i, 0:cols],
                                       start=(n == 0), stop=(n == len(jobs) - 1)))
            return free[i]

        def lhs1(kind, t):
            a = CONST[kind][0]
            if kind == "pair":
                return const[:, a + 32 - 2 * t:a + 32 - 2 * t + 34]
            return const[:, a:a + 34]

        done = fan_in(jobs, 34, lhs1, 7)
        rr, _ = root(PS[0:34, 7, :], TMP[0:34, 4, :], [done], 512)
        weights = {T_QA: (wq8[:, 4 * l:4 * l + 1], 4), T_KA: (Pm("kn_a", l), 4),
                   T_QB: (wq8[:, 4 * l + 1:4 * l + 2], 6), T_KB: (Pm("kn_b", l), 2)}

        def spread(n, tile, lhs, rhs, wgt, cols, free, rows=slice(0, P), src=None):
            b = n % 4
            wait(PE, free[b])
            m = pe(PE.matmul(PS[:, b, 0:cols], lhs, rhs[:, 0:cols], start=True, stop=True))
            wait(VE, m)
            src = T[rows, tile, 0:cols] if src is None else src
            free[b] = dve(VE.scalar_tensor_tensor(T[rows, tile, 0:cols], src, wgt, PS[rows, b, 0:cols],
                                                  ALU.mult, ALU.mult))
            return free[b]

        wait(PE, rr, sel_in, Mark(dve_n, dve_n.v))
        free = [None] * 4
        normed = {}
        for n, (tile, kind, t, cols) in enumerate(jobs):
            if kind == "pair":
                lo_ = max(k for k in weights if k <= tile)
                normed[tile] = spread(n, tile, sel[:, t, :], TMP[0:32, 4, :], weights[lo_][0], cols, free)
            else:
                r = 32 + (kind == "ckv")
                base_, w_ = (T_CQ, "qa_norm") if kind == "cq" else (T_CKV, "kva_norm")
                i = tile - base_
                w_ap = Pm(w_, (6 if kind == "cq" else 4) * l + i)
                normed[tile] = spread(n, tile, const[0:34, r:r + 1].to_broadcast([34, P]), TMP[0:34, 4, :],
                                      w_ap, cols, free)

        def rope(tiles, marks, tmp=(6, 7)):
            free = [None] * 4
            tf = [None] * 2
            out = {}
            for n, tile in enumerate(tiles):
                b, i = n % 4, n % 2
                wait(PE, free[b], marks[tile])
                m = pe(PE.matmul(PS[:, b, 0:L], C("rot"), T[:, tile, 0:L], start=True, stop=True))
                wait(VE, m, tf[i])
                v = dve(VE.tensor_tensor(TMP[:, tmp[i], 0:L], PS[:, b, 0:L], C("sin"), ALU.mult))
                free[b] = v
                wait(PO, m)
                c = pool(PO.tensor_tensor(T[:, tile, 0:L], T[:, tile, 0:L], C("cos"), ALU.mult))
                wait(VE, v, c)
                tf[i] = out[tile] = dve(VE.tensor_tensor(T[:, tile, 0:L], T[:, tile, 0:L],
                                                         TMP[:, tmp[i], 0:L], ALU.add))
            return out

        wait(PE, *[m for m in free])
        wait(VE, done)
        roped = rope([T_QB + t for t in range(6)] + [T_KB + t for t in range(2)], normed)

        wait(VE, everything())
        wait(AC, everything())
        wait(PE, everything(), masked)
        wait(PO, everything(), *z_stored)
        ns = dve(VE.tensor_scalar(nsink[:, :], param[:, s0 + H_B * l:s0 + H_B * (l + 1)], -1.0, None, ALU.mult))
        wait(VE, ns)
        wait(AC, ns)
        state = {"S": [None] * 3, "P": [None] * 3, "PT": {}, "T": [None] * 2, "O": {},
                 "z": None, "stat": [None] * 4, "y": None, "copy": {}, "n": 0, "t": 0, "last_s": [None] * 2}
        queue = []

        def later(due, fn):
            queue.append((due, fn))

        def run_due(u):
            while any(due <= u for due, _ in queue):
                n = min(n for n, (due, _) in enumerate(queue) if due == min(d for d, _ in queue))
                queue.pop(n)[1]()

        def unit(u, terms, nk, sinks):
            b = u % 3
            wait(PE, state["S"][b])
            for j, (lt, rt_, c0, cn) in enumerate(terms):
                mm = PE.matmul(PS[:, b, c0:c0 + cn], lt, rt_, start=(j == 0), stop=(j == len(terms) - 1),
                               skip_group_check=True)
            scored = pe(mm)
            i = u % 4
            wait(VE, scored, state["stat"][i])
            S = PS[:, b, 0:nk]
            mx = dve(VE.tensor_reduce(stat[:, i, 0:1], S, AXX, ALU.max, negate=True))
            if sinks is not None:
                wait(VE, mx)
                mx = dve(VE.tensor_tensor(stat[:, i, 0:1], stat[:, i, 0:1], sinks[0], ALU.min))
            wait(AC, mx, state["P"][b], state["stat"][i])
            ex = act(AC.activation(TMP[:, b, 0:nk], S, ACT.Exp, bias=stat[:, i, 0:1],
                                   accum_out=stat[:, i, 1:2]))
            state["S"][b] = ex
            state["stat"][i] = ex
            if sinks is not None:
                ex = act(AC.activation(stat[:, i, 3:4], sinks[1], ACT.Exp, bias=stat[:, i, 0:1]))
                state["stat"][i] = ex

            return b, ex

        def normalise(u, b, nk, ex, sinks):
            i = u % 4
            wait(VE, ex)
            if sinks is not None:
                sm = dve(VE.tensor_tensor(stat[:, i, 1:2], stat[:, i, 1:2], stat[:, i, 3:4], ALU.add))
                wait(VE, sm)
            rc = dve(VE.reciprocal(stat[:, i, 2:3], stat[:, i, 1:2]))
            wait(VE, rc)
            pn = dve(VE.tensor_scalar(TMP[:, b, 0:nk], TMP[:, b, 0:nk], stat[:, i, 2:3], None, ALU.mult))
            state["stat"][i] = pn
            return pn

        def turned(u, b, pn, nk, pt, q0, pt_free):
            tb = 3 + u % 2
            wait(PE, pn, state["T"][u % 2])
            for kt in range(nk // P):
                mm = PE.transpose(PS[:, tb, kt * P:(kt + 1) * P], TMP[:, b, kt * P:(kt + 1) * P], ident)
            m = pe(mm)
            state["P"][b] = m
            src = PS[:, tb, 0:nk].rearrange("p (a b) -> p a b", b=P)
            dst = pt[:, :, q0:q0 + P]
            if u % 2:
                wait(AC, m, pt_free)
                e = act(AC.activation(dst, src, ACT.Copy))
            else:
                wait(VE, m, pt_free)
                e = dve(VE.tensor_copy(dst, src))
            state["T"][u % 2] = e
            return e

        PTL = TMP[:, 8:10, :].rearrange("p a b -> p (a b)").rearrange("p (k q) -> p k q", q=256)
        PTC = TMP[:, 5, :].rearrange("p (k q) -> p k q", q=256)
        PTC_UP = TMP[:, 3, :].rearrange("p (k q) -> p k q", q=256)
        PT = {(0, 0, False): PTL, (0, 0, True): PTC, (0, 1, False): pt_up, (0, 1, True): PTC_UP}
        if last:
            PT[(1, 0, False)] = LF[:, 0:4, 256:512]
            PT[(1, 1, False)] = HF[:, 0:4, 256:512]
        PTL_UP = T[:, 31:33, :].rearrange("p a b -> p (a b)").rearrange("p (k q) -> p k q", q=256)
        PT_C = {(0, 0, False): PTL, (0, 0, True): PTC, (1, 0, False): PTL_UP, (1, 0, True): PTC_UP}

        def halves_apart(i, tile):
            wait(AC, state["last_s"][i % 2])
            a = act(AC.activation(q_up[:, i % 2, 0:nq], T[:, tile, 0:nq], ACT.Copy, scale=C("halves")[:, 1:2]))
            wait(AC, a)
            state["q"] = act(AC.activation(T[:, tile, 0:nq], T[:, tile, 0:nq], ACT.Copy,
                                           scale=C("halves")[:, 0:1]))
            return state["q"]

        def y_tile(side, heads, score_terms, v_of, v_rows, y_index, sinks_of, zbuf, PT):
            zin = []
            us = [(h, 2 * c + j) for c in range(streams) for h in range(heads) for j in range(2)]
            pt_marks = []
            pset = state["t"] % (1 + ((1, 0, False) in PT))
            o_bank = 5 + (state["t"] % 2 if last else 0)
            state["t"] += 1

            def after(u, h, qt, b, pn):
                ctx_ = qt >= 2
                pt_marks.append(turned(u, b, pn, 256 if ctx_ else 512, PT[(pset, h, ctx_)], P * (qt % 2),
                                       state["PT"].get((pset, ctx_))))
                if qt % 2 == 0 or h < heads - 1:
                    return
                kts = [2, 3] if ctx_ else [0, 1, 2, 3]
                per = max(1, len(kts) // (2 * heads))
                for n in range(0, len(kts), per):
                    later(u + 3 + n // per, lambda n=n: values(ctx_, kts, n, per))
                if (h, qt) == us[-1]:
                    zin.append(z_load())
                    end = u + 3 + len(kts) // per
                    later(end, finish)
                    later(end + 1, finish_lo)

            def z_load():
                wait(PO, state["zfree"][zbuf])
                return load(zbuf + 2, PO, TMP[:, zbuf, 0:nq], z_d[y_index][:, 0:nq])

            def values(ctx_, kts, n0, per):
                wait(PE, pt_marks, state["O"].get(o_bank) if not ctx_ and n0 == 0 else None)
                c0 = 256 * ctx_
                for n in range(n0, n0 + per):
                    for hh in range(heads):
                        mm = PE.matmul(PS[v_rows(hh), o_bank, c0:c0 + 256], v_of(hh, kts[n]),
                                       PT[(pset, hh, ctx_)][:, n, :], start=(n == 0), stop=(n == len(kts) - 1))
                state["PT"][(pset, ctx_)] = state["o_done"] = pe(mm)

            def finish():
                wait(VE, state["o_done"], zin, state["y"])
                y1 = dve(VE.tensor_tensor(TMP[:, 4, 0:nq], PS[:, o_bank, 0:nq], TMP[:, zbuf, 0:nq], ALU.mult))
                state["O"][o_bank] = y1
                state["zfree"][zbuf] = y1
                wait(AC, y1, side and ada_last["turned"])
                state["y_hi"] = act(AC.activation(HH[:, y_index, 0:nq], TMP[:, 4, 0:nq], ACT.Copy))

            def finish_lo():
                wait(VE, state["y_hi"])
                state["y"] = dve(VE.tensor_tensor(HL[:, y_index, 0:nq], TMP[:, 4, 0:nq],
                                                  HH[:, y_index, 0:nq].bitcast(F32), ALU.subtract))

            for h, qt in us:
                u = state["n"]
                state["n"] += 1
                nk = 256 if qt >= 2 else 512
                sinks = sinks_of(h) if sinks_of else None
                b, ex = unit(u, score_terms(h, qt), nk, sinks)
                state["scored"] = Mark(pe_n, pe_n.v)
                if side:
                    side(u, False)
                marks = {}
                later(u + 1, lambda u=u, b=b, nk=nk, ex=ex, sinks=sinks, marks=marks:
                      marks.update(pn=normalise(u, b, nk, ex, sinks)))
                later(u + 2, lambda u=u, h=h, qt=qt, b=b, marks=marks: after(u, h, qt, b, marks["pn"]))
                run_due(u)
                if side:
                    side(u, True)

        state["zfree"] = {6: None, 7: None}

        def drain():
            run_due(1 << 30)

        def half(h):
            return slice(64 * (h % 2), 64 * (h % 2) + 64)

        side = None
        if not last:
            step_ab = ada_beside(ADA_FIRST, HF[0:4, 9, :])

            def side(u, split):
                if split:
                    ahead(1, CH if u < 80 - RING else 2 * 3 * P, u % 4 < 3)
                else:
                    step_ab()
        q_tiles = [T_QA + i for i in range(4)] + [T_QB + i for i in range(6)]
        q_apart = [halves_apart(0, q_tiles[0])]

        def next_queries(n):
            wait(PE, q_apart[n])
            if n + 1 < len(q_tiles):
                q_apart.append(halves_apart(n + 1, q_tiles[n + 1]))

        for i in range(4):
            next_queries(i)

            def terms(h, qt, i=i):
                q = (q_up[:, i % 2, :] if h else T[:, T_QA + i, :])[:, P * qt:P * qt + P]
                if qt >= 2:
                    return [(q, T[:, T_KA + i, 256:512], 0, 256)]
                return [(q, T[:, T_KA + i, :], 0, 512),
                        (C("rev"), bias[qt][:, 2 * i + h::H_A, :], 0, 256)]

            def v_of(h, kt, i=i):
                return T[:, T_VA + kt, P * i + 64 * h:P * i + 64 * h + 64]

            zb = 6 + i % 2
            y_tile(side, 2, terms, v_of, half, i, None, zb, PT)
            state["last_s"][i % 2] = state["scored"]
        for i in range(6):
            kvt = i // 3
            next_queries(4 + i)

            def terms(h, qt, i=i, kvt=kvt):
                q = (q_up[:, i % 2, :] if h else T[:, T_QB + i, :])[:, P * qt:P * qt + P]
                if qt >= 2:
                    return [(q, T[:, T_KB + kvt, 256:512], 0, 256)]
                a = CONST["band"][0] + P * qt
                return [(q, T[:, T_KB + kvt, :], 0, 512),
                        (ident, const[:, a:a + P], P * (1 - qt), P)]

            vflat = T[:, T_VB:T_VB + 2, :].rearrange("p a b -> p (a b)")

            def v_of(h, kt, kvt=kvt):
                c = 256 * kt + P * kvt + 64 * h
                return vflat[:, c:c + 64]

            def sinks_of(h, i=i):
                c = s0 + H_B * l + 2 * i + h
                return nsink[:, 2 * i + h:2 * i + h + 1], param[:, c:c + 1]

            zb = 6 + i % 2
            y_tile(side, 2, terms, v_of, half, 4 + i, sinks_of, zb, PT)
            state["last_s"][i % 2] = state["scored"]
        drain()
        if not last:
            wait(AC, everything())
            ada_row[0] = arow
            ada_flush()

        def split_of(t0, cols):
            def make(k):
                a = act(AC.activation(HH[:, 10 + k, 0:cols], T[:, t0 + k, 0:cols], ACT.Copy))
                wait(VE, a)
                return dve(VE.tensor_tensor(HL[:, 10 + k, 0:cols], T[:, t0 + k, 0:cols],
                                            HH[:, 10 + k, 0:cols].bitcast(F32), ALU.subtract))
            return make

        def evac_c(t0, mt, n):
            def evac(g, bank0, done):
                wait(AC, done)
                wait(VE, done)
                marks = []
                for m in range(mt):
                    dst = T[:, t0 + mt * g + m, 0:n]
                    if m % 2:
                        marks.append(act(AC.activation(dst, PS[:, bank0 + m, 0:n], ACT.Copy)))
                    else:
                        marks.append(dve(VE.tensor_copy(dst, PS[:, bank0 + m, 0:n])))
                return marks
            return evac

        wait(PO, everything())
        sel_in = load(1, PO, sel[:, :, :], sel_d)
        wait(AC, everything())
        wait(VE, everything())
        set_free[0] = set_free[1] = everything()
        gemm(3, 6, 3, nq, HH[:, 10:16, :], HL[:, 10:16, :], evac_c(0, 3, nq), split_of(T_CQ, nq))
        flush()
        wait(AC, everything())
        wait(VE, everything())
        gemm(3, 4, 4, 512, HH[:, 10:14, :], HL[:, 10:14, :], evac_c(T_KN, 4, 512), split_of(T_CKV, 512))
        flush()
        wait(AC, everything())
        wait(PE, everything())
        wait(VE, everything())
        ahead(RING, CH)
        jobs = [(T_KN + h, "nope", 6 + h, 512) for h in range(6)] + [(T_KPE, "kpe", 0, 512)]
        jobs += [(T_QN + h, "nope", h, nq) for h in range(6)] + [(T_QR + t, "rope", t, nq) for t in range(3)]

        def lhs2(kind, t):
            a = CONST[kind][0]
            if kind == "nope":
                return const[:, a + 11 - t:a + 23 - t]
            if kind == "rope":
                return const[:, a + 10 - 2 * t:a + 22 - 2 * t]
            return const[:, a:a + 12]

        done = fan_in(jobs, 12, lhs2, 7)
        rr, _ = root(PS[0:12, 7, :], TMP[0:12, 4, :], [done], 512)
        wait(VE, rr)
        kp = dve(VE.tensor_scalar(T[:, T_KPE, :], T[:, T_KPE, :], Pm("kn_r", l), None, ALU.mult))
        wait(PE, rr, sel_in)
        free = [None] * 4
        n = 0
        marks = {T_KPE: kp}
        for h in range(6):
            for tile, r, w_, cols in ((T_QN + h, h, wq8[:, 4 * l + 2:4 * l + 3], nq),
                                      (T_KN + h, 6 + h, Pm("kn_n", l), 512)):
                spread(n, tile, const[0:12, r:r + 1].to_broadcast([12, P]), TMP[0:12, 4, :], w_, cols, free)
                n += 1
        for t in range(3):
            marks[T_QR + t] = spread(n, T_QR + t, sel[0:12, t, :], TMP[0:12, 4, :], wq8[:, 4 * l + 3:4 * l + 4],
                                     nq, free)
            n += 1
        wait(PE, free)
        wait(VE, done)
        roped = rope([T_KPE] + [T_QR + t for t in range(3)], marks)
        wait(PE, everything())
        wait(VE, roped[T_KPE])
        free = [None] * 4
        for t in range(3):
            b = t
            m = pe(PE.matmul(PS[:, b, :], sel[0:12, 3 + t, :], TMP[0:12, 4, :], start=True, stop=True))
            wait(VE, m)
            dve(VE.tensor_tensor(T[:, T_KR + t, :], T[:, T_KPE, :], PS[:, b, :], ALU.mult))
        turn_values(T_VC, 6, everything())
        for e in (PE, VE, AC, PO):
            wait(e, everything())
        for h_ in range(6):
            qr = act(AC.activation(T[:, T_COPY_C[h_], 0:nq], T[:, T_QR + h_ // 2, 0:nq], ACT.Copy,
                                   scale=C("halves")[:, h_ % 2:h_ % 2 + 1]))
        wait(PE, qr)
        vcf = T[:, T_VC:T_VC + 6, :].rearrange("p a b -> p (a b)")
        if not last:
            step_c = ada_beside(ADA_FIRST + 10, HF[0:4, 15, :])

            def side(u, split):
                for part in range(2):
                    if split:
                        ahead(1, CH, part == 0)
                    else:
                        step_c()
        for h_ in range(6):
            def terms(h, qt, h_=h_):
                q = slice(P * qt, P * qt + P)
                k = slice(256, 512) if qt >= 2 else slice(0, 512)
                n = 256 if qt >= 2 else 512
                return [(T[:, T_QN + h_, q], T[:, T_KN + h_, k], 0, n),
                        (T[:, T_COPY_C[h_], q], T[:, T_KR + h_ // 2, k], 0, n)]

            def v_of(h, kt, h_=h_):
                c = 768 * kt + P * h_
                return vcf[:, c:c + P]

            zb = 6 + h_ % 2
            y_tile(side, 1, terms, v_of, lambda h: slice(0, P), 10 + h_, None, zb, PT_C)
        drain()
        if not last:
            wait(AC, everything())
            ada_row[0] = arow
            ada_flush()

        wait(PO, everything())
        if l == 0:
            xo = [load(5, PO, T[:, 16:32, :], xT)]
        else:
            xo = [load(5, PO, T[:, 16:32, :], x_d)]
            meta_in = load(6, PO, RES[:, :, 0:META], metaT)
        set_free[0] = set_free[1] = everything()
        for e in (AC, VE, PO):
            wait(e, everything())
        x_new = []
        sq = {"free": [None, None], "acc": None, "n": 0}

        def out_evac(g, bank0, done):
            marks = []
            wait(VE, done, xo)
            for m in range(4):
                k = 4 * g + m
                for s in range(streams):
                    c = slice(256 * s, 256 * s + 256)
                    dst = RES[:, k, META:] if last else T[:, k, c]
                    v = dve(VE.scalar_tensor_tensor(dst, PS[:, bank0 + m, c],
                                                    ada[:, A0 + 2 * DT + k, s:s + 1], T[:, 16 + k, c],
                                                    ALU.mult, ALU.add))
                marks.append(v)
                x_new.append(v)
                if last:
                    wait(AC, meta_in)
                    square_add(RES[:, k, :], N2, v, k == 0, sq, [T[:, 2, :], T[:, 3, :]], T[:, 0, :])
                else:
                    square_add(T[:, k, :], 512, v, k == 0, sq)
                if m < 3:
                    yield
            return marks

        gemm(4, DT, 4, nq, HH, HL, out_evac, [state["y"]] * DT)
        ahead(RING, CH)
        flush()
        if last:
            ring["meta"] = meta_in
            ring["acc"] = sq["acc"]
            return x_new
        wait(PO, *x_new)
        ring["x_stored"] = store(4, PO, x_d, T[:, 0:16, :])
        wait(PO, ring["x_stored"])
        ring["acc"] = sq["acc"]
        ring["y_free"] = Mark(pe_n, pe_n.v)
        return x_new

    def square_add(src, n, ready, first, sq, bufs=None, acc=None):
        bufs = bufs or [TMP[:, 8, :], TMP[:, 9, :]]
        acc = acc if acc is not None else TMP[:, 5, :]
        if first:
            wait(AC, ready, sq.get("start"))
            a = act(AC.activation(acc[:, 0:n], src, ACT.Square))
            sq["acc"] = a
            return
        i = sq["n"] % 2
        sq["n"] += 1
        wait(AC, ready, sq["free"][i])
        a = act(AC.activation(bufs[i][:, 0:n], src, ACT.Square))
        wait(PO, a, sq["acc"])
        sq["acc"] = sq["free"][i] = pool(PO.tensor_tensor(acc[:, 0:n], acc[:, 0:n], bufs[i][:, 0:n], ALU.add))

    x_in = load(7, PO, T[:, 0:16, :], xT)
    squares = {"free": [None, None], "acc": None, "n": 0}
    squared = []

    def first_squares():
        for k in range(len(squared), min(len(squared) + 2, DT)):
            square_add(T[:, k, :], 512, x_in, k == 0, squares)
            squared.append(k)

    pr.repeat(ADA_FIRST // 2, ada_turn)
    ring["acc"] = squares["acc"]
    ada_pend[:] = [(ADA_FIRST - 1, 1, ada_pend[0][2])]
    ahead(RING, CH)
    ada_flush()
    set_free[1] = [*ada_free]
    new = layer(0, lambda k: T[:, k, :], [x_in] * DT)
    new = layer(1, lambda k: T[:, k, :], new)
    second(pr, locals(), new)
    return pr


def second(pr, env, x_new):
    nc = pr.nc
    wait = pr.wait
    SP, AC, VE, PO, PE = nc.sync, nc.scalar, nc.vector, nc.gpsimd, nc.tensor
    (act, dve, pool, pe, gemm, flush, C, Pm, PS, RES, NH, NL, PH, PL, CHI, CLO, YA, G4, FH, FL, T2, T3, T4, CV,
     set_free, square_add, ring, param, act_n, dve_n, pe_n, pool_n, store, out_d, root, T) = (
        env[k] for k in ("act dve pool pe gemm flush C Pm PS RES NH NL PH PL CHI CLO YA G4 FH FL T2 T3 T4 CV "
                         "set_free square_add ring param act_n dve_n pe_n pool_n store out_d root T").split())
    N = N2
    everything = lambda: [Mark(x, x.v) for x in (act_n, dve_n, pe_n, pool_n)]
    norm_tmp = [T2[:, j, 0:N] for j in range(4)]
    last_tmp = [T4[:, j, :] for j in range(4)]

    def sync_all():
        for e in (AC, VE, PO, PE):
            wait(e, everything())

    def norm(acc, wname, hi, lo, hi_free=None, out=None, tmp=norm_tmp):
        ACC, RSTD = tmp[:2]
        wait(PE, acc, *set_free)
        msq = pe(PE.matmul(PS[:, 7, 0:N], C("mean").to_broadcast([P, P]), ACC, start=True, stop=True))
        rstd, rt = root(PS[:, 7, 0:N], RSTD, [msq], N)
        set_free[1] = [rt]
        wait(VE, rstd)
        free = [None, None]

        def make(k):
            i = k % 2
            if out is not None:
                return dve(VE.scalar_tensor_tensor(out[:, k, :], RES[:, k, :], Pm(wname, k), RSTD,
                                                   ALU.mult, ALU.mult))
            wait(VE, free[i])
            m = dve(VE.scalar_tensor_tensor(T2[:, 4 + i, 0:N], RES[:, k, :], Pm(wname, k), RSTD,
                                            ALU.mult, ALU.mult))
            wait(AC, m, hi_free)
            a = act(AC.activation(hi[:, k, :], T2[:, 4 + i, 0:N], ACT.Copy))
            wait(VE, a, hi_free)
            free[i] = dve(VE.tensor_tensor(lo[:, k, :], T2[:, 4 + i, 0:N], hi[:, k, :].bitcast(F32), ALU.subtract))
            made["last"] = free[i]
            return free[i]
        return make

    made = {}
    sync_all()
    wait(AC, ring["meta"])
    wait(VE, ring["meta"])
    hn = norm(ring["acc"], "norm_mix", NH, NL, tmp=[T[:, 0, 0:N]] + norm_tmp[1:])

    pooled = []
    uf = {"free": [[], []]}

    def u_evac(g, bank0, done):
        w = WINDOWS[g]
        free = []
        if g == 0:
            wait(VE, made["last"])
            for j in range(8):
                uf["zero"] = dve(VE.memset(T2[:, j, 0:16], 0.0))
        wait(AC, done, uf["zero"])
        for m in range(4):
            k = 4 * g + m
            base = 4 * (m % 2)
            wait(AC, uf["free"][m % 2])
            u = act(AC.activation(T2[:, base, 16:16 + N], PS[:, bank0 + m, 0:N], ACT.Copy))
            free = u
            src, step, prev = base, 1, u
            wait(VE, uf["free"][m % 2])
            while step < w:
                dst = base + 1 + (src - base) % 2
                wait(VE, prev)
                prev = dve(VE.tensor_tensor(T2[:, dst, 16:16 + N], T2[:, src, 16:16 + N],
                                            T2[:, src, 16 - step:16 + N - step], ALU.add))
                src, step = dst, step * 2
            wait(VE, prev)
            q = base + 3
            dve(VE.scalar_tensor_tensor(T2[:, q, 16 + w - 1:16 + N], T2[:, src, 16 + w - 1:16 + N], 1.0 / w,
                                        T2[:, base, 16 + w - 1:16 + N], ALU.mult, ALU.subtract))
            for t in range(w - 1):
                prev = dve(VE.scalar_tensor_tensor(T2[:, q, 16 + t:17 + t], T2[:, src, 16 + t:17 + t],
                                                   1.0 / (t + 1), T2[:, base, 16 + t:17 + t],
                                                   ALU.mult, ALU.subtract))
            wait(AC, prev)
            a = act(AC.activation(PH[:, k, :], T2[:, q, 16:16 + N], ACT.Copy))
            wait(VE, a, prev)
            v = dve(VE.tensor_tensor(PL[:, k, :], T2[:, q, 16:16 + N], PH[:, k, :].bitcast(F32), ALU.subtract))
            uf["free"][m % 2] = [v]
            pooled.append(v)
            if m < 3:
                yield
        return [free]

    gemm(4, DT, 4, N, NH, NL, u_evac, hn)

    for m in range(4):
        zero = dve(VE.memset(CV[:, m, 0:2], 0.0))
    cf = {"conv": None, "gc": [None] * 4, "cv": [None] * 4}
    conv_ready = []

    def gc_evac(g, bank0, done):
        wait(AC, done, zero, cf["conv"])
        out = []
        for m in range(4):
            a = act(AC.activation(CV[:, m, 2:2 + N], PS[:, bank0 + m, 0:N], ACT.Copy))
            cf["gc"][m] = a
        return [a]

    def v_evac(g, bank0, done):
        wait(VE, done, *cf["gc"])
        for m in range(4):
            v = dve(VE.tensor_tensor(CV[:, m, 2:2 + N], CV[:, m, 2:2 + N], PS[:, bank0 + m, 0:N], ALU.mult))
            cf["cv"][m] = v
        free = v
        return [free]

    def gb_evac(j):
        def evac(g, bank0, done):
            wait(VE, done, *cf["cv"])
            for m in range(4):
                k = 4 * j + m
                Y = T3[:, m % 2, 0:N]
                wait(VE, cf.get(("y", m % 2)))
                a = dve(VE.tensor_scalar(Y, CV[:, m, 0:N], Pm("conv_w", k), None, ALU.mult))
                for tap in (1, 2):
                    wait(VE, a)
                    a = dve(VE.scalar_tensor_tensor(Y, CV[:, m, tap:tap + N], Pm("conv_w", DT * tap + k), Y,
                                                    ALU.mult, ALU.add))
                wait(VE, a)
                a = dve(VE.tensor_tensor(Y, Y, PS[:, bank0 + m, 0:N], ALU.mult))
                free = a
                wait(AC, a)
                h = act(AC.activation(CHI[:, k, :], Y, ACT.Copy))
                wait(VE, h)
                v = dve(VE.tensor_tensor(CLO[:, k, :], Y, CHI[:, k, :].bitcast(F32), ALU.subtract))
                cf[("y", m % 2)] = v
                conv_ready.append(v)
                if m < 3:
                    yield
            cf["conv"] = free
            return [free]
        return evac

    def ya_evac(gp):
        def evac(g, bank0, done):
            wait(VE, done)
            for m in range(4):
                k = 4 * gp + m
                v = dve(VE.tensor_scalar(YA[:, k, :], PS[:, bank0 + m, 0:N], Pm("pool_scale", k), None, ALU.mult))
            return [v]
        return evac

    for j in range(4):
        gemm(1, DT, 4, N, NH, NL, gc_evac)
        if j == 0:
            for gp in range(4):
                gemm(1, 4, 4, N, PH[:, 4 * gp:4 * gp + 4, :], PL[:, 4 * gp:4 * gp + 4, :], ya_evac(gp),
                     pooled[4 * gp:4 * gp + 4])
        gemm(1, DT, 4, N, NH, NL, v_evac)
        gemm(1, DT, 4, N, NH, NL, gb_evac(j))

    gt = {"g": None, "y": None}
    mixed = []

    def ga_evac(j):
        def evac(g, bank0, done):
            wait(AC, done)
            for m in range(4):
                k = 4 * j + m
                i = 2 + m % 2
                wait(AC, cf.get(("s", m % 2)))
                a = act(AC.activation(T3[:, i, 0:N], PS[:, bank0 + m, 0:N], ACT.Sigmoid, bias=Pm("b_gate", k)))
                wait(VE, a)
                cf[("s", m % 2)] = dve(VE.tensor_tensor(YA[:, k, :], YA[:, k, :], T3[:, i, 0:N], ALU.mult))
                if m < 3:
                    yield
            gt["ya"] = cf[("s", 1)]
            return [a]
        return evac

    def gbr_evac(j):
        def evac(g, bank0, done):
            wait(AC, done, gt["g"])
            for m in range(4):
                a = act(AC.activation(G4[:, m, :], PS[:, bank0 + m, 0:N], ACT.Sigmoid,
                                      bias=Pm("b_gate", DT + 4 * j + m)))
            gt["gr"] = a
            return [a]
        return evac

    def mix_evac(j):
        def evac(g, bank0, done):
            wait(VE, done, gt["gr"], gt["ya"])
            for m in range(4):
                k = 4 * j + m
                Y = T3[:, m % 2, 0:N]
                wait(VE, cf.get(("y", m % 2)))
                a = dve(VE.tensor_tensor(Y, PS[:, bank0 + m, 0:N], G4[:, m, :], ALU.mult))
                free = a
                wait(VE, a)
                a = dve(VE.tensor_tensor(Y, Y, YA[:, k, :], ALU.add))
                wait(AC, a)
                h = act(AC.activation(PH[:, k, :], Y, ACT.Copy))
                wait(VE, h)
                v = dve(VE.tensor_tensor(PL[:, k, :], Y, PH[:, k, :].bitcast(F32), ALU.subtract))
                cf[("y", m % 2)] = v
                mixed.append(v)
                if m < 3:
                    yield
            gt["g"] = free
            return [free]
        return evac

    for j in range(4):
        gemm(1, DT, 4, N, NH, NL, ga_evac(j))
        gemm(1, DT, 4, N, NH, NL, gbr_evac(j))
        gemm(1, DT, 4, N, CHI, CLO, mix_evac(j), conv_ready)

    def add_evac(sq, tmp):
        def evac(g, bank0, done):
            wait(VE, done)
            for m in range(4):
                k = 4 * g + m
                v = dve(VE.tensor_tensor(RES[:, k, :], RES[:, k, :], PS[:, bank0 + m, 0:N], ALU.add))
                square_add(RES[:, k, :], N, v, k == 0, sq, tmp[2:], tmp[0])
                if m < 3:
                    yield
            return [v]
        return evac

    sq = {"free": [None, None], "acc": None, "n": 0, "start": Mark(pe_n, pe_n.v)}
    gemm(4, DT, 4, N, PH, PL, add_evac(sq, norm_tmp), mixed)
    flush()
    hn = norm(sq["acc"], "norm_ffn", NH, NL, Mark(pe_n, pe_n.v))

    ff = {"s": [None] * 2, "y": [None] * 2, "last": None}

    def ffn_evac(g, bank0, done):
        wait(AC, done, made["last"])
        wait(VE, done)
        for m in range(2):
            wait(AC, ff["s"][m])
            a = act(AC.activation(T3[:, 2 + m, 0:N], PS[:, bank0 + m, 0:N], ACT.Silu))
            wait(VE, a, ff["y"][m])
            Y = T3[:, m, 0:N]
            v = dve(VE.tensor_tensor(Y, T3[:, 2 + m, 0:N], PS[:, bank0 + 2 + m, 0:N], ALU.mult))
            ff["s"][m] = v
            free = v
            wait(AC, v)
            h = act(AC.activation(FH[:, 2 * g + m, :], Y, ACT.Copy))
            wait(VE, h)
            ff["y"][m] = dve(VE.tensor_tensor(FL[:, 2 * g + m, :], Y, FH[:, 2 * g + m, :].bitcast(F32),
                                              ALU.subtract))
            if m < 1:
                yield
        return [a, free]

    gemm(FT // 2, DT, 4, N, NH, NL, ffn_evac, hn)
    before = Mark(dve_n, dve_n.v)
    sq = {"free": [None, None], "acc": None, "n": 0, "start": Mark(pe_n, pe_n.v)}
    gemm(4, FT, 4, N, FH, FL, add_evac(sq, last_tmp), lambda k: before if k < FT - 2 else ff["y"][1])
    flush()
    final = norm(sq["acc"], "norm_final", None, None, out=RES, tmp=last_tmp)
    for k in range(DT):
        final(k)
    wait(SP, *everything())
    o = store(5, SP, out_d, RES[:, :, META:])
    wait(SP, o)
    for e in (AC, VE, PO, PE):
        wait(e, o)


def constants():
    c = np.zeros((P, NCONST), np.float32)

    def put(name, v):
        a, b = CONST[name]
        c[:v.shape[0], a:b] = v

    i = np.arange(P)
    put("ident", np.eye(P, dtype=np.float32))
    rev = np.zeros((P, P), np.float32)
    rev[i, (i // 64) * 64 + 63 - i % 64] = 1
    put("rev", rev)
    rot = np.zeros((P, P), np.float32)
    for m in range(P):
        b = m % 64 // 16
        rot[m + 16 if b % 2 == 0 else m - 16, m] = -1 if b % 2 == 0 else 1
    put("rot", rot)
    t = np.arange(L)
    nf = ROPE // 4
    inv = np.float32(10000.0) ** (-np.arange(nf, dtype=np.float32) / np.float32(nf))
    ar = (t // GRID_W).astype(np.float32)[:, None] * inv
    ac = (t % GRID_W).astype(np.float32)[:, None] * inv
    ang = np.concatenate([ar, ar, ac, ac], axis=-1).T
    put("cos", np.tile(np.cos(ang), (2, 1)).astype(np.float32))
    put("sin", np.tile(np.sin(ang), (2, 1)).astype(np.float32))
    q = np.arange(L)
    band = np.where(np.abs(q[:, None] - q[None, :]) <= SW, 0.0, NEG).astype(np.float32)
    put("band", np.concatenate([band[:P, P:], band[P:, :P]], axis=1))
    qc = 63 - i % 64
    start = np.clip(qc - NA_COLS // 2, 0, GRID_W - NA_COLS)[:, None]
    kc = np.arange(GRID_W)[None, :]
    ok = (kc >= start) & (kc < start + NA_COLS)
    put("cols", np.where(ok, 0.0, NEG).astype(np.float32))
    halves = np.zeros((P, 2), np.float32)
    halves[:64, 0] = halves[64:, 1] = 1
    put("halves", halves)
    v = np.zeros((P, 66), np.float32)
    v[:, 32:34] = halves / HD
    put("pair", v)
    v = np.zeros((P, 34), np.float32)
    v[:, 32] = 1 / Q_LORA
    put("cq", v)
    v = np.zeros((P, 34), np.float32)
    v[:, 33] = 1 / KV_LORA
    put("ckv", v)
    v = np.zeros((P, 23), np.float32)
    v[:, 11] = 1 / QK_C
    put("nope", v)
    v = np.zeros((P, 22), np.float32)
    v[:, 10:12] = halves / QK_C
    put("rope", v)
    v = np.zeros((P, 12), np.float32)
    v[:, 6:] = 1 / (2 * QK_C)
    put("kpe", v)
    put("mean", np.full((P, 1), 1 / D, np.float32))
    put("sum4", np.tile(np.eye(2, dtype=np.float32), (2, 1)))
    put("eps", np.full((P, 1), EPS, np.float32))
    sel = np.zeros((32, 16, P), np.float32)
    for t in range(16):
        sel[2 * t, t, :64] = sel[2 * t + 1, t, 64:] = 1
    return c, sel


def pack(inputs):
    f = {k: np.asarray(v) for k, v in inputs.items()}
    entries = host_chunks()
    stream = np.zeros((len(entries), P, CH), np.float32)
    y_rows = list(range(512)) + [512 + h * HD + d for h in B_ORDER for d in range(HD)] + list(range(1280, 2048))
    w_out = f["w_out"][:, y_rows, :]
    for n, (name, layer, k0, nk, cols) in enumerate(entries):
        w = w_out if name == "w_out" else f[name]
        if layer is not None:
            w = w[layer]
        blk = w[k0 * P:(k0 + nk) * P].reshape(nk, P, -1)
        width = sum(b - a for a, b in cols)
        dst = stream[n, :, :nk * width].reshape(P, nk, width)
        at = 0
        for a, b in cols:
            dst[:, :, at:at + b - a] = blk[:, :, a:b].transpose(1, 0, 2)
            at += b - a
    par = np.zeros((P, NPARAM), np.float32)

    def put(name, v):
        a, b = PARAM[name]
        par[:, a:b] = v

    def cols(v):
        return v.reshape(-1, P).T

    put("b_ada", cols(f["b_ada"]))
    put("norm_w", cols(f["norm_w"]))
    for n in ("qn_a", "kn_a", "qn_b", "kn_b"):
        put(n, np.tile(f[n].T, (2, 1)))
    put("qa_norm", cols(f["qa_norm"]))
    put("kva_norm", cols(f["kva_norm"]))
    for n in ("qn", "kn"):
        put(n + "_n", f[n + "_c"][:, :NOPE].T)
        put(n + "_r", np.tile(f[n + "_c"][:, NOPE:].T, (2, 1)))
    put("sink", np.broadcast_to(f["sink_b"][:, B_ORDER].reshape(1, -1), (P, 2 * H_B)))
    cond = np.stack([f["c"][0], f["c_ctx"]], axis=-1).reshape(DT, P, 2)
    put("cond", cond.transpose(1, 0, 2).reshape(P, -1))
    put("norm_mix", cols(f["norm_mix_g_2"]))
    put("b_gate", cols(f["b_gate_2"]))
    put("pool_scale", cols(f["pool_scale_2"]))
    put("conv_w", cols(f["conv_w_2"]))
    put("norm_ffn", cols(f["norm_ffn_g_2"]))
    put("norm_final", cols(f["norm_final_g_2"]))

    def tokens(x):
        return np.ascontiguousarray(x.T.reshape(DT, P, -1).transpose(1, 0, 2))

    xT = tokens(np.concatenate([f["x"][0], f["ctx"][0]], axis=0))
    metaT = tokens(f["meta_tokens_2"])
    rpb = np.zeros((DEPTH, H_A, 2 * NA_ROWS - 1, 2 * GRID_W - 1), np.float32)
    rpb[..., GRID_W - NA_COLS:GRID_W + NA_COLS - 1] = f["rpb_a"]
    const, sel = constants()
    rpb = np.ascontiguousarray(rpb.transpose(0, 2, 1, 3))
    return {"stream": stream, "xT": xT, "metaT": metaT, "const": const, "param": par, "sel": sel, "rpb": rpb}


def program(nc, arrays):
    a = {n: nc.dram_tensor(f"in_{n}", v.shape, F32, kind="ExternalInput").ap() for n, v in arrays.items()}
    z_d = nc.dram_tensor("z_scratch", (DT, P, 512), F32, kind="Internal").ap()
    x_d = nc.dram_tensor("x_scratch", (P, DT, 512), F32, kind="Internal").ap()
    out = nc.dram_tensor("out", (P, DT, L), F32, kind="ExternalOutput").ap()
    build(nc, a["stream"], a["xT"], a["metaT"], a["const"], a["param"], a["sel"], a["rpb"], z_d, x_d, out)


def kernel(**inputs):
    import concourse.bacc as bacc
    from concourse.bass_utils import run_bass_kernel_spmd

    nc = bacc.Bacc("TRN2", target_bir_lowering=False, num_devices=1)
    arrays = pack(inputs)
    program(nc, arrays)
    r = run_bass_kernel_spmd(nc, [{f"in_{n}": v for n, v in arrays.items()}], core_ids=[0])
    out = r.results[0]["out"]
    return np.ascontiguousarray(out.transpose(1, 0, 2).reshape(D, L).T).reshape(1, L, D)
```

```python
import concourse.bass as bass
import numpy as np
from concourse import mybir

F32 = mybir.dt.float32
F32R = mybir.dt.float32r
ALU = mybir.AluOpType
ACT = mybir.ActivationFunctionType
AXX = mybir.AxisListType.X

P = 128
D = 2048
DT = D // P
L = 256
LC = 256
DEPTH = 2
HD = 64
H_A, H_B, HKV_B, H_C = 8, 12, 4, 6
NOPE, ROPE, V_C = 128, 64, 128
QK_C = NOPE + ROPE
Q_LORA, KV_LORA = 768, 512
GRID_W, NA_COLS, NA_ROWS = 64, 16, 8
SW = 128
META = 16
N2 = META + L
FFN = 5632
FT = FFN // P
WINDOWS = (2, 4, 8, 16)
EPS = 1e-6
NEG = -1e30

ADA_FIRST = 8
CH = 1024
RING = 4

T_QA, T_QB, T_CQ, T_KA, T_VA, T_KB, T_VB, T_CKV, T_KPE = 0, 4, 10, 16, 20, 24, 26, 28, 32
NT = 33
T_QN, T_QR, T_KR, T_KN, T_VC = 0, 6, 10, 16, 22
T_COPY_C = (13, 14, 15, 28, 29, 30)
B_ORDER = [h for g in (0, 6) for a in range(g, g + 3) for h in (a, a + 3)]


def table(fields):
    at, out = 0, {}
    for name, n in fields:
        out[name] = (at, at + n)
        at += n
    return out, at


CONST, NCONST = table([
    ("ident", P), ("rev", P), ("rot", P), ("cos", L), ("sin", L), ("band", 2 * P), ("cols", GRID_W),
    ("pair", 66), ("cq", 34), ("ckv", 34), ("nope", 23), ("rope", 22), ("kpe", 12), ("mean", 1), ("halves", 2), ("sum4", 2), ("eps", 1)])
PARAM, NPARAM = table([
    ("b_ada", 2 * 48), ("norm_w", 2 * DT), ("qn_a", 2), ("kn_a", 2), ("qn_b", 2), ("kn_b", 2),
    ("qa_norm", 2 * 6), ("kva_norm", 2 * 4), ("qn_n", 2), ("qn_r", 2), ("kn_n", 2), ("kn_r", 2),
    ("sink", 2 * H_B), ("cond", 2 * DT), ("norm_mix", DT), ("b_gate", 2 * DT),
    ("pool_scale", DT), ("conv_w", 3 * DT), ("norm_ffn", DT), ("norm_final", DT)])


class Mark:
    __slots__ = ("of", "v")

    def __init__(self, of, v):
        self.of, self.v = of, v


class Count:

    def __init__(self, prog, handle=None, step=1):
        self.prog, self.handle, self.step, self.v = prog, handle, step, 0
        prog.counts.append(self)

    def inc(self, ins):
        ins.then_inc(self.handle, self.step)
        self.v += self.step
        m = Mark(self, self.v)
        self.prog.marks.append(m)
        return m


class Prog:

    def __init__(self, nc):
        self.nc, self.counts, self.marks = nc, [], []
        self.turn = None
        self.start, self.stride = {}, {}
        self.body = 0
        self.nsem = 0

    def sem(self, name, step=1):
        self.nsem += 1
        return Count(self, self.nc.alloc_semaphore(name), step)

    def value(self, of, v):
        if self.turn is None or v <= self.start[of] or not self.stride[of]:
            return v
        return v + (self.turn - 2) * self.stride[of]

    def wait(self, eng, *marks):
        best = {}
        for m in marks:
            if m is None:
                continue
            if isinstance(m, (list, tuple)):
                for x in m:
                    if x is not None and (x.of not in best or best[x.of] < x.v):
                        best[x.of] = x.v
            elif m.of not in best or best[m.of] < m.v:
                best[m.of] = m.v
        for of, v in best.items():
            eng.wait_ge(of.handle, self.value(of, v))

    def repeat(self, n, body):
        if n <= 3:
            for i in range(n):
                body(i)
            return
        assert self.turn is None
        body(0)
        start = {c: c.v for c in self.counts}
        body(1)
        after = {c: c.v for c in self.counts}
        self.marks = []
        with self.nc.Fori(2, n) as turn:
            self.turn, self.start = turn, start
            self.stride = {c: after[c] - start[c] for c in self.counts}
            self.body = 1
            body(turn)
        self.turn, self.body = None, 0
        for c in self.counts:
            assert c.v - after[c] == self.stride[c]
            c.v += (n - 3) * self.stride[c]
        for m in self.marks:
            m.v += (n - 3) * self.stride[m.of]
        self.marks = []


def host_chunks():
    out = []

    def stage(name, layer, kt, groups, mt):
        kpc = CH // (mt * P)
        for cols in groups:
            for k0 in range(0, kt, kpc):
                out.append((name, layer, k0, min(kpc, kt - k0), cols))

    def span(a, n):
        return [[(a + i, a + i + 512)] for i in range(0, n, 512)]

    for l in range(DEPTH):
        stage("w_ada", l, DT, span(0, 3 * D), 4)
    conditioning = out[ADA_FIRST * 8:]
    del out[ADA_FIRST * 8:]

    def conditioned(groups):
        out.extend(conditioning[:8 * groups])
        del conditioning[:8 * groups]

    qa, ka, va = 0, 512, 1024
    qb, kb, vb = 1536, 2304, 2560
    cq, ckv, kpe, z = 2816, 3584, 4096, 4160
    qb_cols = [(qb + h * HD, qb + h * HD + HD) for h in B_ORDER]
    z_cols = [(z, z + 512)] + [(z + 512 + h * HD, z + 512 + h * HD + HD) for h in B_ORDER] + [
        (z + 1280, z + 2048)]

    def grouped(cols):
        flat = [c for a, b in cols for c in range(a, b, HD)]
        return [[(c, c + HD) for c in flat[i:i + 8]] for i in range(0, len(flat), 8)]

    for l in range(DEPTH):
        stage("w_in", l, DT, grouped(z_cols), 4)
        stage("w_in", l, DT, grouped([(qa, qa + 512)] + qb_cols + [(cq, cq + 768)]), 4)
        stage("w_in", l, DT, grouped([(ka, ka + 512), (va, va + 512), (kb, kb + 256),
                                      (vb, vb + 256), (ckv, ckv + 512)]), 4)
        stage("w_in", l, DT, [[(kpe, kpe + HD)] * 2], 1)
        if l == 0:
            conditioned(10)
        c = [(h * QK_C, h * QK_C + NOPE) for h in range(H_C)]
        c += [(h * QK_C + NOPE, (h + 1) * QK_C) for h in range(H_C)]
        flat = [x for a, b in c for x in range(a, b, HD)]
        stage("w_qb", l, 6, [[(x, x + HD) for x in flat[i:i + 6]] for i in range(0, 18, 6)], 3)
        c = [(h * 256, h * 256 + NOPE) for h in range(H_C)]
        c += [(h * 256 + NOPE, h * 256 + 256) for h in range(H_C)]
        stage("w_kvb", l, 4, [c[i:i + 4] for i in range(0, 12, 4)], 4)
        if l == 0:
            conditioned(6)
            assert not conditioning
        stage("w_out", l, DT, span(0, D), 4)
    stage("w_in_2", None, DT, span(0, D), 4)
    for j in range(4):
        for part in (2, 3, 1):
            stage("w_in_2", None, DT, span(part * D + j * 512, 512), 4)
            if (j, part) == (0, 2):
                for g in range(4):
                    stage("pool_w_2", g, 4, span(0, 512), 4)
    for j in range(4):
        for part in (4, 5):
            stage("w_in_2", None, DT, span(part * D + j * 512, 512), 4)
        stage("conv_out_w_2", None, DT, span(j * 512, 512), 4)
    stage("w_o_2", None, DT, span(0, D), 4)
    stage("w_gate_up_2", None, DT,
          [[(g * 256, g * 256 + 256), (FFN + g * 256, FFN + g * 256 + 256)] for g in range(FT // 2)], 4)
    stage("w_down_2", None, FT, span(0, D), 4)
    return out


def build(nc, stream, xT, metaT, const_d, param_d, sel_d, rpb_d, z_d, x_d, out_d, dbg=None):
    pr = Prog(nc)
    wait, value = pr.wait, pr.value
    SP, AC, VE, PO, PE = nc.sync, nc.scalar, nc.vector, nc.gpsimd, nc.tensor

    act_n, dve_n, pool_n, pe_n = (pr.sem(n) for n in ("act_n", "dve_n", "pool_n", "pe_n"))
    raw_n = [pr.sem(f"raw_n{i}", 16) for i in range(RING)]
    load_n = [pr.sem(f"load_n{i}", 16) for i in range(11)]
    store_n = [pr.sem(f"store_n{i}", 16) for i in range(7)]
    chunk = Count(pr)

    def act(ins):
        return act_n.inc(ins)

    def dve(ins):
        return dve_n.inc(ins)

    def pool(ins):
        return pool_n.inc(ins)

    def pe(ins):
        return pe_n.inc(ins)

    base = (nc.sbuf_base + 63) // 64 * 64
    place = [base]

    def region(nbytes):
        at = place[0]
        place[0] += (nbytes + 31) // 32 * 32
        return at

    def sb(name, shape, dt, at):
        n = 4 * int(np.prod(shape[1:]))
        assert at + n <= nc.sbuf_usable_end, (name, at + n)
        return nc.alloc_sbuf_tensor_at("sb_" + name, list(shape), dt, offset=at)

    def own(name, shape, dt=F32):
        return sb(name, shape, dt, region(4 * int(np.prod(shape[1:]))))

    const = own("const", [P, NCONST])
    param = own("param", [P, NPARAM])
    ada = own("ada", [P, 2 * 48, 2])
    amul = own("amul", [P, DT, 2])
    cond = own("cond", [P, DT, 2])
    cond4 = own("cond4", [P, DT, 4], F32R)
    wq8 = own("wq8", [P, 8])
    nsink = own("nsink", [P, H_B])
    stat = own("stat", [P, 4, 4])
    raw = own("raw", [P, RING, CH])
    whi = own("whi", [P, RING, CH], F32R)
    wlo = own("wlo", [P, RING, CH], F32R)
    block = region(153600)
    HB = 16 * 512 * 4
    HH = sb("hi", [P, DT, 512], F32R, block)
    HL = sb("lo", [P, DT, 512], F32R, block + HB)
    T = sb("T", [P, NT, 512], F32, block + 2 * HB)
    tmp_at = block + 2 * HB + NT * 2048
    TMP = sb("tmp", [P, 10, 512], F32, tmp_at)
    arow = sb("arow", [4, 512], F32, tmp_at)
    sel = sb("sel", [32, 16, P], F32, tmp_at)
    bias = [sb(f"bias{t}", [P, 4 * H_A, GRID_W], F32, block + t * HB + 10 * 2048) for t in range(2)]
    TR = sb("T_r", [P, NT, 512], F32R, block + 2 * HB)
    q_up = sb("q_up", [P, 2, 512], F32, block + 14 * 2048)
    pt_up = sb("pt_up", [P, 4, 256], F32, block + HB + 14 * 2048)
    HF = sb("hi_f32", [P, DT, 512], F32, block)
    LF = sb("lo_f32", [P, DT, 512], F32, block + HB)
    NB = DT * N2 * 4
    PH = sb("pooled_hi", [P, DT, N2], F32R, block)
    PL = sb("pooled_lo", [P, DT, N2], F32R, block + NB)
    CHI = sb("conv_hi", [P, DT, N2], F32R, block + 2 * NB)
    CLO = sb("conv_lo", [P, DT, N2], F32R, block + 3 * NB)
    YA = sb("ya", [P, DT, N2], F32, block + 4 * NB)
    G4 = sb("g4", [P, 4, N2], F32, block + 5 * NB)
    FH = sb("ffn_hi", [P, FT, N2], F32R, block)
    FL = sb("ffn_lo", [P, FT, N2], F32R, block + FT * N2 * 4)
    hn_at = block + 2 * FT * N2 * 4
    NH = sb("hn_hi", [P, DT, N2], F32R, hn_at)
    NL = sb("hn_lo", [P, DT, N2], F32R, hn_at + NB)
    t3_at = hn_at + 2 * NB
    res_at = block + 153600 - NB
    assert t3_at + 4 * N2 * 4 <= res_at and block + 5 * NB + 4 * (N2 + 2) * 4 <= hn_at
    RES = sb("res", [P, DT, N2], F32, res_at)
    T2 = sb("tmp2", [P, 8, N2 + 16], F32, block + 3 * NB)
    T3 = sb("tmp3", [P, 4, N2], F32, t3_at)
    T4 = sb("tmp4", [P, 4, N2], F32, hn_at)
    CV = sb("cv", [P, 4, N2 + 2], F32, block + 5 * NB)
    PS = nc.alloc_psum_tensor("ps", [P, 8, 512], F32)

    def C(name, rows=P):
        a, b = CONST[name]
        return const[0:rows, a:b]

    def Pm(name, i, n=1):
        a = PARAM[name][0] + i
        return param[:, a:a + n]

    ident = C("ident")

    def load(q, eng, out, in_):
        return load_n[q].inc(eng.dma_start(out, in_))

    def store(q, eng, out, in_):
        return store_n[q].inc(eng.dma_start(out, in_))

    param_in = load(10, SP, param[:, :], param_d)
    const_in = load(0, PO, const[:, :], const_d)

    raw_free = [None] * RING
    hl_free = [None] * RING
    st = {"pos": 0, "set": 0, "ahead": []}

    def next_weights(width, by_pool=False):
        s = st["pos"] % RING
        st["pos"] += 1
        wait(SP, raw_free[s])
        landed = raw_n[s].inc(SP.dma_start(raw[:, s, 0:width], stream[value(chunk, chunk.v)][:, 0:width]))
        chunk.v += 1
        wait(AC, landed, hl_free[s])
        rounded = act(AC.activation(whi[:, s, 0:width], raw[:, s, 0:width], ACT.Copy))
        lo_by, count = (PO, pool) if by_pool else (VE, dve)
        wait(lo_by, rounded, landed, hl_free[s])
        split = count(lo_by.tensor_tensor(wlo[:, s, 0:width], raw[:, s, 0:width],
                                          whi[:, s, 0:width].bitcast(F32), ALU.subtract))
        raw_free[s] = split
        return s, split

    set_free = [[], []]
    pend = []

    def step_evac():
        if pend:
            fn, g, bank0, done = pend[0]
            rest = st.pop("rest", None) or fn(g, bank0, done)
            if not isinstance(rest, list):
                try:
                    next(rest)
                    st["rest"] = rest
                    return
                except StopIteration as end:
                    rest = end.value
            set_free[bank0 // 4] = rest
            pend.pop(0)

    def flush():
        while pend:
            step_evac()

    def next_set():
        st["set"] ^= 1
        return 4 * (st["set"] ^ 1)

    def ahead(n, width, by_pool=False):
        for _ in range(n):
            st["ahead"].append(next_weights(width, by_pool))

    def weights(width):
        return st["ahead"].pop(0) if st["ahead"] else next_weights(width)

    def gemm(groups, kt, mt, n, hi, lo, evac, ready=None):
        kpc = CH // (mt * P)
        nch = -(-kt // kpc)

        def one(g, first):
            bank0 = next_set()
            free = set_free[bank0 // 4]
            for c in range(nch):
                ks = list(range(c * kpc, min(kt, (c + 1) * kpc)))
                s, split = weights(len(ks) * mt * P)
                made = [ready(k) if callable(ready) else ready[k] for k in ks] if first and ready else []
                wait(PE, split)
                for j, k in enumerate(ks):
                    if made:
                        wait(PE, made[j])
                    for m in range(mt):
                        if k == 0 and (m == 0 or len(free) == 4):
                            wait(PE, free[m] if len(free) == 4 else free)
                        o = PS[:, bank0 + m, 0:n]
                        w0 = (j * mt + m) * P
                        wh, wl = whi[:, s, w0:w0 + P], wlo[:, s, w0:w0 + P]
                        PE.matmul(o, wh, hi[:, k, 0:n], start=(k == 0), stop=False)
                        PE.matmul(o, wh, lo[:, k, 0:n], start=False, stop=False)
                        mm = PE.matmul(o, wl, hi[:, k, 0:n], start=False, stop=(k == kt - 1))
                hl_free[s] = done = pe(mm)
                if c == nch - 1:
                    flush()
                elif c >= RING - 1:
                    step_evac()
            pend.append((evac, g, bank0, done))

        def turn(i):
            if pr.body:
                pend[:] = [(evac, 2 * (i - 1) + 1, pend[0][2], pend[0][3])]
            for u in range(2):
                one(2 * i + u, pr.body == 0 and i == 0 and u == 0)

        if groups % 2 == 0 and groups > 4:
            assert 2 * nch % RING == 0
            pr.repeat(groups // 2, turn)
            pend[:] = [(evac, groups - 1, pend[0][2], pend[0][3])]
        else:
            for g in range(groups):
                one(g, g == 0)

    wait(AC, param_in)
    wait(VE, param_in)
    wait(PE, const_in)
    a0 = PARAM["cond"][0]
    silu_c = act(AC.activation(cond[:, :, :].rearrange("p a b -> p (a b)"), param[:, a0:a0 + 2 * DT], ACT.Silu))
    wait(AC, silu_c)
    chi = act(AC.activation(cond4[:, :, 0:2], cond[:, :, :], ACT.Copy))
    wait(VE, chi)
    cond_ready = dve(VE.tensor_tensor(cond4[:, :, 2:4], cond[:, :, :], cond4[:, :, 0:2].bitcast(F32),
                                      ALU.subtract))
    s0 = PARAM["sink"][0]
    for l in range(DEPTH):
        for j, (name, scale) in enumerate((("qn_a", HD ** -0.5), ("qn_b", HD ** -0.5),
                                           ("qn_n", QK_C ** -0.5), ("qn_r", QK_C ** -0.5))):
            consts_ready = dve(VE.tensor_scalar(wq8[:, 4 * l + j:4 * l + j + 1], Pm(name, l), float(scale),
                                                None, ALU.mult))

    ada_last = {}
    ada_g = ada[:, :, :].rearrange("p (g m) s -> p g m s", m=4)
    b_ada_g = Pm("b_ada", 0, 2 * 48).rearrange("p (g m) -> p g m", m=4)

    ada_pend = []
    ada_free = [None, None]
    ada_row = [arow]

    def ada_flush(parts=(0, 1, 2)):
        if not ada_pend:
            return
        g, b, done = ada_pend[0]
        row = ada_row[0]
        if 0 in parts:
            wait(AC, done, ada_last.get("turned"))
            ada_last["row"] = act(AC.activation(row[:, :], PS[0:4, 6 + b, :], ACT.Copy))
        if 1 in parts:
            wait(PE, ada_last["row"], ada_last.get("added"))
            for m in range(4):
                mm = PE.matmul(PS[:, 6 + b, 2 * m:2 * m + 2], row[:, m * P:(m + 1) * P], C("sum4", 4),
                               start=True, stop=True)
            ada_last["turned"] = pe(mm)
        if 2 in parts:
            wait(VE, ada_last["turned"])
            for s in range(2):
                added = dve(VE.tensor_tensor(ada_g[:, g, :, s], PS[:, 6 + b, s:8:2], b_ada_g[:, g, :], ALU.add))
            ada_last["added"] = ada_free[b] = added
            ada_pend.pop(0)

    def ada_chunk(g, c, b):
        s, split = weights(CH)
        wait(PE, split, cond_ready)
        if c == 0:
            wait(PE, ada_free[b])
        for j in range(2):
            k = 2 * c + j
            o = PS[0:4, 6 + b, :]
            PE.matmul(o, cond4[:, k, :], whi[:, s, j * 512:(j + 1) * 512], start=(k == 0), stop=False)
            mm = PE.matmul(o, cond4[:, k, :], wlo[:, s, j * 512:(j + 1) * 512], start=False,
                           stop=(k == DT - 1))
        hl_free[s] = done = pe(mm)
        return done

    def ada_turn(i):
        if pr.body:
            ada_pend[:] = [(2 * (i - 1) + 1, 1, ada_pend[0][2])]
        for u in range(2):
            for c in range(8):
                done = ada_chunk(2 * i + u, c, u)
                if pr.body == 0 and i == 0 and (u or c >= 6):
                    first_squares()
                if c == RING - 1:
                    ada_flush()
            ada_pend.append((2 * i + u, u, done))

    def ada_beside(first, row):
        ada_row[0] = row
        at = [0]

        def step():
            g, c = divmod(at[0], 8)
            at[0] += 1
            done = ada_chunk(first + g, c, g % 2)
            if c in (2, 4, 6):
                ada_flush([c // 2 - 1])
            if c == 7:
                ada_pend.append((first + g, g % 2, done))
        return step

    ring = {}

    def slot(name, n):
        r = ring.setdefault(name, [0, [None] * n])
        i = r[0] % n
        r[0] += 1
        return i, r

    def root(src, dst, marks, n, mean_scale=1.0):
        wait(AC, *marks)
        rows = dst.shape[0]
        r = act(AC.activation(dst, src, ACT.Sqrt, bias=C("eps", rows), scale=mean_scale))
        wait(VE, r)
        return dve(VE.reciprocal(dst, dst)), r

    def layer(l, x_tiles, x_ready):
        last = l == DEPTH - 1
        nq = L if last else L + LC
        streams = 1 if last else 2
        A0 = 48 * l
        wait(VE, Mark(dve_n, dve_n.v), ring.get("amul_free"))
        for s in range(2):
            nw = param[:, PARAM["norm_w"][0] + DT * l:PARAM["norm_w"][0] + DT * (l + 1)]
            am = dve(VE.scalar_tensor_tensor(amul[:, :, s], ada[:, A0 + DT:A0 + 2 * DT, s], 1.0, nw,
                                             ALU.add, ALU.mult))
        wait(VE, am)
        wait(AC, am)
        rstd = rms_rows(ring["squares"], 512, TMP[:, 4, :])
        hs = {"free": [[None] * 2 for _ in range(2)], "last": None}
        wait(VE, rstd)

        def scaled(k):
            i = k % 2
            wait(VE, hs["free"][0][i], x_ready[k])
            for s in range(2):
                c = slice(256 * s, 256 * s + 256)
                m1 = dve(VE.scalar_tensor_tensor(TMP[:, 6 + i, c], x_tiles(k)[:, c], amul[:, k, s:s + 1],
                                                 TMP[:, 4, c], ALU.mult, ALU.mult))
            hs["scaled"] = ring["amul_free"] = m1

        def make_h(k):
            i = k % 2
            if k == 0:
                wait(AC, ring.get("y_free"))
                scaled(0)
            wait(AC, hs["scaled"], hs["free"][1][i])
            for s in range(2):
                c = slice(256 * s, 256 * s + 256)
                m2 = act(AC.activation(TMP[:, 8 + i, c], TMP[:, 6 + i, c], ACT.Identity,
                                       bias=ada[:, A0 + k, s:s + 1]))
            hs["free"][0][i] = m2
            wait(AC, m2)
            m3 = act(AC.activation(HH[:, k, :], TMP[:, 8 + i, :], ACT.Copy))
            if k + 1 < DT:
                scaled(k + 1)
            wait(VE, m3)
            m4 = dve(VE.tensor_tensor(HL[:, k, :], TMP[:, 8 + i, :], HH[:, k, :].bitcast(F32), ALU.subtract))
            hs["free"][1][i] = hs["last"] = m4
            return m4

        x_kept = ring.get("x_stored")

        zr = {"free": [None] * 4}

        def z_evac(g, bank0, done):
            wait(AC, done, hs["last"])
            out = []
            for m in range(4):
                wait(AC, zr["free"][m])
                out.append(act(AC.activation(TMP[:, 6 + m, 0:nq], PS[:, bank0 + m, 0:nq], ACT.Silu)))
                wait(PO, out[m])
                zr["free"][m] = store(m, PO, z_d[4 * g + m][:, 0:nq], TMP[:, 6 + m, 0:nq])
            return out

        def to_T(t0, n):
            def evac(g, bank0, done):
                wait(AC, done, x_kept)
                wait(VE, done, x_kept)
                out = []
                for m in range(4):
                    dst = T[:, t0 + 4 * g + m, 0:n]
                    if m % 2:
                        out.append(act(AC.activation(dst, PS[:, bank0 + m, 0:n], ACT.Copy)))
                    else:
                        out.append(dve(VE.tensor_copy(dst, PS[:, bank0 + m, 0:n])))
                return out
            return evac

        gemm(4, DT, 4, nq, HH, HL, z_evac, make_h)
        gemm(4, DT, 4, nq, HH, HL, to_T(T_QA, nq))
        gemm(4, DT, 4, 512, HH, HL, to_T(T_KA, 512))

        def kpe_evac(g, bank0, done):
            wait(AC, done)
            return [act(AC.activation(T[:, T_KPE, :], PS[:, bank0, :], ACT.Copy))]

        gemm(1, DT, 1, 512, HH, HL, kpe_evac)
        z_stored = list(zr["free"])
        ahead(3 if last else RING, 2 * 3 * P if last else CH)
        flush()
        proj = [set_free[0], set_free[1]]
        everything = lambda: [Mark(x, x.v) for x in (act_n, dve_n, pe_n, pool_n)]

        jobs = [(T_QA + t, "pair", t, nq) for t in range(4)]
        jobs += [(T_KA + t, "pair", 4 + t, 512) for t in range(4)]
        jobs += [(T_QB + t, "pair", 8 + t, nq) for t in range(6)]
        jobs += [(T_KB + t, "pair", 14 + t, 512) for t in range(2)]
        jobs += [(T_CQ + t, "cq", 0, nq) for t in range(6)]
        jobs += [(T_CKV + t, "ckv", 0, 512) for t in range(4)]
        jobs.sort(key=lambda j: -j[3])
        all_done = everything()
        wait(PO, all_done)
        sel_in = load(1, PO, sel[:, :, :], sel_d)
        wait(AC, all_done, z_stored)
        wait(PE, all_done)
        wait(VE, all_done)
        def turn_values(t0, nf, marks, b0):
            wait(PE, marks)
            for t in range(4):
                for f in range(nf):
                    at = (t * nf + f) * P
                    mm = PE.transpose(PS[:, b0 + at // 512, at % 512:at % 512 + P],
                                      T[:, t0 + f, t * P:(t + 1) * P], ident)
            m = pe(mm)
            wait(AC, m)
            return [act(AC.activation(T[:, t0 + b, :], PS[:, b0 + b, :], ACT.Copy)) for b in range(nf)]

        wait(SP, everything())
        pad = 2 * GRID_W - 1
        for t in range(2):
            for half in range(2):
                off = (l * (2 * NA_ROWS - 1) + NA_ROWS - 1 - (2 * t + half)) * H_A * pad
                src = bass.AP(rpb_d.tensor, off, [[1, 64], [pad, 4 * H_A], [1, 64]])
                load(2 + t, SP, bias[t][64 * half:64 * half + 64, :, :], src)
        masked = []
        for t in range(2):
            wait(PO, Mark(load_n[2 + t], load_n[2 + t].v))
            masked.append(pool(PO.tensor_tensor(bias[t][:, :, :], bias[t][:, :, :],
                                                C("cols").unsqueeze(1).to_broadcast([P, 4 * H_A, 64]), ALU.add)))


        def fan_in(jobs, rows, lhs, nb):
            free = [None] * 3
            for n, (tile, kind, t, cols) in enumerate(jobs):
                i = n % 3
                wait(AC, free[i])
                a = act(AC.activation(TMP[:, 5 + i, 0:cols], T[:, tile, 0:cols], ACT.Square))
                wait(PE, a)
                free[i] = pe(PE.matmul(PS[0:rows, nb, 0:cols], lhs(kind, t), TMP[:, 5 + i, 0:cols],
                                       start=(n == 0), stop=(n == len(jobs) - 1)))
            return free[i]

        def lhs1(kind, t):
            a = CONST[kind][0]
            if kind == "pair":
                return const[:, a + 32 - 2 * t:a + 32 - 2 * t + 34]
            return const[:, a:a + 34]

        done = fan_in(jobs, 34, lhs1, 7)
        rr, _ = root(PS[0:34, 7, :], TMP[0:34, 4, :], [done], 512)
        turned_a = turn_values(T_VA, 4, None, 0)
        turn_values(T_VB, 2, None, 4)
        weights = {T_QA: (wq8[:, 4 * l:4 * l + 1], 4), T_KA: (Pm("kn_a", l), 4),
                   T_QB: (wq8[:, 4 * l + 1:4 * l + 2], 6), T_KB: (Pm("kn_b", l), 2)}

        def spread(n, tile, lhs, rhs, wgt, cols, free, rows=slice(0, P), src=None):
            b = n % 4
            wait(PE, free[b])
            m = pe(PE.matmul(PS[:, b, 0:cols], lhs, rhs[:, 0:cols], start=True, stop=True))
            wait(VE, m)
            src = T[rows, tile, 0:cols] if src is None else src
            free[b] = dve(VE.scalar_tensor_tensor(T[rows, tile, 0:cols], src, wgt, PS[rows, b, 0:cols],
                                                  ALU.mult, ALU.mult))
            return free[b]

        wait(PE, rr, sel_in)
        free = list(turned_a)
        normed = {}
        for n, (tile, kind, t, cols) in enumerate(jobs):
            if kind == "pair":
                lo_ = max(k for k in weights if k <= tile)
                normed[tile] = spread(n, tile, sel[:, t, :], TMP[0:32, 4, :], weights[lo_][0], cols, free)
            else:
                r = 32 + (kind == "ckv")
                base_, w_ = (T_CQ, "qa_norm") if kind == "cq" else (T_CKV, "kva_norm")
                i = tile - base_
                w_ap = Pm(w_, (6 if kind == "cq" else 4) * l + i)
                normed[tile] = spread(n, tile, const[0:34, r:r + 1].to_broadcast([34, P]), TMP[0:34, 4, :],
                                      w_ap, cols, free)

        def rope(tiles, marks, tmp=(6, 7)):
            free = [None] * 4
            tf = [None] * 2
            out = {}
            for n, tile in enumerate(tiles):
                b, i = n % 4, n % 2
                wait(PE, free[b], marks[tile])
                m = pe(PE.matmul(PS[:, b, 0:L], C("rot"), T[:, tile, 0:L], start=True, stop=True))
                wait(VE, m, tf[i])
                v = dve(VE.tensor_tensor(TMP[:, tmp[i], 0:L], PS[:, b, 0:L], C("sin"), ALU.mult))
                free[b] = v
                wait(PO, m)
                c = pool(PO.tensor_tensor(T[:, tile, 0:L], T[:, tile, 0:L], C("cos"), ALU.mult))
                wait(VE, v, c)
                tf[i] = out[tile] = dve(VE.tensor_tensor(T[:, tile, 0:L], T[:, tile, 0:L],
                                                         TMP[:, tmp[i], 0:L], ALU.add))
            return out

        wait(PE, *[m for m in free])
        wait(VE, done)
        roped = rope([T_QB + t for t in range(6)] + [T_KB + t for t in range(2)], normed)

        cq_split = {}

        def split_cq(k):
            a = act(AC.activation(HH[:, 10 + k, 0:nq], T[:, T_CQ + k, 0:nq], ACT.Copy))
            wait(VE, a)
            cq_split[k] = dve(VE.tensor_tensor(HL[:, 10 + k, 0:nq], T[:, T_CQ + k, 0:nq],
                                               HH[:, 10 + k, 0:nq].bitcast(F32), ALU.subtract))

        wait(VE, everything())
        wait(AC, everything())
        wait(PE, everything(), masked)
        wait(PO, everything(), *z_stored)
        ns = dve(VE.tensor_scalar(nsink[:, :], param[:, s0 + H_B * l:s0 + H_B * (l + 1)], -1.0, None, ALU.mult))
        wait(VE, ns)
        wait(AC, ns)
        state = {"S": [None] * 3, "P": [None] * 3, "PT": {}, "T": [None] * 2, "O": {},
                 "z": None, "stat": [None] * 4, "y": None, "copy": {}, "n": 0, "t": 0, "last_s": [None] * 2}
        queue = []

        def later(due, fn):
            queue.append((due, fn))

        def run_due(u):
            while any(due <= u for due, _ in queue):
                n = min(n for n, (due, _) in enumerate(queue) if due == min(d for d, _ in queue))
                queue.pop(n)[1]()

        def unit(u, terms, nk, sinks):
            b = u % 3
            wait(PE, state["S"][b])
            for j, (lt, rt_, c0, cn) in enumerate(terms):
                mm = PE.matmul(PS[:, b, c0:c0 + cn], lt, rt_, start=(j == 0), stop=(j == len(terms) - 1),
                               skip_group_check=True)
            scored = pe(mm)
            i = u % 4
            wait(VE, scored, state["stat"][i])
            S = PS[:, b, 0:nk]
            mx = dve(VE.tensor_reduce(stat[:, i, 0:1], S, AXX, ALU.max, negate=True))
            if sinks is not None:
                wait(VE, mx)
                mx = dve(VE.tensor_tensor(stat[:, i, 0:1], stat[:, i, 0:1], sinks[0], ALU.min))
            wait(AC, mx, state["P"][b], state["stat"][i])
            ex = act(AC.activation(TMP[:, b, 0:nk], S, ACT.Exp, bias=stat[:, i, 0:1],
                                   accum_out=stat[:, i, 1:2]))
            state["S"][b] = ex
            state["stat"][i] = ex
            if sinks is not None:
                ex = act(AC.activation(stat[:, i, 3:4], sinks[1], ACT.Exp, bias=stat[:, i, 0:1]))
                state["stat"][i] = ex

            return b, ex

        def normalise(u, b, nk, ex, sinks):
            i = u % 4
            wait(VE, ex)
            if sinks is not None:
                sm = dve(VE.tensor_tensor(stat[:, i, 1:2], stat[:, i, 1:2], stat[:, i, 3:4], ALU.add))
                wait(VE, sm)
            rc = dve(VE.reciprocal(stat[:, i, 2:3], stat[:, i, 1:2]))
            wait(VE, rc)
            pn = dve(VE.tensor_scalar(TMP[:, b, 0:nk], TMP[:, b, 0:nk], stat[:, i, 2:3], None, ALU.mult))
            state["stat"][i] = pn
            return pn

        def turned(u, b, pn, nk, pt, q0, pt_free):
            tb = 3 + u % 2
            wait(PE, pn, state["T"][u % 2])
            for kt in range(nk // P):
                mm = PE.transpose(PS[:, tb, kt * P:(kt + 1) * P], TMP[:, b, kt * P:(kt + 1) * P], ident)
            m = pe(mm)
            state["P"][b] = m
            src = PS[:, tb, 0:nk].rearrange("p (a b) -> p a b", b=P)
            dst = pt[:, :, q0:q0 + P]
            if u % 4 == 3:
                wait(AC, m, pt_free)
                e = act(AC.activation(dst, src, ACT.Copy))
            else:
                wait(VE, m, pt_free)
                e = dve(VE.tensor_copy(dst, src))
            state["T"][u % 2] = e
            return e

        PTL = TMP[:, 8:10, :].rearrange("p a b -> p (a b)").rearrange("p (k q) -> p k q", q=256)
        PTC = TMP[:, 5, :].rearrange("p (k q) -> p k q", q=256)
        PTC_UP = TMP[:, 3, :].rearrange("p (k q) -> p k q", q=256)
        PT = {(0, 0, False): PTL, (0, 0, True): PTC, (0, 1, False): pt_up, (0, 1, True): PTC_UP}
        if last:
            PT[(1, 0, False)] = LF[:, 0:4, 256:512]
            PT[(1, 1, False)] = HF[:, 0:4, 256:512]
        PTL_UP = T[:, 31:33, :].rearrange("p a b -> p (a b)").rearrange("p (k q) -> p k q", q=256)
        PT_C = {(0, 0, False): PTL, (0, 0, True): PTC, (1, 0, False): PTL_UP, (1, 0, True): PTC_UP}

        def halves_apart(i, tile):
            wait(AC, state["last_s"][i % 2])
            a = act(AC.activation(q_up[:, i % 2, 0:nq], T[:, tile, 0:nq], ACT.Copy, scale=C("halves")[:, 1:2]))
            wait(AC, a)
            state["q"] = act(AC.activation(T[:, tile, 0:nq], T[:, tile, 0:nq], ACT.Copy,
                                           scale=C("halves")[:, 0:1]))
            return state["q"]

        def y_tile(side, heads, score_terms, v_of, v_rows, y_index, sinks_of, zbuf, PT):
            zin = []
            us = [(h, 2 * c + j) for c in range(streams) for h in range(heads) for j in range(2)]
            pt_marks = []
            pset = state["t"] % (1 + ((1, 0, False) in PT))
            o_bank = 5 + (state["t"] % 2 if last else 0)
            state["t"] += 1

            def after(u, h, qt, b, pn):
                ctx_ = qt >= 2
                pt_marks.append(turned(u, b, pn, 256 if ctx_ else 512, PT[(pset, h, ctx_)], P * (qt % 2),
                                       state["PT"].get((pset, ctx_))))
                if qt % 2 == 0 or h < heads - 1:
                    return
                kts = [2, 3] if ctx_ else [0, 1, 2, 3]
                per = max(1, len(kts) // (2 * heads))
                for n in range(0, len(kts), per):
                    later(u + 3 + n // per, lambda n=n: values(ctx_, kts, n, per))
                if (h, qt) == us[-1]:
                    zin.append(z_load())
                    end = u + 3 + len(kts) // per
                    later(end, finish)
                    later(end + 1, finish_lo)

            def z_load():
                wait(PO, state["zfree"][zbuf])
                return load(zbuf + 2, PO, TMP[:, zbuf, 0:nq], z_d[y_index][:, 0:nq])

            def values(ctx_, kts, n0, per):
                wait(PE, pt_marks, state["O"].get(o_bank) if not ctx_ and n0 == 0 else None)
                c0 = 256 * ctx_
                for n in range(n0, n0 + per):
                    for hh in range(heads):
                        mm = PE.matmul(PS[v_rows(hh), o_bank, c0:c0 + 256], v_of(hh, kts[n]),
                                       PT[(pset, hh, ctx_)][:, n, :], start=(n == 0), stop=(n == len(kts) - 1))
                state["PT"][(pset, ctx_)] = state["o_done"] = pe(mm)

            def finish():
                wait(VE, state["o_done"], zin, state["y"])
                y1 = dve(VE.tensor_tensor(TMP[:, 4, 0:nq], PS[:, o_bank, 0:nq], TMP[:, zbuf, 0:nq], ALU.mult))
                state["O"][o_bank] = y1
                state["zfree"][zbuf] = y1
                wait(AC, y1, side and ada_last["turned"])
                state["y_hi"] = act(AC.activation(HH[:, y_index, 0:nq], TMP[:, 4, 0:nq], ACT.Copy))

            def finish_lo():
                wait(VE, state["y_hi"])
                state["y"] = dve(VE.tensor_tensor(HL[:, y_index, 0:nq], TMP[:, 4, 0:nq],
                                                  HH[:, y_index, 0:nq].bitcast(F32), ALU.subtract))

            for h, qt in us:
                u = state["n"]
                state["n"] += 1
                nk = 256 if qt >= 2 else 512
                sinks = sinks_of(h) if sinks_of else None
                b, ex = unit(u, score_terms(h, qt), nk, sinks)
                state["scored"] = Mark(pe_n, pe_n.v)
                if side:
                    side(u, False)
                marks = {}
                later(u + 1, lambda u=u, b=b, nk=nk, ex=ex, sinks=sinks, marks=marks:
                      marks.update(pn=normalise(u, b, nk, ex, sinks)))
                later(u + 2, lambda u=u, h=h, qt=qt, b=b, marks=marks: after(u, h, qt, b, marks["pn"]))
                run_due(u)
                if side:
                    side(u, True)

        state["zfree"] = {6: None, 7: None}

        def drain():
            run_due(1 << 30)

        def half(h):
            return slice(64 * (h % 2), 64 * (h % 2) + 64)

        side = None
        if not last:
            step_ab = ada_beside(ADA_FIRST, HF[0:4, 9, :])

            def side(u, split):
                if split:
                    ahead(1, CH if u < 80 - RING else 2 * 3 * P, True)
                else:
                    step_ab()
        q_tiles = [T_QA + i for i in range(4)] + [T_QB + i for i in range(6)]
        q_apart = [halves_apart(0, q_tiles[0])]

        def next_queries(n):
            wait(PE, q_apart[n])
            if n + 1 < len(q_tiles):
                q_apart.append(halves_apart(n + 1, q_tiles[n + 1]))

        for i in range(4):
            next_queries(i)

            def terms(h, qt, i=i):
                q = (q_up[:, i % 2, :] if h else T[:, T_QA + i, :])[:, P * qt:P * qt + P]
                if qt >= 2:
                    return [(q, T[:, T_KA + i, 256:512], 0, 256)]
                return [(q, T[:, T_KA + i, :], 0, 512),
                        (C("rev"), bias[qt][:, 2 * i + h::H_A, :], 0, 256)]

            def v_of(h, kt, i=i):
                return T[:, T_VA + kt, P * i + 64 * h:P * i + 64 * h + 64]

            zb = 6 + i % 2
            y_tile(side, 2, terms, v_of, half, i, None, zb, PT)
            state["last_s"][i % 2] = state["scored"]
        bias_read = state["scored"]
        for i in range(6):
            kvt = i // 3
            next_queries(4 + i)
            if 1 <= i <= 4:
                wait(AC, bias_read)
                wait(VE, bias_read)
                split_cq(i - 1)

            def terms(h, qt, i=i, kvt=kvt):
                q = (q_up[:, i % 2, :] if h else T[:, T_QB + i, :])[:, P * qt:P * qt + P]
                if qt >= 2:
                    return [(q, T[:, T_KB + kvt, 256:512], 0, 256)]
                a = CONST["band"][0] + P * qt
                return [(q, T[:, T_KB + kvt, :], 0, 512),
                        (ident, const[:, a:a + P], P * (1 - qt), P)]

            vflat = T[:, T_VB:T_VB + 2, :].rearrange("p a b -> p (a b)")

            def v_of(h, kt, kvt=kvt):
                c = 256 * kt + P * kvt + 64 * h
                return vflat[:, c:c + 64]

            def sinks_of(h, i=i):
                c = s0 + H_B * l + 2 * i + h
                return nsink[:, 2 * i + h:2 * i + h + 1], param[:, c:c + 1]

            zb = 6 + i % 2
            y_tile(side, 2, terms, v_of, half, 4 + i, sinks_of, zb, PT)
            state["last_s"][i % 2] = state["scored"]
        if not last:
            ada_row[0] = T[0:4, 0, :]
            ada_flush([0])
        scores_done = Mark(pe_n, pe_n.v)
        drain()
        ada_flush([1, 2])
        after_ab = everything()

        def cq_ready(k):
            if k == 4:
                wait(AC, after_ab)
                wait(VE, after_ab)
            if k >= 4:
                split_cq(k)
            return cq_split[k]

        def split_ckv(k):
            wait(AC, scores_done, cq_split[5])
            a = act(AC.activation(TR[:, 9 + k, :], T[:, T_CKV + k, :], ACT.Copy))
            wait(VE, a)
            return dve(VE.tensor_tensor(TR[:, T_CKV + k, :], T[:, T_CKV + k, :],
                                        TR[:, 9 + k, :].bitcast(F32), ALU.subtract))

        def evac_c(t0, mt, n):
            def evac(g, bank0, done):
                wait(AC, done)
                wait(VE, done)
                marks = []
                for m in range(mt):
                    dst = T[:, t0 + mt * g + m, 0:n]
                    if m % 2:
                        marks.append(act(AC.activation(dst, PS[:, bank0 + m, 0:n], ACT.Copy)))
                    else:
                        marks.append(dve(VE.tensor_copy(dst, PS[:, bank0 + m, 0:n])))
                return marks
            return evac

        wait(PO, after_ab)
        sel_in = load(1, PO, sel[:, :, :], sel_d)
        st["set"] = 0
        set_free[0] = [*state["S"], state["T"][0]]
        set_free[1] = [state["T"][1], *state["O"].values(), *ada_free, *after_ab]
        gemm(3, 6, 3, nq, HH[:, 10:16, :], HL[:, 10:16, :], evac_c(0, 3, nq), cq_ready)
        ckv_split = [split_ckv(k) for k in range(4)]
        gemm(3, 4, 4, 512, TR[:, 9:13, :], TR[:, T_CKV:T_CKV + 4, :], evac_c(T_KN, 4, 512), ckv_split)
        n_bank = 4 * st["set"] + 3
        for e in (AC, PE):
            wait(e, after_ab, *set_free)
        jobs = [(T_KN + h, "nope", 6 + h, 512) for h in range(6)] + [(T_KPE, "kpe", 0, 512)]
        jobs += [(T_QN + h, "nope", h, nq) for h in range(6)] + [(T_QR + t, "rope", t, nq) for t in range(3)]

        def lhs2(kind, t):
            a = CONST[kind][0]
            if kind == "nope":
                return const[:, a + 11 - t:a + 23 - t]
            if kind == "rope":
                return const[:, a + 10 - 2 * t:a + 22 - 2 * t]
            return const[:, a:a + 12]

        done = fan_in(jobs, 12, lhs2, n_bank)
        flush()
        values_in = [*set_free[0], *set_free[1]]
        rr, root_read = root(PS[0:12, n_bank, :], TMP[0:12, 4, :], [done], 512)
        wait(PE, values_in, root_read)
        turned_c = turn_values(T_VC, 6, None, 0)
        wait(VE, rr)
        kp = dve(VE.tensor_scalar(T[:, T_KPE, :], T[:, T_KPE, :], Pm("kn_r", l), None, ALU.mult))
        wait(PE, rr, sel_in)
        free = turned_c[0:4]
        n = 0
        marks = {T_KPE: kp}
        for h in range(6):
            for tile, r, w_, cols in ((T_QN + h, h, wq8[:, 4 * l + 2:4 * l + 3], nq),
                                      (T_KN + h, 6 + h, Pm("kn_n", l), 512)):
                spread(n, tile, const[0:12, r:r + 1].to_broadcast([12, P]), TMP[0:12, 4, :], w_, cols, free)
                n += 1
        for t in range(3):
            marks[T_QR + t] = spread(n, T_QR + t, sel[0:12, t, :], TMP[0:12, 4, :], wq8[:, 4 * l + 3:4 * l + 4],
                                     nq, free)
            n += 1
        wait(PE, free)
        wait(VE, done)
        roped = rope([T_KPE] + [T_QR + t for t in range(3)], marks)
        wait(PE, everything())
        wait(VE, roped[T_KPE])
        free = [None] * 4
        for t in range(3):
            b = t
            m = pe(PE.matmul(PS[:, b, :], sel[0:12, 3 + t, :], TMP[0:12, 4, :], start=True, stop=True))
            wait(VE, m)
            dve(VE.tensor_tensor(T[:, T_KR + t, :], T[:, T_KPE, :], PS[:, b, :], ALU.mult))
        for e in (PE, VE, AC, PO):
            wait(e, everything())
        c_apart = []

        def copy_c():
            n = len(c_apart)
            if n < 6:
                c_apart.append(act(AC.activation(T[:, T_COPY_C[n], 0:nq], T[:, T_QR + n // 2, 0:nq],
                                                 ACT.Copy, scale=C("halves")[:, n % 2:n % 2 + 1])))

        copy_c()
        ahead(RING, CH)
        vcf = T[:, T_VC:T_VC + 6, :].rearrange("p a b -> p (a b)")
        if not last:
            step_c = ada_beside(ADA_FIRST + 10, T[0:4, 9, :])

            def side(u, split):
                for part in range(2):
                    if split:
                        ahead(1, CH, part == 1)
                    else:
                        step_c()
        for h_ in range(6):
            def terms(h, qt, h_=h_):
                q = slice(P * qt, P * qt + P)
                k = slice(256, 512) if qt >= 2 else slice(0, 512)
                n = 256 if qt >= 2 else 512
                return [(T[:, T_QN + h_, q], T[:, T_KN + h_, k], 0, n),
                        (T[:, T_COPY_C[h_], q], T[:, T_KR + h_ // 2, k], 0, n)]

            def v_of(h, kt, h_=h_):
                c = 768 * kt + P * h_
                return vcf[:, c:c + P]

            copy_c()
            wait(PE, c_apart[h_])
            zb = 6 + h_ % 2
            y_tile(side, 1, terms, v_of, lambda h: slice(0, P), 10 + h_, None, zb, PT_C)
        ada_flush([0])
        drain()
        ada_flush([1, 2])

        wait(PO, everything())
        if l == 0:
            xo = [load(5, PO, T[:, 16:32, :], xT)]
        else:
            xo = [load(5, PO, T[:, 16:32, :], x_d)]
            meta_in = load(6, PO, RES[:, :, 0:META], metaT)
        set_free[0] = set_free[1] = everything()
        for e in (AC, VE, PO):
            wait(e, everything())
        x_new = []
        sq = new_squares()

        def out_evac(g, bank0, done):
            marks = []
            wait(VE, done, xo)
            for m in range(4):
                k = 4 * g + m
                for s in range(streams):
                    c = slice(256 * s, 256 * s + 256)
                    dst = RES[:, k, META:] if last else T[:, k, c]
                    v = dve(VE.scalar_tensor_tensor(dst, PS[:, bank0 + m, c],
                                                    ada[:, A0 + 2 * DT + k, s:s + 1], T[:, 16 + k, c],
                                                    ALU.mult, ALU.add))
                marks.append(v)
                x_new.append(v)
                if last:
                    wait(AC, meta_in)
                    square_add(RES[:, k, :], N2, v, k, sq, [T[:, 2, :], T[:, 3, :]], T[:, 0, :])
                else:
                    square_add(T[:, k, :], 512, v, k, sq)
                if m < 3:
                    yield
            return marks

        gemm(4, DT, 4, nq, HH, HL, out_evac, [state["y"]] * DT)
        sqrt_table()
        ahead(RING - 1, CH)
        flush()
        ahead(1, CH)
        ring["squares"] = sq
        if last:
            ring["meta"] = meta_in
            return x_new
        wait(PO, *x_new)
        ring["x_stored"] = store(4, PO, x_d, T[:, 0:16, :])
        wait(PO, ring["x_stored"])
        ring["y_free"] = Mark(pe_n, pe_n.v)
        return x_new

    def new_squares(by_pe=lambda k: k >= DT - 4, start=None):
        return {"free": {}, "acc": None, "n": 0, "by_pe": by_pe, "start": start, "bank": None}

    def square_add(src, n, ready, k, sq, bufs=None, acc=None):
        bufs = bufs or [TMP[:, 8, :], TMP[:, 9, :]]
        acc = acc if acc is not None else TMP[:, 5, :]
        if k == 0:
            wait(AC, ready, sq["start"])
            sq["acc"] = act(AC.activation(acc[:, 0:n], src, ACT.Square))
            return
        i = sq["n"] % len(bufs)
        sq["n"] += 1
        wait(AC, ready, sq["free"].get(i))
        a = act(AC.activation(bufs[i][:, 0:n], src, ACT.Square))
        if not sq["by_pe"](k):
            wait(PO, a, sq["acc"])
            sq["acc"] = sq["free"][i] = pool(PO.tensor_tensor(acc[:, 0:n], acc[:, 0:n], bufs[i][:, 0:n],
                                                              ALU.add))
            return

        if sq["bank"] is None:
            sq["set"] = st["set"]
            sq["bank"] = 4 * st["set"] + 3
            wait(PE, set_free[st["set"]])
            if not sq["by_pe"](1):
                wait(PE, sq["acc"])
                mean(sq, acc, n, True, False)
        wait(PE, a)
        sq["free"][i] = sq["msq"] = mean(sq, bufs[i], n, k == 1, k == DT - 1)

    def mean(sq, buf, n, first, last_):
        for t, a0 in enumerate(range(0, n, P)):
            w = min(P, n - a0)
            mm = PE.matmul(PS[0:w, sq["bank"], t:t + 1], buf[:, a0:a0 + w], C("mean"),
                           start=first and t == 0, stop=last_, skip_group_check=True)
        return pe(mm)

    def sqrt_table():
        act(AC.activation(stat[:, 1, 0:1], C("eps"), ACT.Sqrt))

    def rms_rows(sq, n, dst):
        full, rest = n // P, n % P
        parts = [(stat[:, 0, 0:full], PS[:, sq["bank"], 0:full], P)]
        if rest:
            parts.append((stat[0:rest, 0, full:full + 1], PS[0:rest, sq["bank"], full:full + 1], rest))
        wait(AC, sq["msq"])
        for small, src, rows in parts:
            r = act(AC.activation(small, src, ACT.Sqrt, bias=C("eps", rows)))
        wait(VE, r)
        for small, src, rows in parts:
            r = dve(VE.reciprocal(small, small))
        wait(PE, r)
        for t, a0 in enumerate(range(0, n, P)):
            w = min(P, n - a0)
            mm = PE.matmul(PS[:, sq["bank"], a0:a0 + w], stat[0:w, 0, t:t + 1].to_broadcast([w, P]),
                           ident[0:w, 0:w], start=True, stop=True)
        wait(VE, pe(mm))
        c = dve(VE.tensor_copy(dst, PS[:, sq["bank"], 0:n]))
        set_free[sq["set"]] = list(set_free[sq["set"]]) + [c]
        return c

    x_in = load(7, PO, T[:, 0:16, :], xT)
    squares = new_squares(by_pe=lambda k: k % 2 == 1)
    squared = []

    def first_squares():
        for k in range(len(squared), min(len(squared) + 2, DT)):
            square_add(T[:, k, :], 512, x_in, k, squares, [TMP[:, 6 + j, :] for j in range(4)])
            squared.append(k)

    pr.repeat(ADA_FIRST // 2, ada_turn)
    wait(PE, squares["acc"])
    squares["msq"] = mean(squares, TMP[:, 5, :], 512, False, True)
    ring["squares"] = squares
    ada_pend[:] = [(ADA_FIRST - 1, 1, ada_pend[0][2])]
    wait(AC, const_in)
    wait(VE, const_in)
    wait(PO, const_in)
    sqrt_table()
    ahead(RING - 2, CH)
    ada_flush()
    ahead(2, CH)
    set_free[1] = [*ada_free]
    new = layer(0, lambda k: T[:, k, :], [x_in] * DT)
    new = layer(1, lambda k: T[:, k, :], new)
    second(pr, locals(), new)
    return pr


def second(pr, env, x_new):
    nc = pr.nc
    wait = pr.wait
    SP, AC, VE, PO, PE = nc.sync, nc.scalar, nc.vector, nc.gpsimd, nc.tensor
    (act, dve, pool, pe, gemm, flush, C, Pm, PS, RES, NH, NL, PH, PL, CHI, CLO, YA, G4, FH, FL, T2, T3, T4, CV,
     set_free, square_add, ring, param, act_n, dve_n, pe_n, pool_n, store, out_d, T, new_squares, rms_rows, sqrt_table, ahead) = (
        env[k] for k in ("act dve pool pe gemm flush C Pm PS RES NH NL PH PL CHI CLO YA G4 FH FL T2 T3 T4 CV "
                         "set_free square_add ring param act_n dve_n pe_n pool_n store out_d T new_squares rms_rows "
                         "sqrt_table ahead").split())
    N = N2
    everything = lambda: [Mark(x, x.v) for x in (act_n, dve_n, pe_n, pool_n)]
    norm_tmp = [T2[:, j, 0:N] for j in range(4)]
    last_tmp = [T4[:, j, :] for j in range(4)]

    def sync_all():
        for e in (AC, VE, PO, PE):
            wait(e, everything())

    def norm(squares, wname, hi, lo, n, hi_free=None, out=None, tmp=norm_tmp):
        RSTD = tmp[1][:, 0:n]
        rstd = rms_rows(squares, n, RSTD)
        wait(VE, rstd)
        free = [None, None]

        def scaled(k):
            wait(VE, free[k % 2])
            made["scaled"] = dve(VE.scalar_tensor_tensor(T2[:, 4 + k % 2, 0:n], RES[:, k, N - n:], Pm(wname, k),
                                                         RSTD, ALU.mult, ALU.mult))

        def make(k):
            i = k % 2
            if out is not None:
                return dve(VE.scalar_tensor_tensor(out[:, k, N - n:], RES[:, k, N - n:], Pm(wname, k), RSTD,
                                                   ALU.mult, ALU.mult))
            if k == 0:
                scaled(0)
            wait(AC, made["scaled"], hi_free)
            a = act(AC.activation(hi[:, k, 0:n], T2[:, 4 + i, 0:n], ACT.Copy))
            if k + 1 < DT:
                scaled(k + 1)
            wait(VE, a, hi_free)
            free[i] = dve(VE.tensor_tensor(lo[:, k, 0:n], T2[:, 4 + i, 0:n], hi[:, k, 0:n].bitcast(F32),
                                           ALU.subtract))
            made["last"] = free[i]
            return free[i]
        return make

    made = {}
    sync_all()
    wait(AC, ring["meta"])
    wait(VE, ring["meta"])
    hn = norm(ring["squares"], "norm_mix", NH, NL, N)

    pooled = []
    uf = {"free": [[], []]}

    def u_evac(g, bank0, done):
        w = WINDOWS[g]
        free = []
        if g == 0:
            wait(VE, made["last"])
            for j in range(8):
                uf["zero"] = dve(VE.memset(T2[:, j, 0:16], 0.0))
        wait(AC, done, uf["zero"])
        for m in range(4):
            k = 4 * g + m
            base = 4 * (m % 2)
            wait(AC, uf["free"][m % 2])
            u = act(AC.activation(T2[:, base, 16:16 + N], PS[:, bank0 + m, 0:N], ACT.Copy))
            free = u
            src, step, prev = base, 1, u
            wait(VE, uf["free"][m % 2])
            while step < w:
                dst = base + 1 + (src - base) % 2
                wait(VE, prev)
                prev = dve(VE.tensor_tensor(T2[:, dst, 16:16 + N], T2[:, src, 16:16 + N],
                                            T2[:, src, 16 - step:16 + N - step], ALU.add))
                src, step = dst, step * 2
            wait(VE, prev)
            q = base + 3
            prev = dve(VE.scalar_tensor_tensor(T2[:, q, 0:L], T2[:, src, 16 + META:16 + N], 1.0 / w,
                                               T2[:, base, 16 + META:16 + N], ALU.mult, ALU.subtract))
            wait(AC, prev)
            a = act(AC.activation(PH[:, k, 0:L], T2[:, q, 0:L], ACT.Copy))
            wait(VE, a, prev)
            v = dve(VE.tensor_tensor(PL[:, k, 0:L], T2[:, q, 0:L], PH[:, k, 0:L].bitcast(F32), ALU.subtract))
            uf["free"][m % 2] = [v]
            pooled.append(v)
            if m < 3:
                yield
        return [free]

    gemm(4, DT, 4, N, NH, NL, u_evac, hn)
    latent_hi, latent_lo = NH[:, :, META:], NL[:, :, META:]

    cf = {"conv": None, "gc": [None] * 4, "cv": [None] * 4}
    conv_ready = []

    def gc_evac(g, bank0, done):
        wait(AC, done, cf["conv"])
        out = []
        for m in range(4):
            a = act(AC.activation(CV[:, m, 0:N], PS[:, bank0 + m, 0:N], ACT.Copy))
            cf["gc"][m] = a
        return [a]

    def v_evac(g, bank0, done):
        wait(VE, done, *cf["gc"])
        for m in range(4):
            v = dve(VE.tensor_tensor(CV[:, m, 0:N], CV[:, m, 0:N], PS[:, bank0 + m, 0:N], ALU.mult))
            cf["cv"][m] = v
        free = v
        return [free]

    def gb_evac(j):
        def evac(g, bank0, done):
            wait(VE, done, *cf["cv"])
            for m in range(4):
                k = 4 * j + m
                Y = T3[:, m % 2, 0:L]
                wait(VE, cf.get(("y", m % 2)))
                a = dve(VE.tensor_scalar(Y, CV[:, m, META - 2:N - 2], Pm("conv_w", k), None, ALU.mult))
                for tap in (1, 2):
                    wait(VE, a)
                    a = dve(VE.scalar_tensor_tensor(Y, CV[:, m, META - 2 + tap:N - 2 + tap], Pm("conv_w", DT * tap + k), Y,
                                                    ALU.mult, ALU.add))
                wait(VE, a)
                a = dve(VE.tensor_tensor(Y, Y, PS[:, bank0 + m, 0:L], ALU.mult))
                free = a
                wait(AC, a)
                h = act(AC.activation(CHI[:, k, 0:L], Y, ACT.Copy))
                wait(VE, h)
                v = dve(VE.tensor_tensor(CLO[:, k, 0:L], Y, CHI[:, k, 0:L].bitcast(F32), ALU.subtract))
                cf[("y", m % 2)] = v
                conv_ready.append(v)
                if m < 3:
                    yield
            cf["conv"] = free
            return [free]
        return evac

    def ya_evac(gp):
        def evac(g, bank0, done):
            wait(VE, done)
            for m in range(4):
                k = 4 * gp + m
                v = dve(VE.tensor_scalar(YA[:, k, 0:L], PS[:, bank0 + m, 0:L], Pm("pool_scale", k), None, ALU.mult))
            return [v]
        return evac

    for j in range(4):
        gemm(1, DT, 4, N, NH, NL, gc_evac)
        if j == 0:
            for gp in range(4):
                gemm(1, 4, 4, L, PH[:, 4 * gp:4 * gp + 4, :], PL[:, 4 * gp:4 * gp + 4, :], ya_evac(gp),
                     pooled[4 * gp:4 * gp + 4])
        gemm(1, DT, 4, N, NH, NL, v_evac)
        gemm(1, DT, 4, L, latent_hi, latent_lo, gb_evac(j))

    gt = {"g": None, "y": None}
    mixed = []

    def ga_evac(j):
        def evac(g, bank0, done):
            wait(AC, done)
            for m in range(4):
                k = 4 * j + m
                i = 2 + m % 2
                wait(AC, cf.get(("s", m % 2)))
                a = act(AC.activation(T3[:, i, 0:L], PS[:, bank0 + m, 0:L], ACT.Sigmoid, bias=Pm("b_gate", k)))
                wait(VE, a)
                cf[("s", m % 2)] = dve(VE.tensor_tensor(YA[:, k, 0:L], YA[:, k, 0:L], T3[:, i, 0:L], ALU.mult))
                if m < 3:
                    yield
            gt["ya"] = cf[("s", 1)]
            return [a]
        return evac

    def gbr_evac(j):
        def evac(g, bank0, done):
            wait(AC, done, gt["g"])
            for m in range(4):
                a = act(AC.activation(G4[:, m, 0:L], PS[:, bank0 + m, 0:L], ACT.Sigmoid,
                                      bias=Pm("b_gate", DT + 4 * j + m)))
            gt["gr"] = a
            return [a]
        return evac

    def mix_evac(j):
        def evac(g, bank0, done):
            wait(VE, done, gt["gr"], gt["ya"])
            for m in range(4):
                k = 4 * j + m
                Y = T3[:, m % 2, 0:L]
                wait(VE, cf.get(("y", m % 2)))
                a = dve(VE.tensor_tensor(Y, PS[:, bank0 + m, 0:L], G4[:, m, 0:L], ALU.mult))
                free = a
                wait(VE, a)
                a = dve(VE.tensor_tensor(Y, Y, YA[:, k, 0:L], ALU.add))
                wait(AC, a)
                h = act(AC.activation(PH[:, k, 0:L], Y, ACT.Copy))
                wait(VE, h)
                v = dve(VE.tensor_tensor(PL[:, k, 0:L], Y, PH[:, k, 0:L].bitcast(F32), ALU.subtract))
                cf[("y", m % 2)] = v
                mixed.append(v)
                if m < 3:
                    yield
            gt["g"] = free
            return [free]
        return evac

    for j in range(4):
        gemm(1, DT, 4, L, latent_hi, latent_lo, ga_evac(j))
        gemm(1, DT, 4, L, latent_hi, latent_lo, gbr_evac(j))
        gemm(1, DT, 4, L, CHI, CLO, mix_evac(j), conv_ready)

    def add_evac(sq, tmp):
        def evac(g, bank0, done):
            wait(VE, done)
            for m in range(4):
                k = 4 * g + m
                v = dve(VE.tensor_tensor(RES[:, k, META:], RES[:, k, META:], PS[:, bank0 + m, 0:L], ALU.add))
                square_add(RES[:, k, META:], L, v, k, sq, tmp[2:], tmp[0])
                if m < 3:
                    yield
            return [v]
        return evac

    sq = new_squares(start=Mark(pe_n, pe_n.v))
    gemm(4, DT, 4, L, PH, PL, add_evac(sq, norm_tmp), mixed)
    sqrt_table()
    ahead(RING - 1, CH)
    flush()
    ahead(1, CH)
    hn = norm(sq, "norm_ffn", NH, NL, L, Mark(pe_n, pe_n.v))

    ff = {"s": [None] * 2, "y": [None] * 2, "last": None}

    def ffn_evac(g, bank0, done):
        wait(AC, done, made["last"])
        wait(VE, done)
        for m in range(2):
            wait(AC, ff["s"][m])
            a = act(AC.activation(T3[:, 2 + m, 0:L], PS[:, bank0 + m, 0:L], ACT.Silu))
            wait(VE, a, ff["y"][m])
            Y = T3[:, m, 0:L]
            v = dve(VE.tensor_tensor(Y, T3[:, 2 + m, 0:L], PS[:, bank0 + 2 + m, 0:L], ALU.mult))
            ff["s"][m] = v
            free = v
            wait(AC, v)
            h = act(AC.activation(FH[:, 2 * g + m, 0:L], Y, ACT.Copy))
            wait(VE, h)
            ff["y"][m] = dve(VE.tensor_tensor(FL[:, 2 * g + m, 0:L], Y, FH[:, 2 * g + m, 0:L].bitcast(F32),
                                              ALU.subtract))
            if m < 1:
                yield
        return [a, free]

    gemm(FT // 2, DT, 4, L, NH, NL, ffn_evac, hn)
    before = Mark(dve_n, dve_n.v)
    sq = new_squares(start=Mark(pe_n, pe_n.v))
    gemm(4, FT, 4, L, FH, FL, add_evac(sq, last_tmp), lambda k: before if k < FT - 2 else ff["y"][1])
    sqrt_table()
    flush()
    final = norm(sq, "norm_final", None, None, L, out=RES, tmp=last_tmp)
    for k in range(DT):
        final(k)
    wait(SP, *everything())
    o = store(5, SP, out_d, RES[:, :, META:])
    wait(SP, o)
    for e in (AC, VE, PO, PE):
        wait(e, o)


def constants():
    c = np.zeros((P, NCONST), np.float32)

    def put(name, v):
        a, b = CONST[name]
        c[:v.shape[0], a:b] = v

    i = np.arange(P)
    put("ident", np.eye(P, dtype=np.float32))
    rev = np.zeros((P, P), np.float32)
    rev[i, (i // 64) * 64 + 63 - i % 64] = 1
    put("rev", rev)
    rot = np.zeros((P, P), np.float32)
    for m in range(P):
        b = m % 64 // 16
        rot[m + 16 if b % 2 == 0 else m - 16, m] = -1 if b % 2 == 0 else 1
    put("rot", rot)
    t = np.arange(L)
    nf = ROPE // 4
    inv = np.float32(10000.0) ** (-np.arange(nf, dtype=np.float32) / np.float32(nf))
    ar = (t // GRID_W).astype(np.float32)[:, None] * inv
    ac = (t % GRID_W).astype(np.float32)[:, None] * inv
    ang = np.concatenate([ar, ar, ac, ac], axis=-1).T
    put("cos", np.tile(np.cos(ang), (2, 1)).astype(np.float32))
    put("sin", np.tile(np.sin(ang), (2, 1)).astype(np.float32))
    q = np.arange(L)
    band = np.where(np.abs(q[:, None] - q[None, :]) <= SW, 0.0, NEG).astype(np.float32)
    put("band", np.concatenate([band[:P, P:], band[P:, :P]], axis=1))
    qc = 63 - i % 64
    start = np.clip(qc - NA_COLS // 2, 0, GRID_W - NA_COLS)[:, None]
    kc = np.arange(GRID_W)[None, :]
    ok = (kc >= start) & (kc < start + NA_COLS)
    put("cols", np.where(ok, 0.0, NEG).astype(np.float32))
    halves = np.zeros((P, 2), np.float32)
    halves[:64, 0] = halves[64:, 1] = 1
    put("halves", halves)
    v = np.zeros((P, 66), np.float32)
    v[:, 32:34] = halves / HD
    put("pair", v)
    v = np.zeros((P, 34), np.float32)
    v[:, 32] = 1 / Q_LORA
    put("cq", v)
    v = np.zeros((P, 34), np.float32)
    v[:, 33] = 1 / KV_LORA
    put("ckv", v)
    v = np.zeros((P, 23), np.float32)
    v[:, 11] = 1 / QK_C
    put("nope", v)
    v = np.zeros((P, 22), np.float32)
    v[:, 10:12] = halves / QK_C
    put("rope", v)
    v = np.zeros((P, 12), np.float32)
    v[:, 6:] = 1 / (2 * QK_C)
    put("kpe", v)
    put("mean", np.full((P, 1), 1 / D, np.float32))
    put("sum4", np.tile(np.eye(2, dtype=np.float32), (2, 1)))
    put("eps", np.full((P, 1), EPS, np.float32))
    sel = np.zeros((32, 16, P), np.float32)
    for t in range(16):
        sel[2 * t, t, :64] = sel[2 * t + 1, t, 64:] = 1
    return c, sel


def pack(inputs):
    f = {k: np.asarray(v) for k, v in inputs.items()}
    entries = host_chunks()
    stream = np.zeros((len(entries), P, CH), np.float32)
    y_rows = list(range(512)) + [512 + h * HD + d for h in B_ORDER for d in range(HD)] + list(range(1280, 2048))
    w_out = f["w_out"][:, y_rows, :]
    for n, (name, layer, k0, nk, cols) in enumerate(entries):
        w = w_out if name == "w_out" else f[name]
        if layer is not None:
            w = w[layer]
        blk = w[k0 * P:(k0 + nk) * P].reshape(nk, P, -1)
        width = sum(b - a for a, b in cols)
        dst = stream[n, :, :nk * width].reshape(P, nk, width)
        at = 0
        for a, b in cols:
            dst[:, :, at:at + b - a] = blk[:, :, a:b].transpose(1, 0, 2)
            at += b - a
    par = np.zeros((P, NPARAM), np.float32)

    def put(name, v):
        a, b = PARAM[name]
        par[:, a:b] = v

    def cols(v):
        return v.reshape(-1, P).T

    put("b_ada", cols(f["b_ada"]))
    put("norm_w", cols(f["norm_w"]))
    for n in ("qn_a", "kn_a", "qn_b", "kn_b"):
        put(n, np.tile(f[n].T, (2, 1)))
    put("qa_norm", cols(f["qa_norm"]))
    put("kva_norm", cols(f["kva_norm"]))
    for n in ("qn", "kn"):
        put(n + "_n", f[n + "_c"][:, :NOPE].T)
        put(n + "_r", np.tile(f[n + "_c"][:, NOPE:].T, (2, 1)))
    put("sink", np.broadcast_to(f["sink_b"][:, B_ORDER].reshape(1, -1), (P, 2 * H_B)))
    cond = np.stack([f["c"][0], f["c_ctx"]], axis=-1).reshape(DT, P, 2)
    put("cond", cond.transpose(1, 0, 2).reshape(P, -1))
    put("norm_mix", cols(f["norm_mix_g_2"]))
    put("b_gate", cols(f["b_gate_2"]))
    put("pool_scale", cols(f["pool_scale_2"]))
    put("conv_w", cols(f["conv_w_2"]))
    put("norm_ffn", cols(f["norm_ffn_g_2"]))
    put("norm_final", cols(f["norm_final_g_2"]))

    def tokens(x):
        return np.ascontiguousarray(x.T.reshape(DT, P, -1).transpose(1, 0, 2))

    xT = tokens(np.concatenate([f["x"][0], f["ctx"][0]], axis=0))
    metaT = tokens(f["meta_tokens_2"])
    rpb = np.zeros((DEPTH, H_A, 2 * NA_ROWS - 1, 2 * GRID_W - 1), np.float32)
    rpb[..., GRID_W - NA_COLS:GRID_W + NA_COLS - 1] = f["rpb_a"]
    const, sel = constants()
    rpb = np.ascontiguousarray(rpb.transpose(0, 2, 1, 3))
    return {"stream": stream, "xT": xT, "metaT": metaT, "const": const, "param": par, "sel": sel, "rpb": rpb}


def program(nc, arrays):
    a = {n: nc.dram_tensor(f"in_{n}", v.shape, F32, kind="ExternalInput").ap() for n, v in arrays.items()}
    z_d = nc.dram_tensor("z_scratch", (DT, P, 512), F32, kind="Internal").ap()
    x_d = nc.dram_tensor("x_scratch", (P, DT, 512), F32, kind="Internal").ap()
    out = nc.dram_tensor("out", (P, DT, L), F32, kind="ExternalOutput").ap()
    build(nc, a["stream"], a["xT"], a["metaT"], a["const"], a["param"], a["sel"], a["rpb"], z_d, x_d, out)


def kernel(**inputs):
    import concourse.bacc as bacc
    from concourse.bass_utils import run_bass_kernel_spmd

    nc = bacc.Bacc("TRN2", target_bir_lowering=False, num_devices=1)
    arrays = pack(inputs)
    program(nc, arrays)
    r = run_bass_kernel_spmd(nc, [{f"in_{n}": v for n, v in arrays.items()}], core_ids=[0])
    out = r.results[0]["out"]
    return np.ascontiguousarray(out.transpose(1, 0, 2).reshape(D, L).T).reshape(1, L, D)
```
